# Optimizing a Trainium2 kernel written in Bass

```python
import math
import jax, jax.numpy as jnp
from jax import lax
import numpy as np

D_MODEL = 1024
BATCH = 1
SEQ = 256
DEPTH = 2

A_HEADS = 4
A_HEAD_DIM = 64
A_WIDTH = A_HEADS * 2 * A_HEAD_DIM
Q_BLOCK = 128
B_WIDTH = 512
B_GROUPS = 4
B_GROUP_DIM = B_WIDTH // B_GROUPS
B_CHUNK = 128
C_HEADS = 8
C_HEAD_DIM = 64
C_WIDTH = C_HEADS * C_HEAD_DIM
C_PATTERNS = ((128, 1), (512, 4), (2048, 16))
C_BLOCK = 128
N_BRANCH = 3
BRANCH_WIDTH = 512
IN_COLS = 4 * A_WIDTH + 3 * B_WIDTH + 4 * C_WIDTH + N_BRANCH * D_MODEL
ROPE_THETA = 500000.0
ROPE_FRAC = 4
EPS = 1e-6


def rmsnorm(t, g):
    tf = t.astype(jnp.float32)
    y = tf * lax.rsqrt(jnp.mean(tf * tf, axis=-1, keepdims=True) + EPS)
    return (y * g.astype(jnp.float32)).astype(t.dtype)

def layernorm(t, g, b):
    tf = t.astype(jnp.float32)
    mu = jnp.mean(tf, axis=-1, keepdims=True)
    var = jnp.mean(jnp.square(tf - mu), axis=-1, keepdims=True)
    y = (tf - mu) * lax.rsqrt(var + EPS)
    return (y * g.astype(jnp.float32) + b.astype(jnp.float32)).astype(t.dtype)

def partial_rope(t, positions):
    dh = t.shape[-1]
    rot = dh // ROPE_FRAC
    half = rot // 2
    inv = jnp.power(jnp.float32(ROPE_THETA), -jnp.arange(half, dtype=jnp.float32) * 2.0 / rot)
    ang = positions.astype(jnp.float32)[:, :, None] * inv
    cos = jnp.cos(ang)[:, :, None, :]
    sin = jnp.sin(ang)[:, :, None, :]
    tf = t.astype(jnp.float32)
    x1 = tf[..., :half]
    x2 = tf[..., half:rot]
    out = jnp.concatenate([x1 * cos - x2 * sin, x2 * cos + x1 * sin, tf[..., rot:]], axis=-1)
    return out.astype(t.dtype)

def split_cols(proj):
    sizes = [A_WIDTH, A_WIDTH, A_WIDTH, A_WIDTH,
             2 * B_WIDTH, B_WIDTH,
             C_WIDTH, C_WIDTH, C_WIDTH, C_WIDTH,
             N_BRANCH * D_MODEL]
    idx = np.cumsum(sizes)[:-1].tolist()
    return jnp.split(proj, idx, axis=-1)

def diff_attention(q, k, v, lam):
    B, S, H, _, d = q.shape
    nb = S // Q_BLOCK
    scale = 1.0 / math.sqrt(d)
    qb = q.reshape(B, nb, Q_BLOCK, H, 2, d).transpose(1, 0, 2, 3, 4, 5)
    kpos = jnp.arange(S)

    def block(args):
        i, qblk = args
        s = jnp.einsum('bqhmd,bkhmd->bhmqk', qblk, k,
                       preferred_element_type=jnp.float32) * scale
        qpos = i * Q_BLOCK + jnp.arange(Q_BLOCK)
        mask = kpos[None, :] <= qpos[:, None]
        s = jnp.where(mask, s, -jnp.inf)
        p = jax.nn.softmax(s, axis=-1)
        pd = p[:, :, 0] - lam * p[:, :, 1]
        return jnp.einsum('bhqk,bkhe->bqhe', pd.astype(v.dtype), v)

    out = lax.map(block, (jnp.arange(nb), qb))
    return out.transpose(1, 0, 2, 3, 4).reshape(B, S, H, 2 * d)

def dilated_window_attention(q, k, v, window, dil):
    B, S, H, dh = q.shape
    L = S // dil
    n_back = window // dil
    nb = -(-L // C_BLOCK)
    Lp = nb * C_BLOCK
    BD = B * dil
    scale = 1.0 / math.sqrt(dh)

    def to_sub(t):
        t = t.reshape(B, L, dil, H, dh).transpose(0, 2, 1, 3, 4).reshape(BD, L, H, dh)
        return jnp.pad(t, ((0, 0), (0, Lp - L), (0, 0), (0, 0)))

    def windows(t):
        t = jnp.pad(t, ((0, 0), (C_BLOCK, 0), (0, 0), (0, 0))).reshape(BD, nb + 1, C_BLOCK, H, dh)
        return jnp.concatenate([t[:, :-1], t[:, 1:]], axis=2)

    qb = to_sub(q).reshape(BD, nb, C_BLOCK, H, dh)
    kw = windows(to_sub(k))
    vw = windows(to_sub(v))
    s = jnp.einsum('bnqhd,bnkhd->bnhqk', qb, kw,
                   preferred_element_type=jnp.float32) * scale
    qi = jnp.arange(nb)[:, None, None] * C_BLOCK + jnp.arange(C_BLOCK)[None, :, None]
    ki = jnp.arange(nb)[:, None, None] * C_BLOCK - C_BLOCK + jnp.arange(2 * C_BLOCK)[None, None, :]
    rel = qi - ki
    mask = (rel >= 0) & (rel <= n_back) & (ki >= 0)
    s = jnp.where(mask[None, :, None], s, -jnp.inf)
    m = jnp.max(s, axis=-1, keepdims=True)
    e = jnp.exp(s - m)
    den = jnp.sum(e, axis=-1)
    o = jnp.einsum('bnhqk,bnkhd->bnqhd', e, vw.astype(jnp.float32))
    den_q = den.transpose(0, 1, 3, 2)
    o = o / den_q[..., None]
    lse = m[..., 0].transpose(0, 1, 3, 2) + jnp.log(den_q)

    def from_sub(t):
        rest = t.shape[3:]
        t = t.reshape((B, dil, Lp) + rest)[:, :, :L]
        t = jnp.moveaxis(t, 1, 2)
        return t.reshape((B, S) + rest)

    return from_sub(o), from_sub(lse)

def hybrid_layer(x, positions, layer_idx, norm_g, w_in, lam_q1, lam_k1, lam_q2, lam_k2,
                 subln_g, sgu_ln_g, sgu_ln_b, sgu_w, sgu_b, w_branch, w_out):
    B, S, D = x.shape
    h = rmsnorm(x, norm_g)
    proj = jnp.einsum('bsd,dc->bsc', h, w_in)
    aq, ak, av, az, buv, bz, cq, ck, cv, cz, gl = split_cols(proj)

    lam_init = 0.8 - 0.6 * math.exp(-0.3 * layer_idx)
    lam = (jnp.exp(jnp.sum(lam_q1.astype(jnp.float32) * lam_k1.astype(jnp.float32)))
           - jnp.exp(jnp.sum(lam_q2.astype(jnp.float32) * lam_k2.astype(jnp.float32)))
           + lam_init)
    qa = partial_rope(aq.reshape(B, S, 2 * A_HEADS, A_HEAD_DIM), positions).reshape(B, S, A_HEADS, 2, A_HEAD_DIM)
    ka = partial_rope(ak.reshape(B, S, 2 * A_HEADS, A_HEAD_DIM), positions).reshape(B, S, A_HEADS, 2, A_HEAD_DIM)
    va = av.reshape(B, S, A_HEADS, 2 * A_HEAD_DIM)
    oa = diff_attention(qa, ka, va, lam)
    oa = rmsnorm(oa, subln_g) * (1.0 - lam_init)
    ya = oa.reshape(B, S, A_WIDTH) * jax.nn.silu(az)

    uv = jax.nn.gelu(buv)
    u, vb = uv[..., :B_WIDTH], uv[..., B_WIDTH:]
    vb = layernorm(vb, sgu_ln_g, sgu_ln_b).reshape(B, S // B_CHUNK, B_CHUNK, B_GROUPS, B_GROUP_DIM)
    w_causal = sgu_w * jnp.tril(jnp.ones((B_CHUNK, B_CHUNK), dtype=sgu_w.dtype))
    mixed = jnp.einsum('gts,bnsgc->bntgc', w_causal, vb) + sgu_b.T[None, None, :, :, None]
    yb = u * mixed.reshape(B, S, B_WIDTH) * jax.nn.silu(bz)

    qc = partial_rope(cq.reshape(B, S, C_HEADS, C_HEAD_DIM), positions)
    kc = partial_rope(ck.reshape(B, S, C_HEADS, C_HEAD_DIM), positions)
    vc = cv.reshape(B, S, C_HEADS, C_HEAD_DIM)
    outs = []
    lses = []
    for window, dil in C_PATTERNS:
        o_p, lse_p = dilated_window_attention(qc, kc, vc, window, dil)
        outs.append(o_p)
        lses.append(lse_p)
    wts = jax.nn.softmax(jnp.stack(lses, axis=0), axis=0)
    oc = jnp.sum(wts[..., None] * jnp.stack(outs, axis=0), axis=0).astype(x.dtype)
    yc = oc.reshape(B, S, C_WIDTH) * jax.nn.silu(cz)

    ys = jnp.stack([ya, yb, yc], axis=0)
    pb = jnp.einsum('nbsc,ncd->nbsd', ys, w_branch)
    gates = jax.nn.sigmoid(gl.reshape(B, S, N_BRANCH, D))
    merged = jnp.einsum('bsnd,nbsd->bsd', gates, pb)
    return x + jnp.einsum('bsd,de->bse', merged, w_out)

def first_inputs(seed: int = 0) -> dict:
    key = jax.random.key(seed)
    ks = jax.random.split(key, 16)
    f32 = jnp.float32
    x = jax.random.normal(ks[0], (BATCH, SEQ, D_MODEL), f32)
    positions = jnp.broadcast_to(jnp.arange(SEQ, dtype=jnp.int32)[None, :], (BATCH, SEQ))
    norm_g = 1.0 + 0.05 * jax.random.normal(ks[1], (DEPTH, D_MODEL), f32)
    w_in = jax.random.normal(ks[2], (DEPTH, D_MODEL, IN_COLS), f32) * D_MODEL ** -0.5
    lam_q1 = 0.1 * jax.random.normal(ks[3], (DEPTH, A_HEAD_DIM), f32)
    lam_k1 = 0.1 * jax.random.normal(ks[4], (DEPTH, A_HEAD_DIM), f32)
    lam_q2 = 0.1 * jax.random.normal(ks[5], (DEPTH, A_HEAD_DIM), f32)
    lam_k2 = 0.1 * jax.random.normal(ks[6], (DEPTH, A_HEAD_DIM), f32)
    subln_g = 1.0 + 0.05 * jax.random.normal(ks[7], (DEPTH, 2 * A_HEAD_DIM), f32)
    sgu_ln_g = 1.0 + 0.05 * jax.random.normal(ks[8], (DEPTH, B_WIDTH), f32)
    sgu_ln_b = 0.02 * jax.random.normal(ks[9], (DEPTH, B_WIDTH), f32)
    sgu_w = jax.random.normal(ks[10], (DEPTH, B_GROUPS, B_CHUNK, B_CHUNK), f32) * B_CHUNK ** -0.5
    sgu_b = 1.0 + 0.1 * jax.random.normal(ks[11], (DEPTH, B_GROUPS, B_CHUNK), f32)
    w_branch = jax.random.normal(ks[12], (DEPTH, N_BRANCH, BRANCH_WIDTH, D_MODEL), f32) * BRANCH_WIDTH ** -0.5
    w_out = jax.random.normal(ks[13], (DEPTH, D_MODEL, D_MODEL), f32) * (2.0 * D_MODEL) ** -0.5
    final_g = 1.0 + 0.05 * jax.random.normal(ks[14], (D_MODEL,), f32)
    return {'x': x, 'positions': positions, 'norm_g': norm_g, 'w_in': w_in,
            'lam_q1': lam_q1, 'lam_k1': lam_k1, 'lam_q2': lam_q2, 'lam_k2': lam_k2,
            'subln_g': subln_g, 'sgu_ln_g': sgu_ln_g, 'sgu_ln_b': sgu_ln_b,
            'sgu_w': sgu_w, 'sgu_b': sgu_b, 'w_branch': w_branch, 'w_out': w_out,
            'final_g': final_g}

def first_block(x, positions, norm_g, w_in, lam_q1, lam_k1, lam_q2, lam_k2, subln_g,
              sgu_ln_g, sgu_ln_b, sgu_w, sgu_b, w_branch, w_out, final_g):
    h = x
    for l in range(DEPTH):
        h = hybrid_layer(h, positions, l, norm_g[l], w_in[l], lam_q1[l], lam_k1[l],
                         lam_q2[l], lam_k2[l], subln_g[l], sgu_ln_g[l], sgu_ln_b[l],
                         sgu_w[l], sgu_b[l], w_branch[l], w_out[l])
    return rmsnorm(h, final_g)


N_META = 16
CHUNK = 128
PAD = CHUNK - N_META
NEG_INF = -1e30
D_FF = 2816

FOX_HEADS = 8
FOX_DIM = 64
FOX_W = FOX_HEADS * FOX_DIM
GDN_HEADS = 4
GDN_DK = 128
GDN_DV = 128
GDN_CONV = 4
GDN_QKW = GDN_HEADS * GDN_DK
GDN_VW = GDN_HEADS * GDN_DV
GDN_QKV = 2 * GDN_QKW + GDN_VW
HYB_SIZES = (FOX_W, FOX_W, FOX_W, FOX_HEADS, GDN_QKV, GDN_HEADS, GDN_HEADS, GDN_VW)
HYB_IN = 3 * FOX_W + FOX_HEADS + GDN_QKV + 2 * GDN_HEADS + GDN_VW
MIX_W = FOX_W + GDN_VW
RWKV_HEAD = 64
RWKV_HEADS = D_MODEL // RWKV_HEAD
RWKV_DECAY_LORA = 64
RWKV_A_LORA = 64
RWKV_GATE_LORA = 160
RWKV_GN_EPS = 64e-5


def rms_norm(x, gain):
    x32 = x.astype(jnp.float32)
    y = x32 * lax.rsqrt(jnp.mean(x32 * x32, axis=-1, keepdims=True) + EPS)
    return (y * gain.astype(jnp.float32)).astype(x.dtype)

def l2_normalize(x):
    x32 = x.astype(jnp.float32)
    return x32 * lax.rsqrt(jnp.sum(x32 * x32, axis=-1, keepdims=True) + EPS)

def swiglu_ffn(h, w_in, w_out):
    gate, up = jnp.split(h @ w_in, 2, axis=-1)
    return (jax.nn.silu(gate) * up) @ w_out

def split_cols_2(z, sizes):
    return jnp.split(z, [int(s) for s in np.cumsum(sizes)[:-1]], axis=-1)

def to_heads(t, n, d):
    B_, L, _ = t.shape
    return t.reshape(B_, L, n, d).transpose(0, 2, 1, 3).astype(jnp.float32)

def pad_seq(t):
    widths = [(0, 0)] * t.ndim
    widths[2] = (PAD, 0)
    return jnp.pad(t, widths)

def causal_depthwise_conv(x, w):
    K = w.shape[0]
    L = x.shape[1]
    xp = jnp.pad(x, ((0, 0), (K - 1, 0), (0, 0)))
    y = xp[:, 0:L] * w[0]
    for j in range(1, K):
        y = y + xp[:, j:j + L] * w[j]
    return y

def forgetting_attention(q, k, v, log_f):
    B_, H, LP, Dh = q.shape
    n_blocks = LP // CHUNK
    c = jnp.cumsum(log_f, axis=-1)
    kpos = jnp.arange(LP)
    scale = Dh ** -0.5

    def block(i):
        start = i * CHUNK
        qb = lax.dynamic_slice_in_dim(q, start, CHUNK, axis=2)
        cb = lax.dynamic_slice_in_dim(c, start, CHUNK, axis=2)
        qpos = start + jnp.arange(CHUNK)
        logits = jnp.einsum('bhqd,bhkd->bhqk', qb, k) * scale + cb[..., :, None] - c[..., None, :]
        valid = (kpos[None, :] <= qpos[:, None]) & (kpos[None, :] >= PAD)
        p = jax.nn.softmax(jnp.where(valid, logits, NEG_INF), axis=-1)
        return jnp.einsum('bhqk,bhkd->bhqd', p, v)

    out = lax.map(block, jnp.arange(n_blocks))
    return jnp.moveaxis(out, 0, 2).reshape(B_, H, LP, Dh)

def gated_delta_rule(q, k, v, log_g, beta):
    B_, H, LP, Dk = q.shape
    Dv = v.shape[-1]
    nc = LP // CHUNK
    q = (q * Dk ** -0.5).reshape(B_, H, nc, CHUNK, Dk)
    k = k.reshape(B_, H, nc, CHUNK, Dk)
    v = v.reshape(B_, H, nc, CHUNK, Dv)
    beta = beta.reshape(B_, H, nc, CHUNK)
    gc = jnp.cumsum(log_g.reshape(B_, H, nc, CHUNK), axis=-1)
    idx = jnp.arange(CHUNK)
    causal = idx[:, None] >= idx[None, :]
    strict = idx[:, None] > idx[None, :]
    decay = jnp.exp(jnp.where(causal, gc[..., :, None] - gc[..., None, :], -jnp.inf))
    kb = k * beta[..., None]
    lower = jnp.where(strict, jnp.einsum('bhnid,bhnjd->bhnij', kb, k) * decay, 0.0)
    egc = jnp.exp(gc)[..., None]
    rhs = jnp.concatenate([v * beta[..., None], kb * egc], axis=-1)
    sol = lax.linalg.triangular_solve(lower, rhs, left_side=True, lower=True, unit_diagonal=True)
    u_base, w = sol[..., :Dv], sol[..., Dv:]
    attn = jnp.where(causal, jnp.einsum('bhnid,bhnjd->bhnij', q, k) * decay, 0.0)
    q_dec = q * egc
    g_last = gc[..., -1]
    k_dec = k * jnp.exp(g_last[..., None] - gc)[..., None]
    xs = (jnp.moveaxis(u_base, 2, 0), jnp.moveaxis(w, 2, 0), jnp.moveaxis(attn, 2, 0),
          jnp.moveaxis(q_dec, 2, 0), jnp.moveaxis(k_dec, 2, 0), jnp.moveaxis(jnp.exp(g_last), 2, 0))

    def step(S, inp):
        u_b, w_c, a_c, qd, kd, dl = inp
        u = u_b - jnp.einsum('bhck,bhkv->bhcv', w_c, S)
        o = jnp.einsum('bhck,bhkv->bhcv', qd, S) + jnp.einsum('bhij,bhjv->bhiv', a_c, u)
        S = S * dl[..., None, None] + jnp.einsum('bhck,bhcv->bhkv', kd, u)
        return S, o

    S0 = jnp.zeros((B_, H, Dk, Dv), jnp.float32)
    _, o = lax.scan(step, S0, xs)
    return jnp.moveaxis(o, 0, 2).reshape(B_, H, LP, Dv)

def hybrid_attention_mixer(h, w_in, fox_bf, conv_w, a_log, dt_bias, o_gain, w_out):
    B_, L, _ = h.shape
    f32 = jnp.float32
    fq, fk, fv, ff, gqkv, ga, gb, gz = split_cols_2(h @ w_in, HYB_SIZES)
    q_f = pad_seq(to_heads(fq, FOX_HEADS, FOX_DIM))
    k_f = pad_seq(to_heads(fk, FOX_HEADS, FOX_DIM))
    v_f = pad_seq(to_heads(fv, FOX_HEADS, FOX_DIM))
    log_f = pad_seq(jax.nn.log_sigmoid((ff + fox_bf).astype(f32)).transpose(0, 2, 1))
    o_fox = forgetting_attention(q_f, k_f, v_f, log_f)[:, :, PAD:]
    o_fox = o_fox.transpose(0, 2, 1, 3).reshape(B_, L, FOX_W)
    gqkv = jax.nn.silu(causal_depthwise_conv(gqkv, conv_w))
    gq, gk, gv = split_cols_2(gqkv, (GDN_QKW, GDN_QKW, GDN_VW))
    q_g = pad_seq(l2_normalize(to_heads(gq, GDN_HEADS, GDN_DK)))
    k_g = pad_seq(l2_normalize(to_heads(gk, GDN_HEADS, GDN_DK)))
    v_g = pad_seq(to_heads(gv, GDN_HEADS, GDN_DV))
    log_g = -jnp.exp(a_log.astype(f32)) * jax.nn.softplus((ga + dt_bias).astype(f32))
    log_g = pad_seq(log_g.transpose(0, 2, 1))
    beta = pad_seq(jax.nn.sigmoid(gb.astype(f32)).transpose(0, 2, 1))
    o_gdn = gated_delta_rule(q_g, k_g, v_g, log_g, beta)[:, :, PAD:].transpose(0, 2, 1, 3)
    o_gdn = rms_norm(o_gdn, o_gain) * jax.nn.silu(gz.reshape(B_, L, GDN_HEADS, GDN_DV).astype(f32))
    o = jnp.concatenate([o_fox, o_gdn.reshape(B_, L, GDN_VW)], axis=-1)
    return o @ w_out

def rwkv7_recurrence(r, decay, k, v, a, b):
    B_, L, H, N = r.shape
    xs = (jnp.moveaxis(r, 1, 0), jnp.moveaxis(decay, 1, 0), jnp.moveaxis(k, 1, 0),
          jnp.moveaxis(v, 1, 0), jnp.moveaxis(a, 1, 0), jnp.moveaxis(b, 1, 0))

    def step(S, inp):
        r_t, w_t, k_t, v_t, a_t, b_t = inp
        sa = jnp.einsum('bhvk,bhk->bhv', S, a_t)
        S = S * w_t[:, :, None, :] + sa[..., None] * b_t[:, :, None, :] + v_t[..., None] * k_t[:, :, None, :]
        return S, jnp.einsum('bhvk,bhk->bhv', S, r_t)

    S0 = jnp.zeros((B_, H, N, N), jnp.float32)
    _, y = lax.scan(step, S0, xs)
    return jnp.moveaxis(y, 0, 1)

def rwkv7_time_mix(h, mu, w_r, w_k, w_v, w0, w1, w2, a0, a1, a2, g1, g2, k_k, k_a, r_k, ln_w, ln_b, w_o):
    B_, L, D = h.shape
    H, N = RWKV_HEADS, RWKV_HEAD
    f32 = jnp.float32
    xx = jnp.pad(h, ((0, 0), (1, 0), (0, 0)))[:, :L] - h
    xr, xw, xk, xv, xa, xg = [h + xx * mu[i] for i in range(6)]
    r = xr @ w_r
    k = xk @ w_k
    v = xv @ w_v
    w_log = -jax.nn.softplus(-(w0 + jnp.tanh(xw @ w1) @ w2)) - 0.5
    a = jax.nn.sigmoid(a0 + (xa @ a1) @ a2)
    g = jax.nn.sigmoid(xg @ g1) @ g2
    kk = l2_normalize((k * k_k).reshape(B_, L, H, N))
    k = k * (1 + (a - 1) * k_a)
    r_h = r.reshape(B_, L, H, N).astype(f32)
    k_h = k.reshape(B_, L, H, N).astype(f32)
    v_h = v.reshape(B_, L, H, N).astype(f32)
    a_h = a.reshape(B_, L, H, N).astype(f32)
    decay = jnp.exp(-jnp.exp(w_log.reshape(B_, L, H, N).astype(f32)))
    y = rwkv7_recurrence(r_h, decay, k_h, v_h, -kk, kk * a_h)
    mean = jnp.mean(y, axis=-1, keepdims=True)
    var = jnp.mean(jnp.square(y - mean), axis=-1, keepdims=True)
    y = ((y - mean) * lax.rsqrt(var + RWKV_GN_EPS)).reshape(B_, L, D) * ln_w + ln_b
    bonus = jnp.sum(r_h * k_h * r_k.astype(f32), axis=-1, keepdims=True) * v_h
    return ((y + bonus.reshape(B_, L, D)) * g) @ w_o

def second_inputs(seed: int = 0) -> dict:
    key = jax.random.key(seed)
    ks = iter(jax.random.split(key, 40))
    f32 = jnp.float32
    NE = (DEPTH + 1) // 2
    NO = DEPTH // 2

    def nrm(shape, scale):
        return jax.random.normal(next(ks), shape, f32) * scale

    def unif(shape, lo, hi):
        return jax.random.uniform(next(ks), shape, f32, minval=lo, maxval=hi)

    dt = jnp.exp(unif((NE, GDN_HEADS), math.log(1e-3), math.log(1e-1)))
    return {
        'x': nrm((BATCH, SEQ, D_MODEL), 1.0),
        'meta': nrm((N_META, D_MODEL), 1.0),
        'ffn_norm': 1.0 + nrm((DEPTH, 2, D_MODEL), 0.02),
        'ffn_w_in': nrm((DEPTH, 2, D_MODEL, 2 * D_FF), D_MODEL ** -0.5),
        'ffn_w_out': nrm((DEPTH, 2, D_FF, D_MODEL), D_FF ** -0.5),
        'mix_norm': 1.0 + nrm((DEPTH, D_MODEL), 0.02),
        'hyb_w_in': nrm((NE, D_MODEL, HYB_IN), D_MODEL ** -0.5),
        'hyb_fox_bf': 3.0 + nrm((NE, FOX_HEADS), 0.5),
        'hyb_conv': nrm((NE, GDN_CONV, GDN_QKV), GDN_CONV ** -0.5),
        'hyb_a_log': jnp.log(unif((NE, GDN_HEADS), 1.0, 16.0)),
        'hyb_dt_bias': dt + jnp.log(-jnp.expm1(-dt)),
        'hyb_o_gain': 1.0 + nrm((NE, GDN_DV), 0.02),
        'hyb_w_out': nrm((NE, MIX_W, D_MODEL), MIX_W ** -0.5),
        'rwkv_mu': unif((NO, 6, D_MODEL), 0.0, 1.0),
        'rwkv_w_r': nrm((NO, D_MODEL, D_MODEL), D_MODEL ** -0.5),
        'rwkv_w_k': nrm((NO, D_MODEL, D_MODEL), D_MODEL ** -0.5),
        'rwkv_w_v': nrm((NO, D_MODEL, D_MODEL), D_MODEL ** -0.5),
        'rwkv_w0': unif((NO, D_MODEL), -6.0, -1.0),
        'rwkv_w1': nrm((NO, D_MODEL, RWKV_DECAY_LORA), D_MODEL ** -0.5),
        'rwkv_w2': nrm((NO, RWKV_DECAY_LORA, D_MODEL), 0.1 * RWKV_DECAY_LORA ** -0.5),
        'rwkv_a0': nrm((NO, D_MODEL), 0.1),
        'rwkv_a1': nrm((NO, D_MODEL, RWKV_A_LORA), D_MODEL ** -0.5),
        'rwkv_a2': nrm((NO, RWKV_A_LORA, D_MODEL), 0.1 * RWKV_A_LORA ** -0.5),
        'rwkv_g1': nrm((NO, D_MODEL, RWKV_GATE_LORA), D_MODEL ** -0.5),
        'rwkv_g2': nrm((NO, RWKV_GATE_LORA, D_MODEL), RWKV_GATE_LORA ** -0.5),
        'rwkv_k_k': 0.85 + nrm((NO, D_MODEL), 0.02),
        'rwkv_k_a': 1.0 + nrm((NO, D_MODEL), 0.02),
        'rwkv_r_k': nrm((NO, RWKV_HEADS, RWKV_HEAD), 0.1),
        'rwkv_ln_w': 1.0 + nrm((NO, D_MODEL), 0.02),
        'rwkv_ln_b': nrm((NO, D_MODEL), 0.02),
        'rwkv_w_o': nrm((NO, D_MODEL, D_MODEL), D_MODEL ** -0.5),
        'final_norm': 1.0 + nrm((D_MODEL,), 0.02),
    }

def second_block(x, meta, ffn_norm, ffn_w_in, ffn_w_out, mix_norm, hyb_w_in, hyb_fox_bf, hyb_conv,
              hyb_a_log, hyb_dt_bias, hyb_o_gain, hyb_w_out, rwkv_mu, rwkv_w_r, rwkv_w_k, rwkv_w_v,
              rwkv_w0, rwkv_w1, rwkv_w2, rwkv_a0, rwkv_a1, rwkv_a2, rwkv_g1, rwkv_g2, rwkv_k_k,
              rwkv_k_a, rwkv_r_k, rwkv_ln_w, rwkv_ln_b, rwkv_w_o, final_norm):
    B_ = x.shape[0]
    h = jnp.concatenate([jnp.broadcast_to(meta[None], (B_, N_META, D_MODEL)).astype(x.dtype), x], axis=1)
    for layer in range(DEPTH):
        j = layer // 2
        h = h + 0.5 * swiglu_ffn(rms_norm(h, ffn_norm[layer, 0]), ffn_w_in[layer, 0], ffn_w_out[layer, 0])
        hn = rms_norm(h, mix_norm[layer])
        if layer % 2 == 0:
            h = h + hybrid_attention_mixer(hn, hyb_w_in[j], hyb_fox_bf[j], hyb_conv[j], hyb_a_log[j],
                                           hyb_dt_bias[j], hyb_o_gain[j], hyb_w_out[j])
        else:
            h = h + rwkv7_time_mix(hn, rwkv_mu[j], rwkv_w_r[j], rwkv_w_k[j], rwkv_w_v[j], rwkv_w0[j],
                                   rwkv_w1[j], rwkv_w2[j], rwkv_a0[j], rwkv_a1[j], rwkv_a2[j],
                                   rwkv_g1[j], rwkv_g2[j], rwkv_k_k[j], rwkv_k_a[j], rwkv_r_k[j],
                                   rwkv_ln_w[j], rwkv_ln_b[j], rwkv_w_o[j])
        h = h + 0.5 * swiglu_ffn(rms_norm(h, ffn_norm[layer, 1]), ffn_w_in[layer, 1], ffn_w_out[layer, 1])
    return rms_norm(h, final_norm)[:, N_META:]


_first_inputs = second_inputs


def second_inputs(seed=0):
    import zlib

    import numpy as np

    out = dict(_first_inputs(seed))
    spreads = {}
    factors = {'ffn_norm': 3.141,
     'hyb_o_gain': 5.659,
     'rwkv_w1': 8.0,
     'rwkv_w2': 8.0,
     'rwkv_a0': 3.339,
     'rwkv_a1': 3.27,
     'rwkv_a2': 3.265,
     'rwkv_k_k': 49.854,
     'rwkv_k_a': 21.933,
     'rwkv_ln_w': 37.421,
     'rwkv_ln_b': 39.313,
     'final_norm': 8.427}
    for name, (base, spread) in spreads.items():
        noise = np.random.default_rng([zlib.crc32(name.encode()), seed]).standard_normal(out[name].shape)
        drawn = base * np.exp(spread * noise) if base else spread * noise
        out[name] = __import__('jax').numpy.asarray(drawn.astype(out[name].dtype))
    for name, factor in factors.items():
        out[name] = (out[name] * factor).astype(out[name].dtype)
    return out


_narrow_inputs = second_inputs


def second_inputs(seed=0):

    out = dict(_narrow_inputs(seed))
    wider = {'rwkv_k_k': 4.04, 'rwkv_ln_w': 3.39, 'rwkv_ln_b': 3.36, 'final_norm': 3.26}
    for name, times in wider.items():
        mean = out[name].mean()
        out[name] = (mean + times * (out[name] - mean)).astype(out[name].dtype)
    return out


def setup_inputs(seed=0):
    out = dict(first_inputs(seed))
    for name, value in second_inputs(seed + 1).items():
        if name != "x":
            out[name + "_2"] = value
    return out


def reference(
    x, positions, norm_g, w_in, lam_q1, lam_k1, lam_q2, lam_k2, subln_g, sgu_ln_g, sgu_ln_b,
    sgu_w, sgu_b, w_branch, w_out, final_g, meta_2, ffn_norm_2, ffn_w_in_2, ffn_w_out_2,
    mix_norm_2, hyb_w_in_2, hyb_fox_bf_2, hyb_conv_2, hyb_a_log_2, hyb_dt_bias_2, hyb_o_gain_2,
    hyb_w_out_2, rwkv_mu_2, rwkv_w_r_2, rwkv_w_k_2, rwkv_w_v_2, rwkv_w0_2, rwkv_w1_2, rwkv_w2_2,
    rwkv_a0_2, rwkv_a1_2, rwkv_a2_2, rwkv_g1_2, rwkv_g2_2, rwkv_k_k_2, rwkv_k_a_2, rwkv_r_k_2,
    rwkv_ln_w_2, rwkv_ln_b_2, rwkv_w_o_2, final_norm_2,
):
    x = first_block(
        x, positions, norm_g, w_in, lam_q1, lam_k1, lam_q2, lam_k2, subln_g, sgu_ln_g, sgu_ln_b,
        sgu_w, sgu_b, w_branch, w_out, final_g,
    )
    return second_block(
        x, meta_2, ffn_norm_2, ffn_w_in_2, ffn_w_out_2, mix_norm_2, hyb_w_in_2, hyb_fox_bf_2,
        hyb_conv_2, hyb_a_log_2, hyb_dt_bias_2, hyb_o_gain_2, hyb_w_out_2, rwkv_mu_2,
        rwkv_w_r_2, rwkv_w_k_2, rwkv_w_v_2, rwkv_w0_2, rwkv_w1_2, rwkv_w2_2, rwkv_a0_2,
        rwkv_a1_2, rwkv_a2_2, rwkv_g1_2, rwkv_g2_2, rwkv_k_k_2, rwkv_k_a_2, rwkv_r_k_2,
        rwkv_ln_w_2, rwkv_ln_b_2, rwkv_w_o_2, final_norm_2,
    )


_drawn_inputs = setup_inputs


def setup_inputs(seed=0):
    import zlib

    import numpy as np

    out = dict(_drawn_inputs(seed))
    spreads = {}
    factors = {'sgu_ln_b': 4.784, 'rwkv_k_a_2': 20.66}
    for name, (base, spread) in spreads.items():
        noise = np.random.default_rng([zlib.crc32(name.encode()), seed]).standard_normal(out[name].shape)
        drawn = base * np.exp(spread * noise) if base else spread * noise
        out[name] = __import__('jax').numpy.asarray(drawn.astype(out[name].dtype))
    for name, factor in factors.items():
        out[name] = (out[name] * factor).astype(out[name].dtype)
    return out
```

```python
import math
from contextlib import ExitStack

import numpy as np
import concourse.bass as bass
from concourse import mybir

F32 = mybir.dt.float32
F32R = mybir.dt.float32r
I32 = mybir.dt.int32
ALU = mybir.AluOpType
ACT = mybir.ActivationFunctionType
AXX = mybir.AxisListType.X

P = 128
D = 1024
KC = D // P
DEPTH = 2
S1 = 256
META = 16
S2 = S1 + META
T1 = 128
T2 = 68
NT1, NT2 = S1 // T1, S2 // T2
RING = 4
ARENA = 36700
FIRST_AT = 31744
SPLIT = 2
EPS = 1e-6
NEG = -1e30

AQ, AK, AV, AZ, BU, BV, BZ, CQ, CK, CV, CZ, GL = 0, 4, 8, 12, 16, 20, 24, 28, 32, 36, 40, 44
IN_CH = 68
A_HEADS, C_HEADS, F_HEADS, G_HEADS, R_HEADS = 4, 8, 8, 4, 16
FF_CH = 22
FQ, FK, FV, GQ, GK, GV, GZ = 0, 4, 8, 12, 16, 20, 24
HYB_CH = 28

BLOCKS = {}
_n = 0
for _l in range(DEPTH):
    for _name, _count in (("w_in", IN_CH), ("w_branch", 12), ("w_out", KC)):
        BLOCKS[_name, _l] = (_n, _count)
        _n += _count
for _l in range(DEPTH):
    for _name, _count in (("ffn_in0", 2 * FF_CH), ("ffn_out0", FF_CH), ("mix_in", HYB_CH if _l == 0 else 24),
                          ("mix_out", KC), ("ffn_in1", 2 * FF_CH), ("ffn_out1", FF_CH)):
        BLOCKS[_name, _l] = (_n, _count)
        _n += _count
N_BLOCKS = _n


def _columns(table):
    at, out = 0, {}
    for name, width in table:
        out[name] = (at, width)
        at += width
    return out, at


CONST, CONST_W = _columns([
    ("ident", P), ("ones", P), ("half_ones", P), ("inv_freq", 1),
    ("mask_f", NT2 * S2),
    ("tri", 4 * T2), ("levels", 7 * T2), ("restart", S2), ("neg_tri", T2), ("row_one", S2), ("gate_sign", 1),
])
FIRST, FIRST_W = _columns([
    ("rope", P), ("causal_w", P), ("mask_a", 2 * S1), ("mask_c", 2 * S1), ("count_c", 2 * S1),
    ("lam", DEPTH * 4 * 64), ("sgu_w", DEPTH * 4 * P), ("sgu_b", DEPTH * 4 * P),
])
VEC, VEC_W = _columns([
    ("norm_g", DEPTH * KC), ("final_g", KC), ("subln_g", DEPTH), ("ln_g", DEPTH * 4), ("ln_b", DEPTH * 4),
    ("ffn_g", DEPTH * 2 * KC), ("mix_g", DEPTH * KC), ("final2_g", KC), ("hyb_small", KC * T2),
    ("conv", 12 * 4), ("o_gain", 1), ("mu", 6 * KC), ("w0", KC), ("a0", KC),
    ("k_k", KC), ("k_a", KC), ("r_k", KC), ("ln_w", KC), ("ln_bb", KC),
    ("gate_b", 3),
])


def host_constants():
    c, first = np.zeros((P, CONST_W), np.float32), np.zeros((P, FIRST_W), np.float32)

    def put(name, value):
        table, into = (CONST, c) if name in CONST else (FIRST, first)
        at, width = table[name]
        into[:value.shape[0], at:at + width] = value.reshape(value.shape[0], width)

    p = np.arange(P)
    put("ident", np.eye(P, dtype=np.float32))
    put("ones", np.ones((P, P), np.float32))
    put("half_ones", (p[:, None] // 64 == p[None] // 64).astype(np.float32))
    half, rot = 8, 16
    perm = np.zeros((P, P), np.float32)
    for base in (0, 64):
        for i in range(half):
            perm[base + half + i, base + i] = -1.0
            perm[base + i, base + half + i] = 1.0
    put("rope", perm)
    put("causal_w", (p[:, None] <= p[None]).astype(np.float32))
    inv = np.power(np.float32(500000.0), -np.arange(half, dtype=np.float32) * np.float32(2.0) / np.float32(rot))
    f = np.zeros((P, 1), np.float32)
    for base in (0, 64):
        f[base:base + half, 0] = inv
        f[base + half:base + rot, 0] = inv
    put("inv_freq", f)
    q = np.arange(2)[None, :, None] * T1 + p[:, None, None]
    rel = q - np.arange(S1)[None, None, :]
    put("mask_a", np.where(rel >= 0, 0.0, NEG).astype(np.float32))
    count = ((rel >= 0) & (rel <= 128)).astype(np.float32) + ((rel >= 0) & (rel % 4 == 0)) + ((rel >= 0) & (rel % 16 == 0))
    put("mask_c", np.where(count > 0, 0.0, NEG).astype(np.float32))
    put("count_c", count.astype(np.float32))
    t = np.arange(T2)
    q = np.arange(NT2)[None, :, None] * T2 + t[:, None, None]
    put("mask_f", np.where(q >= np.arange(S2)[None, None, :], 0.0, NEG).astype(np.float32))
    strict, incl = t[:, None] < t[None], t[:, None] <= t[None]
    put("tri", np.stack([strict, incl, strict, incl], 1).astype(np.float32))
    put("neg_tri", np.where(incl, 0.0, NEG).astype(np.float32))
    lev = [(t[:, None] // (2 * b) == t[None] // (2 * b)) & (t[:, None] // b != t[None] // b) & strict
           for b in (1, 2, 4, 8, 16, 32, 64)]
    put("levels", np.stack(lev, 1).astype(np.float32))
    put("restart", np.tile((np.arange(S2) % T2 != 0).astype(np.float32), (P, 1)))
    put("row_one", np.ones((P, S2), np.float32))
    put("gate_sign", np.where(p < 32, -1.0, 1.0).astype(np.float32)[:, None])
    return c, first


def host_vectors(i, first):
    v = np.zeros((P, VEC_W), np.float32)

    def put(name, value):
        table, into = (VEC, v) if name in VEC else (FIRST, first)
        at, width = table[name]
        into[:value.shape[0], at:at + width] = value.reshape(value.shape[0], width)

    def cols(a):
        a = np.asarray(a)
        return np.ascontiguousarray(a.reshape(-1, P).T)

    def every(a):
        return np.broadcast_to(np.asarray(a).reshape(1, -1), (P, np.asarray(a).size))

    put("norm_g", cols(i["norm_g"]))
    put("final_g", cols(i["final_g"]))
    put("subln_g", cols(i["subln_g"]))
    put("ln_g", cols(i["sgu_ln_g"]))
    put("ln_b", cols(i["sgu_ln_b"]))
    put("lam", every(np.stack([i[n] for n in ("lam_q1", "lam_k1", "lam_q2", "lam_k2")], 1)))
    put("sgu_w", np.ascontiguousarray(np.asarray(i["sgu_w"]).transpose(3, 0, 1, 2)).reshape(P, -1))
    put("sgu_b", every(i["sgu_b"]))
    put("ffn_g", cols(i["ffn_norm_2"]))
    put("mix_g", cols(i["mix_norm_2"]))
    put("final2_g", cols(i["final_norm_2"]))
    w = np.asarray(i["hyb_w_in_2"])[0]
    small = np.zeros((D, T2), np.float32)
    small[:, 0:8], small[:, 32:36], small[:, 64:68] = w[:, 1536:1544], w[:, 3080:3084], w[:, 3084:3088]
    put("hyb_small", small.reshape(KC, P, T2).transpose(1, 0, 2).reshape(P, -1))
    put("conv", np.asarray(i["hyb_conv_2"])[0].reshape(4, 12, P).transpose(2, 1, 0).reshape(P, -1))
    put("o_gain", cols(i["hyb_o_gain_2"]))
    put("mu", cols(i["rwkv_mu_2"][0]))
    for name, key in (("w0", "rwkv_w0_2"), ("a0", "rwkv_a0_2"), ("k_k", "rwkv_k_k_2"), ("k_a", "rwkv_k_a_2"),
                      ("r_k", "rwkv_r_k_2"), ("ln_w", "rwkv_ln_w_2"), ("ln_bb", "rwkv_ln_b_2")):
        put(name, cols(i[key]))
    b = np.zeros((P, 3), np.float32)
    b[0:8, 0] = np.asarray(i["hyb_fox_bf_2"])[0]
    b[32:36, 0] = np.asarray(i["hyb_dt_bias_2"])[0]
    b[32:36, 1] = np.asarray(i["hyb_a_log_2"])[0]
    put("gate_b", b)
    lora = np.concatenate([i[n][0] for n in ("rwkv_w1_2", "rwkv_a1_2", "rwkv_g1_2")], 1)
    lora = lora.reshape(KC, P, 288).transpose(1, 0, 2).reshape(P, -1)
    inner = np.zeros((P, 4, D), np.float32)
    inner[0:64, 0], inner[0:64, 1] = i["rwkv_w2_2"][0], i["rwkv_a2_2"][0]
    inner[:, 2], inner[0:32, 3] = i["rwkv_g2_2"][0][:P], i["rwkv_g2_2"][0][P:]
    return v, np.concatenate([lora, inner.reshape(P, -1)], 1)


def host_weights(i):
    w = np.empty((N_BLOCKS, P, D), np.float32)

    def by_output(a):
        a = np.asarray(a)
        m = a.shape[1] // P
        return a.reshape(KC, P, m, P).transpose(2, 1, 0, 3).reshape(m, P, D)

    def put(key, value):
        at, count = BLOCKS[key]
        w[at:at + count] = value

    for l in range(DEPTH):
        put(("w_in", l), by_output(i["w_in"][l]))
        wb = np.asarray(i["w_branch"][l])
        wb = wb.reshape(3, 4, P, 4, 2, P).transpose(3, 0, 2, 4, 1, 5).reshape(12, P, D)
        put(("w_branch", l), wb)
        put(("w_out", l), by_output(i["w_out"][l]))
        for f in range(2):
            a = by_output(i["ffn_w_in_2"][l, f]).reshape(2, FF_CH, P, D).transpose(1, 0, 2, 3)
            put((f"ffn_in{f}", l), a.reshape(2 * FF_CH, P, D))
            put((f"ffn_out{f}", l), np.asarray(i["ffn_w_out_2"][l, f]).reshape(FF_CH, P, D))
    h = np.asarray(i["hyb_w_in_2"])[0]
    h = np.concatenate([h[:, 0:1536], h[:, 1544:3080], h[:, 3088:3600]], 1)
    put(("mix_in", 0), by_output(h))
    put(("mix_out", 0), by_output(i["hyb_w_out_2"][0]))
    put(("mix_in", 1), np.concatenate([by_output(i[n][0]) for n in ("rwkv_w_r_2", "rwkv_w_k_2", "rwkv_w_v_2")]))
    put(("mix_out", 1), by_output(i["rwkv_w_o_2"][0]))
    return w


def build(nc, x_in, pos_in, const_in, first_in, vec_in, weights_in, out):
    ctx = ExitStack()
    with ctx:
        def sb(name, shape, dt=F32):
            return ctx.enter_context(nc.sbuf_tensor(name, shape, dt))

        sems = {}

        def sem(name):
            if name not in sems:
                sems[name] = ctx.enter_context(nc.semaphore(name))
            return sems[name]

        C = sb("consts", [P, CONST_W])
        V = sb("vectors", [P, VEC_W])
        W = sb("weight_ring", [P, RING, D])
        WH, WL = sb("weights_high", [P, SPLIT, D], F32R), sb("weights_low", [P, SPLIT, D], F32R)
        X = sb("residual", [P, KC, S2])
        H = sb("normed", [P, KC, S2])
        SQ = sb("squares", [P, KC, S2])
        RS = sb("rstd", [P, 3, S2])
        SM = sb("small", [P, 64])
        AR_BYTE = nc.sbuf_base
        AR = sb("arena", [P, ARENA])
        PS = ctx.enter_context(nc.psum_tensor("psum", [P, 8, 512], F32))

        def const(name, rows=P):
            at, width = CONST[name]
            return C[0:rows, at:at + width]

        def vec(name, at=0, width=None, rows=P):
            start, w = VEC[name]
            return V[0:rows, start + at:start + at + (w - at if width is None else width)]

        def first(name):
            at, width = FIRST[name]
            return AR[:, FIRST_AT + at:FIRST_AT + at + width]

        def part(name, at, chunks, n):
            return nc.alloc_sbuf_tensor_at(name, [P, chunks, n], F32R, offset=AR_BYTE + 4 * at)

        def parts(name, at, chunks, n):
            return part(f"{name}_high", at, chunks, n), part(f"{name}_low", at + chunks * n, chunks, n)

        def arena(at, *shape):
            n = math.prod(shape)
            v = AR[:, at:at + n]
            if len(shape) == 2:
                return v.rearrange("p (a b) -> p a b", a=shape[0])
            if len(shape) == 3:
                return v.rearrange("p (a b c) -> p a b c", a=shape[0], b=shape[1])
            return v

        STAGES_BEFORE_RWKV = 1 + 6 * DEPTH + 1 + 1 + 9 + 1 + 1 + 1
        IDENT, ONES, HALF = const("ident"), const("ones"), const("half_ones")
        XA = X[:, :, META:S2]

        class Chain:

            def __init__(self, eng, name):
                self.eng, self.sem, self.n = eng, sem(name), 0

            def __call__(self, step):
                self.n += 1
                step.then_inc(self.sem, 1)
                self.eng.wait_ge(self.sem, self.n)

        act_chain = dve_chain = None
        stage_end = sem("stage_end")
        stages = {}

        def end_stage(eng, name):
            stages[name] = stages.get(name, 0) + 1
            eng.drain().then_inc(stage_end, 1)
            eng.wait_ge(stage_end, 4 * stages[name])

        landed = [sem(f"weights_landed{u}") for u in range(RING)]
        weights_high, weights_low = sem("weights_high_ready"), sem("weights_low_ready")
        blocks_done = sem("blocks_done")

        def at_turn(value, g, step):
            return value if g is None else g * step + value

        def act_split(act, n, g=None):
            if n >= N_BLOCKS:
                return
            act.wait_ge(landed[n % RING], at_turn(16 * (n // RING + 1), g, 16))
            if n >= SPLIT:
                act.wait_ge(blocks_done, at_turn(n - SPLIT + 1, g, RING))
            for half in (slice(0, 512), slice(512, 1024)):
                nc.scalar.activation(WH[:, n % SPLIT, half], W[:, n % RING, half], ACT.Copy).then_inc(weights_high, 1)

        def dve_split(dve, n, g=None):
            if n >= N_BLOCKS:
                return
            for j, half in enumerate((slice(0, 512), slice(512, 1024))):
                dve.wait_ge(weights_high, at_turn(2 * n + j + 1, g, 2 * RING))
                nc.vector.tensor_tensor(WL[:, n % SPLIT, half], W[:, n % RING, half],
                                        WH[:, n % SPLIT, half].bitcast(F32), ALU.subtract).then_inc(weights_low, 1)

        def split_ahead(eng, split, first, count):
            if count >= RING:
                with eng.Fori(0, count // RING) as g:
                    for u in range(RING):
                        split(eng, first + u + SPLIT, g)
            for n in range(first + count // RING * RING, first + count):
                split(eng, n + SPLIT)

        def pe_arrived(pe, n, g=None):
            pe.wait_ge(weights_low, at_turn(2 * n + 2, g, 2 * RING))

        def pe_tile(psum, n, t, high, low, start, stop):
            s, cols = n % SPLIT, slice(t * P, (t + 1) * P)
            nc.tensor.matmul(psum, WH[:, s, cols], high, start=start, stop=False)
            nc.tensor.matmul(psum, WH[:, s, cols], low, start=False, stop=False)
            return nc.tensor.matmul(psum, WL[:, s, cols], high, start=False, stop=stop)

        act_high, act_low = sem("activation_high_ready"), sem("activation_low_ready")
        JOBS = {name: j for j, name in enumerate(
            [("w_in", 0), ("w_out", 0), ("w_in", 1), ("w_out", 1), ("ffn", 0), ("hybrid", 0), ("hybrid", 1), ("ffn", 1), ("ffn", 2),
             ("r", 0), ("r", 1), ("r", 2), ("r", 3), ("ffn", 3)])}

        def act_parts(act, job, source, high, ready, base):
            for k in range(KC):
                act.wait_ge(ready, base + k + 1)
                nc.scalar.activation(high[:, k], source[:, k], ACT.Copy).then_inc(act_high, 1)

        def dve_parts(dve, job, source, high, low):
            for k in range(KC):
                dve.wait_ge(act_high, KC * JOBS[job] + k + 1)
                nc.vector.tensor_tensor(low[:, k], source[:, k], high[:, k].bitcast(F32), ALU.subtract).then_inc(act_low, 1)

        taken = [sem("even_outputs_taken"), sem("odd_outputs_taken")]
        OUTS = {}
        total = 0
        for l in range(DEPTH):
            for name in ("w_in", "w_out"):
                OUTS[name, l] = total
                total += BLOCKS[name, l][1]
        for l in range(DEPTH):
            for name in ("mix_in", "mix_out"):
                OUTS[name, l] = total
                total += BLOCKS[name, l][1]
        assert all(v % 4 == 0 for v in OUTS.values())

        def pe_project(pe, key, job, high, low, n, part=(0, None)):
            block, count = BLOCKS[key]
            o = OUTS[key] + part[0]
            block += part[0]
            count = part[1] or count
            pe.wait_ge(act_low, KC * (JOBS[job] + 1))
            with pe.Fori(0, count // 4) as g:
                for u in range(4):
                    pe_arrived(pe, block + u, g)
                    pe.wait_ge(taken[u % 2], g * 2 + (o + u) // 2 + 1)
                    for k in range(KC):
                        mm = pe_tile(PS[:, u, 0:n], block + u, k, high[:, k], low[:, k], k == 0, k == KC - 1)
                    mm.then_inc(blocks_done, 1)
        def take_outputs(eng, split, key, parities, take, part=(0, None)):
            block, count = BLOCKS[key]
            block += part[0]
            count = part[1] or count
            with eng.Fori(0, count // 4) as g:
                for u in range(4):
                    split(eng, block + u + SPLIT, g)
                    if u % 2 in parities:
                        eng.wait_ge(blocks_done, g * 4 + block + u + 1)
                        take(g * 4 + (part[0] + u), u).then_inc(taken[u % 2], 1)

        def act_take(dest, n):
            def take(chunk, bank):
                nc.scalar.wait_ge(blocks_done, 1)
                return nc.scalar.activation(dest[:, chunk, 0:n], PS[:, bank, 0:n], ACT.Copy)
            return take

        def dve_take(dest, n):
            return lambda chunk, bank: nc.vector.tensor_scalar(
                dest[:, chunk, 0:n], PS[:, bank, 0:n], 1.0, None, ALU.mult)

        def dve_add(dest, n):
            return lambda chunk, bank: nc.vector.scalar_tensor_tensor(
                out=dest[:, chunk, 0:n], in0=PS[:, bank, 0:n], scalar=1.0, in1=dest[:, chunk, 0:n],
                op0=ALU.mult, op1=ALU.add)

        squares_ready, ssum_ready = sem("squares_ready"), sem("square_sum_ready")
        mean_ready, rstd_ready, normed_ready = sem("mean_square_ready"), sem("rstd_ready"), sem("normed_ready")

        def act_norm(act, use, x, n):
            nc.scalar.activation(SQ[:, :, 0:n], x, ACT.Square).then_inc(squares_ready, 1)
            act.wait_ge(mean_ready, use + 1)
            act_chain(nc.scalar.activation(RS[:, 1, 0:n], RS[:, 0, 0:n], ACT.Ln))
            nc.scalar.activation(RS[:, 2, 0:n], RS[:, 1, 0:n], ACT.Exp, scale=-0.5).then_inc(rstd_ready, 1)

        def pe_norm(pe, use, n):
            pe.wait_ge(squares_ready, use + 1)
            for k in range(KC):
                mm = nc.tensor.matmul(PS[:, 7, 0:n], ONES, SQ[:, k, 0:n], start=(k == 0), stop=(k == KC - 1))
            mm.then_inc(ssum_ready, 1)

        def dve_norm(dve, use, x, n, gain, dest):
            dve.wait_ge(ssum_ready, use + 1)
            nc.vector.tensor_scalar(RS[:, 0, 0:n], PS[:, 7, 0:n], 1.0 / D, EPS, ALU.mult, ALU.add)\
                .then_inc(mean_ready, 1)
            dve.wait_ge(rstd_ready, use + 1)
            for k in range(KC):
                nc.vector.scalar_tensor_tensor(out=dest[:, k, 0:n], in0=x[:, k], scalar=gain[:, k:k + 1],
                                               in1=RS[:, 2, 0:n], op0=ALU.mult, op1=ALU.mult)\
                    .then_inc(normed_ready, 1)
            dve.wait_ge(normed_ready, KC * (use + 1))

        class Attn:

            def __init__(self, kind, layer):
                self.kind, self.layer = kind, layer
                self.heads, self.maps = {"A": (A_HEADS, 2), "C": (C_HEADS, 1), "F": (F_HEADS, 1)}[kind]
                self.t, self.nt = (T2, NT2) if kind == "F" else (T1, NT1)
                self.n = self.t * self.nt
                self.base = layer * self.heads
                self.e = 128 if kind == "A" else 64
                name = {"A": "diff", "C": "dilated", "F": "fox"}[kind]
                self.s = {k: sem(f"{name}_{k}") for k in (
                    "scores_ready", "scores_taken", "neg_max_ready", "exp_ready", "probs_ready",
                    "turned", "turned_taken", "out_ready", "out_taken")}

            def score(self, h, m, qi):
                b, w = h % 2, self.t * (qi + 1)
                if self.kind == "A":
                    return PS[0:self.t, 2 * b + m, 256 * qi:256 * qi + w]
                if self.kind == "C":
                    return PS[0:self.t, h % 4, 256 * qi:256 * qi + w]
                bank, at = [(0, 0), (0, 68), (0, 204), (1, 0)][qi]
                return PS[0:self.t, 2 * b + bank, at:at + w]

            def rows(self, h, m):
                r = 64 * (m if self.kind == "A" else h % 2)
                return slice(r, r + 64), (h if self.kind == "A" else h // 2)

            def turn_at(self, h, kj):
                if self.kind == "F":
                    bank, at = [(4, 0), (4, 272), (5, 0), (5, 136)][kj]
                else:
                    bank, at = 4 + h % 2, 256 * kj
                return bank, at, self.n - self.t * kj

        def pe_attention(pe, A, q, k, v, gates=None):
            s = A.s

            def scores(h):
                if h >= 2:
                    pe.wait_ge(s["scores_taken"], A.base + h - 1)
                for m in range(A.maps):
                    r, c = A.rows(h, m)
                    for qi in range(A.nt):
                        w = A.t * (qi + 1)
                        mm = nc.tensor.matmul(A.score(h, m, qi), q[r, c, qi * A.t:(qi + 1) * A.t], k[r, c, 0:w],
                                              start=True, stop=gates is None)
                        if gates is not None:
                            g = slice(64 * (h % 2), 64 * (h % 2) + 33)
                            mm = nc.tensor.matmul(A.score(h, m, qi), gates[0][g, h // 2, qi * A.t:(qi + 1) * A.t],
                                                  gates[1][g, h // 2, 0:w], start=False, stop=True)
                mm.then_inc(s["scores_ready"], 1)

            def turn(h):
                pe.wait_ge(s["probs_ready"], A.base + h + 1)
                back = 1 if A.kind == "F" else 2
                if h >= back:
                    pe.wait_ge(s["turned_taken"], A.base + h - back + 1)
                for kj in range(A.nt):
                    bank, at, _ = A.turn_at(h, kj)
                    for qi in range(kj, A.nt):
                        o = at + A.t * (qi - kj)
                        mm = nc.tensor.transpose(PS[0:A.t, bank, o:o + A.t],
                                                 A.probs(h, qi)[:, kj * A.t:(kj + 1) * A.t], IDENT[0:A.t, 0:A.t])
                mm.then_inc(s["turned"], 1)

            def weigh(h):
                pe.wait_ge(s["turned_taken"], A.base + h + 1)
                if h >= 2:
                    pe.wait_ge(s["out_taken"], A.base + h - 1)
                o = 64 * (h % 2) if A.e == 64 else 0
                for kj in range(A.nt):
                    mm = nc.tensor.matmul(PS[o:o + A.e, 6 + h % 2, kj * A.t:A.n],
                                          v[0:A.t, kj, h * A.e:(h + 1) * A.e], A.probs_t(h, kj),
                                          start=(kj == 0), stop=(kj == A.nt - 1))
                mm.then_inc(s["out_ready"], 1)

            scores(0)
            scores(1)
            for h in range(A.heads):
                turn(h)
                if h + 2 < A.heads:
                    scores(h + 2)
                weigh(h)

        def act_attention(act, A):
            s = A.s
            for h in range(A.heads):
                act.wait_ge(s["neg_max_ready"], A.base + h + 1)
                for m in range(A.maps):
                    for qi in range(A.nt):
                        j = m * A.nt + qi
                        step = nc.scalar.activation(
                            A.logits(h, m, qi), A.logits(h, m, qi), ACT.Exp, bias=A.stat(h, 1, j), scale=0.125,
                            **({} if A.kind == "C" else {"accum_out": A.stat(h, 2, j)}))
                step.then_inc(s["exp_ready"], 1)
                if h >= 1:
                    act_turned(act, A, h - 1)
            act_turned(act, A, A.heads - 1)

        def act_turned(act, A, h):
            act.wait_ge(A.s["turned"], A.base + h + 1)
            if h >= 2:
                act.wait_ge(A.s["out_ready"], A.base + h - 1)
            if A.kind == "F":
                act_chain(nc.scalar.activation(A.turned(h)[:, 0:476], PS[0:A.t, 4, 0:476], ACT.Copy))
                step = nc.scalar.activation(A.turned(h)[:, 476:680], PS[0:A.t, 5, 0:204], ACT.Copy)
            else:
                step = nc.scalar.activation(A.turned(h)[:, 0:384], PS[0:A.t, 4 + h % 2, 0:384], ACT.Copy)
            step.then_inc(A.s["turned_taken"], 1)

        def dve_attention(dve, A, mask, dest, neg_lam=None):
            s = A.s

            def masked_max(h):
                dve.wait_ge(s["scores_ready"], A.base + h + 1)
                if h >= 2:
                    dve.wait_ge(s["turned"], A.base + h - 1)
                for m in range(A.maps):
                    for qi in range(A.nt):
                        w = A.t * (qi + 1)
                        dve_chain(nc.vector.tensor_tensor_reduce(
                            A.logits(h, m, qi), A.score(h, m, qi), mask[0:A.t, qi, 0:w], 1.0, -3e38,
                            ALU.add, ALU.max, A.stat(h, 0, m * A.nt + qi)))
                n = A.maps * A.nt
                dve_chain(nc.vector.tensor_scalar(A.stat(h, 1, 0, n), A.stat(h, 0, 0, n), -0.125, None, ALU.mult))
                dve.sem_inc(s["scores_taken"], 1)
                dve.sem_inc(s["neg_max_ready"], 1)

            def normalise(h):
                n = A.maps * A.nt
                dve.wait_ge(s["exp_ready"], A.base + h + 1)
                if A.kind == "C":
                    for qi in range(A.nt):
                        w = A.t * (qi + 1)
                        dve_chain(nc.vector.tensor_tensor_reduce(
                            A.logits(h, 0, qi), A.logits(h, 0, qi), first("count_c").rearrange(
                                "p (a b) -> p a b", a=2)[:, qi, 0:w], 1.0, 0.0, ALU.mult, ALU.add, A.stat(h, 2, qi)))
                dve_chain(nc.vector.reciprocal(A.stat(h, 3, 0, n), A.stat(h, 2, 0, n)))
                if A.kind == "A":
                    dve_chain(nc.vector.tensor_scalar(A.stat(h, 3, 2, 2), A.stat(h, 3, 2, 2), neg_lam, None, ALU.mult))
                    for qi in range(A.nt):
                        dve_chain(nc.vector.tensor_scalar(A.logits(h, 1, qi), A.logits(h, 1, qi),
                                                          A.stat(h, 3, 2 + qi), None, ALU.mult))
                        dve_chain(nc.vector.scalar_tensor_tensor(
                            out=A.logits(h, 0, qi), in0=A.logits(h, 0, qi), scalar=A.stat(h, 3, qi),
                            in1=A.logits(h, 1, qi), op0=ALU.mult, op1=ALU.add))
                else:
                    for qi in range(A.nt):
                        dve_chain(nc.vector.tensor_scalar(A.logits(h, 0, qi), A.logits(h, 0, qi),
                                                          A.stat(h, 3, qi), None, ALU.mult))
                dve.sem_inc(s["probs_ready"], 1)

            def take(h):
                dve.wait_ge(s["out_ready"], A.base + h + 1)
                o = 64 * (h % 2) if A.e == 64 else 0
                c = h if A.e == 128 else h // 2
                nc.vector.tensor_copy(dest[o:o + A.e, c, 0:A.n], PS[o:o + A.e, 6 + h % 2, 0:A.n])\
                    .then_inc(s["out_taken"], 1)

            masked_max(0)
            for h in range(A.heads):
                if h + 1 < A.heads:
                    masked_max(h + 1)
                normalise(h)
                if h >= 1:
                    take(h - 1)
            take(A.heads - 1)

        def place_attention(A, at):
            width = A.maps * A.nt * A.n
            base_t = at + 2 * width
            A.logits = lambda h, m, qi: AR[0:A.t, at + (h % 2) * width + (m * A.nt + qi) * A.n:][:, 0:A.t * (qi + 1)]
            A.probs = lambda h, qi: A.logits(h, 0, qi)
            A.turned = lambda h: AR[0:A.t, base_t + 1024 * (h % 2):base_t + 1024 * (h % 2) + 1024]

            def probs_t(h, kj):
                starts = [0, 272, 476, 612] if A.kind == "F" else [0, 256]
                return A.turned(h)[:, starts[kj]:starts[kj] + A.n - A.t * kj]
            A.probs_t = probs_t
            A.stat = lambda h, row, j, n=1: SM[0:A.t, 32 * (h % 2) + 8 * row + j:32 * (h % 2) + 8 * row + j + n]
            return A
        PT = arena(0, IN_CH, S1)
        AVN, CVN, BVN = (arena(17408 + 1024 * j, 2, 512) for j in range(3))
        YS = arena(20480, 12, S1)
        SCR = 23552
        NEG_LAM, SUB_G = sb("neg_lam", [P, 8]), sb("subln_gain", [P, 2])
        attn = {}
        for l in range(DEPTH):
            attn["A", l] = place_attention(Attn("A", l), SCR)
            attn["C", l] = place_attention(Attn("C", l), SCR)
        DIFF_OUT, DIFF_RS = arena(SCR, 4, S1), arena(SCR + 1024, 4, S1)
        POS = arena(2048, S1).bitcast(I32)
        COS, SIN = arena(FIRST_AT + FIRST_W, S1), arena(FIRST_AT + FIRST_W + S1, S1)
        YS_H, YS_L = part("branches_high", 17408, 12, S1), part("branches_low", SCR + 1024, 12, S1)
        H1_H, H1_L = parts("first_normed", SCR + 4096, KC, S1)
        H2_H, H2_L = parts("ffn_normed", 0, KC, S2)
        F_H, F_L = parts("ffn_inner", 2 * KC * S2, FF_CH, S2)
        FFN_GATE, FFN_PROD = (arena((2 * KC + 2 * FF_CH + 2 * j) * S2, 2, S2) for j in range(2))
        mask_a = first("mask_a").rearrange("p (a b) -> p a b", a=2)
        mask_c = first("mask_c").rearrange("p (a b) -> p a b", a=2)
        LAM_INIT = [0.8 - 0.6 * math.exp(-0.3 * l) for l in range(DEPTH)]

        inputs_ready = sem("inputs_ready")
        tables = sem("rope_tables")
        gated = sem("nonlinear_ready")
        permuted, rope_sin, rope_cos, roped = (sem(n) for n in ("rope_permuted", "rope_sin_part", "rope_cos_part", "roped"))
        values_turned, values_taken = sem("values_turned"), sem("values_taken")
        sum_ready, row_ready, stat_ready = sem("sum_ready"), sem("row_ready"), sem("stat_ready")
        norm_ready, mixed_ready = sem("norm_ready"), sem("mixed_ready")
        branches_ready, branch_parts = sem("branches_ready"), sem("branch_parts_ready")
        merged_in, merged_part, merged_ready = sem("branch_ready"), sem("branch_gated"), sem("merged_ready")
        gates_taken, ups_taken = sem("gates_taken"), sem("ups_taken")

        def dve_setup(dve):
            ang, turns, ang2 = arena(0, S1), arena(256, S1), arena(512, S1)
            dve_chain(nc.vector.tensor_copy(ang, POS))
            dve_chain(nc.vector.tensor_scalar(ang, ang, const("inv_freq"), None, ALU.mult))
            magic = 12582912.0
            for dest, shift in ((ang2, 0.0), (arena(768, S1), 0.25)):
                dve_chain(nc.vector.tensor_scalar(turns, ang, 1.0 / (2 * math.pi), shift, ALU.mult, ALU.add))
                dve_chain(nc.vector.tensor_scalar(turns, turns, magic, None, ALU.add))
                dve_chain(nc.vector.tensor_scalar(turns, turns, magic, None, ALU.subtract))
                last = ang
                for part in (-6.28125, -0.0019350051879882812, -3.0199159819567e-07):
                    dve_chain(nc.vector.scalar_tensor_tensor(out=dest, in0=turns, scalar=part, in1=last,
                                                             op0=ALU.mult, op1=ALU.add))
                    last = dest
                if shift:
                    dve_chain(nc.vector.tensor_scalar(dest, dest, math.pi / 2, None, ALU.add))
                dve_chain(nc.vector.tensor_scalar(dest, dest, 3.1415925, -3.1415925, ALU.min, ALU.max))
                dve.sem_inc(tables, 1)
            prod = arena(1024, 4, 64)
            lam = first("lam").rearrange("p (l a b) -> p l a b", l=DEPTH, a=4)
            for l in range(DEPTH):
                for j in range(2):
                    dve_chain(nc.vector.tensor_tensor_reduce(prod[:, 2 * l + j], lam[:, l, 2 * j], lam[:, l, 2 * j + 1],
                                                             1.0, 0.0, ALU.mult, ALU.add, SM[:, 2 * l + j:2 * l + j + 1]))
            dve.sem_inc(tables, 1)
            dve.wait_ge(stat_ready, 1)
            for l in range(DEPTH):
                dve_chain(nc.vector.tensor_tensor(NEG_LAM[:, l:l + 1], SM[:, 8 + 2 * l + 1:8 + 2 * l + 2],
                                                  SM[:, 8 + 2 * l:8 + 2 * l + 1], ALU.subtract))
                dve_chain(nc.vector.tensor_scalar(NEG_LAM[:, l:l + 1], NEG_LAM[:, l:l + 1], -LAM_INIT[l], None, ALU.add))
                dve_chain(nc.vector.tensor_scalar(SUB_G[:, l:l + 1], vec("subln_g", l, 1), 1.0 - LAM_INIT[l], None, ALU.mult))

        def act_setup(act):
            act.wait_ge(tables, 1)
            act_chain(nc.scalar.activation(SIN, arena(512, S1), ACT.Sin))
            act.wait_ge(tables, 2)
            act_chain(nc.scalar.activation(COS, arena(768, S1), ACT.Sin))
            act.wait_ge(tables, 3)
            act_chain(nc.scalar.activation(SM[:, 8:12], SM[:, 0:4], ACT.Exp))
            act.sem_inc(stat_ready, 1)

        ROPE_PAIRS = [AQ, AQ + 2, AK, AK + 2, CQ, CQ + 2, CK, CK + 2]

        def act_shape(act, l):
            for at, n, func in ((AZ, 4, ACT.Silu), (BZ, 4, ACT.Silu), (CZ, 4, ACT.Silu),
                                (BU, 8, ACT.Gelu_apprx_tanh), (GL, 24, ACT.Sigmoid)):
                act_chain(nc.scalar.activation(PT[:, at:at + n], PT[:, at:at + n], func))
            for j, (dest, tile) in enumerate(((AVN, 0), (AVN, 1), (CVN, 0), (CVN, 1))):
                act.wait_ge(values_turned, 4 * l + j + 1)
                nc.scalar.activation(dest[:, tile], PS[:, j, 0:512], ACT.Copy).then_inc(values_taken, 1)

        def pe_shape(pe, l):
            for j, at in enumerate(ROPE_PAIRS):
                nc.tensor.matmul(PS[:, j, 0:512], first("rope"), PT[:, at:at + 2], start=True, stop=True)\
                    .then_inc(permuted, 1)
            for j, (at, tile) in enumerate(((AV, 0), (AV, 1), (CV, 0), (CV, 1))):
                pe.wait_ge(rope_sin, 8 * l + j + 1)
                for c in range(4):
                    mm = nc.tensor.transpose(PS[:, j, c * P:(c + 1) * P], PT[:, at + c, tile * T1:(tile + 1) * T1], IDENT)
                mm.then_inc(values_turned, 1)

        def dve_shape(dve, l):
            part = arena(SCR, 8, 512)
            for j in range(8):
                dve.wait_ge(permuted, 8 * l + j + 1)
                nc.vector.tensor_tensor(part[:, j].rearrange("p (a b) -> p a b", a=2),
                                        PS[:, j, 0:512].rearrange("p (a b) -> p a b", a=2),
                                        SIN.unsqueeze(1).broadcast_to([P, 2, S1]), ALU.mult).then_inc(rope_sin, 1)
            for j, at in enumerate(ROPE_PAIRS):
                dve.wait_ge(rope_cos, 8 * l + j + 1)
                dve.wait_ge(rope_sin, 8 * l + j + 1)
                nc.vector.tensor_tensor(PT[:, at:at + 2].rearrange("p a b -> p (a b)"), PT[:, at:at + 2].rearrange("p a b -> p (a b)"),
                                        part[:, j], ALU.add).then_inc(roped, 1)

        def pool_shape(pool, l):
            for j, at in enumerate(ROPE_PAIRS):
                pool.wait_ge(permuted, 8 * l + j + 1)
                nc.gpsimd.tensor_tensor(PT[:, at:at + 2], PT[:, at:at + 2],
                                        COS.unsqueeze(1).broadcast_to([P, 2, S1]), ALU.mult).then_inc(rope_cos, 1)

        def act_diff_norm(act, l):
            act_chain(nc.scalar.activation(DIFF_RS, YS[:, 0:4], ACT.Square))
            act.sem_inc(stat_ready, 1)
            act.wait_ge(row_ready, 3 * l + 1)
            act_chain(nc.scalar.activation(DIFF_RS, DIFF_RS, ACT.Ln))
            act_chain(nc.scalar.activation(DIFF_RS, DIFF_RS, ACT.Exp, scale=-0.5))
            act.sem_inc(stat_ready, 1)

        def pe_diff_norm(pe, l):
            pe.wait_ge(stat_ready, 1 + 4 * l + 1)
            for h in range(4):
                mm = nc.tensor.matmul(PS[:, h // 2, (h % 2) * S1:(h % 2 + 1) * S1], ONES, DIFF_RS[:, h], start=True, stop=True)
            mm.then_inc(sum_ready, 1)

        def dve_diff_norm(dve, l):
            dve.wait_ge(sum_ready, 3 * l + 1)
            dve_chain(nc.vector.tensor_scalar(DIFF_RS.rearrange("p (a b) c -> p a (b c)", a=2), PS[:, 0:2, :],
                                              1.0 / 128, EPS, ALU.mult, ALU.add))
            dve.sem_inc(row_ready, 1)
            dve.wait_ge(stat_ready, 1 + 4 * l + 2)
            y = YS[:, 0:4].rearrange("p a b -> p (a b)")
            dve_chain(nc.vector.scalar_tensor_tensor(out=y, in0=y, scalar=SUB_G[:, l:l + 1],
                                                     in1=DIFF_RS.rearrange("p a b -> p (a b)"), op0=ALU.mult, op1=ALU.mult))
            dve_chain(nc.vector.tensor_tensor(y, y, PT[:, AZ:AZ + 4].rearrange("p a b -> p (a b)"), ALU.mult))
            y = YS[:, 8:12].rearrange("p a b -> p (a b)")
            dve_chain(nc.vector.tensor_tensor(y, y, PT[:, CZ:CZ + 4].rearrange("p a b -> p (a b)"), ALU.mult))

        B_SQ, B_MEAN, B_WC = arena(SCR + 2048, 4, S1), arena(SCR + 3072, 2, S1), arena(SCR + 3584, 4, P)
        B_V = PT[:, BV:BV + 4]

        def pe_sgu(pe, l):
            for k in range(4):
                mm = nc.tensor.matmul(PS[:, 4, 0:S1], ONES, B_V[:, k], start=(k == 0), stop=(k == 3))
            mm.then_inc(sum_ready, 1)
            pe.wait_ge(stat_ready, 1 + 4 * l + 3)
            for k in range(4):
                mm = nc.tensor.matmul(PS[:, 5, 0:S1], ONES, B_SQ[:, k], start=(k == 0), stop=(k == 3))
            mm.then_inc(sum_ready, 1)
            pe.wait_ge(norm_ready, 2 * l + 1)
            for tile in range(2):
                for c in range(4):
                    mm = nc.tensor.transpose(PS[:, 6 + tile, c * P:(c + 1) * P], B_V[:, c, tile * T1:(tile + 1) * T1], IDENT)
                mm.then_inc(mixed_ready, 1)
            pe.wait_ge(norm_ready, 2 * l + 2)
            for tile in range(2):
                pe.wait_ge(merged_in, 2 * l + tile + 1)
                for g in range(4):
                    mm = nc.tensor.matmul(PS[:, 2 + tile, g * P:(g + 1) * P], BVN[:, tile, g * P:(g + 1) * P],
                                          B_WC[:, g], start=True, stop=True)
                mm.then_inc(mixed_ready, 1)

        def act_sgu(act, l):
            act.wait_ge(row_ready, 3 * l + 2)
            act_chain(nc.scalar.activation(B_SQ, B_V, ACT.Square))
            act.sem_inc(stat_ready, 1)
            act.wait_ge(row_ready, 3 * l + 3)
            act_chain(nc.scalar.activation(B_MEAN[:, 1], B_MEAN[:, 1], ACT.Ln))
            act_chain(nc.scalar.activation(B_MEAN[:, 1], B_MEAN[:, 1], ACT.Exp, scale=-0.5))
            act.sem_inc(stat_ready, 1)
            for tile in range(2):
                act.wait_ge(mixed_ready, 4 * l + tile + 1)
                nc.scalar.activation(BVN[:, tile], PS[:, 6 + tile, 0:512], ACT.Copy).then_inc(merged_in, 1)

        def dve_sgu(dve, l):
            dve.wait_ge(sum_ready, 3 * l + 2)
            dve_chain(nc.vector.tensor_scalar(B_MEAN[:, 0], PS[:, 4, 0:S1], 1.0 / 512, None, ALU.mult))
            dve_chain(nc.vector.tensor_tensor(B_V, B_V, B_MEAN[:, 0:1].broadcast_to([P, 4, S1]), ALU.subtract))
            dve.sem_inc(row_ready, 1)
            dve_chain(nc.vector.tensor_tensor(B_WC, first("sgu_w")[:, l * 512:(l + 1) * 512].rearrange("p (a b) -> p a b", a=4),
                                              first("causal_w").unsqueeze(1).broadcast_to([P, 4, P]), ALU.mult))
            dve.wait_ge(sum_ready, 3 * l + 3)
            dve_chain(nc.vector.tensor_scalar(B_MEAN[:, 1], PS[:, 5, 0:S1], 1.0 / 512, EPS, ALU.mult, ALU.add))
            dve.sem_inc(row_ready, 1)
            dve.wait_ge(stat_ready, 1 + 4 * l + 4)
            dve_chain(nc.vector.tensor_tensor(B_V, B_V, B_MEAN[:, 1:2].broadcast_to([P, 4, S1]), ALU.mult))
            for k in range(4):
                dve_chain(nc.vector.tensor_scalar(B_V[:, k], B_V[:, k], vec("ln_g", 4 * l + k, 1), vec("ln_b", 4 * l + k, 1),
                                                  ALU.mult, ALU.add))
            dve.sem_inc(norm_ready, 2)
            bias = first("sgu_b")[:, l * 512:(l + 1) * 512].rearrange("p (a b) -> p a b", a=4)
            y = YS[:, 4:8]
            for tile in range(2):
                dve.wait_ge(mixed_ready, 4 * l + 3 + tile)
                ts = slice(tile * T1, (tile + 1) * T1)
                dve_chain(nc.vector.tensor_tensor(y[:, :, ts], PS[:, 2 + tile, :].rearrange("p (a b) -> p a b", a=4),
                                                  bias, ALU.add))
            y = y.rearrange("p a b -> p (a b)")
            dve_chain(nc.vector.tensor_tensor(y, y, PT[:, BU:BU + 4].rearrange("p a b -> p (a b)"), ALU.mult))
            dve_chain(nc.vector.tensor_tensor(y, y, PT[:, BZ:BZ + 4].rearrange("p a b -> p (a b)"), ALU.mult))

        def pe_merge(pe, l):
            block, _ = BLOCKS["w_branch", l]
            pe.wait_ge(branch_parts, 2 * l + 2)
            for j in range(12):
                pe_arrived(pe, block + j)
                if j >= 4:
                    pe.wait_ge(merged_part, 12 * l + j - 3)
                for c in range(2):
                    for k in range(4):
                        y = 4 * (j % 3) + k
                        mm = pe_tile(PS[:, j % 4, c * S1:(c + 1) * S1], block + j, c * 4 + k, YS_H[:, y], YS_L[:, y],
                                     k == 0, k == 3)
                mm.then_inc(blocks_done, 1)

        def act_branch_parts(act, l):
            act.wait_ge(branches_ready, l + 1)
            nc.scalar.activation(YS_H[:, :, :], YS, ACT.Copy).then_inc(branch_parts, 1)

        def dve_branch_parts(dve, l):
            dve.sem_inc(branches_ready, 1)
            dve.wait_ge(branch_parts, 2 * l + 1)
            nc.vector.tensor_tensor(YS_L[:, :, :], YS, YS_H[:, :, :].bitcast(F32), ALU.subtract).then_inc(branch_parts, 1)

        def act_merge(act, l):
            block, _ = BLOCKS["w_branch", l]
            for j in range(12):
                act_split(act, block + j + SPLIT)
                if j % 3 == 2:
                    act.wait_ge(merged_ready, KC * l + 2 * (j // 3) + 2)
                    for k in (2 * (j // 3), 2 * (j // 3) + 1):
                        nc.scalar.activation(H1_H[:, k], H[:, k, 0:S1], ACT.Copy).then_inc(act_high, 1)

        def dve_merge(dve, l):
            block, _ = BLOCKS["w_branch", l]
            product = arena(SCR, 2, 512)
            for j in range(12):
                dve_split(dve, block + j + SPLIT)
                dve.wait_ge(blocks_done, block + j + 1)
                pair, n = divmod(j, 3)
                gate = PT[:, GL + 8 * n + 2 * pair:GL + 8 * n + 2 * pair + 2]
                dest = H[:, 2 * pair:2 * pair + 2, 0:S1]
                psum = PS[:, j % 4, :].rearrange("p (a b) -> p a b", a=2)
                to = dest if n == 0 else product[:, n - 1].rearrange("p (a b) -> p a b", a=2)
                nc.vector.tensor_tensor(to, psum, gate, ALU.mult).then_inc(merged_part, 1)
                dve.wait_ge(merged_part, 12 * l + j + 1)
                if n:
                    dve_chain(nc.vector.tensor_tensor(dest, dest, to, ALU.add))
                if n == 2:
                    dve.sem_inc(merged_ready, 2)
            dve_parts(dve, ("w_out", l), H[:, :, 0:S1], H1_H, H1_L)

        inner_high, inner_low = sem("inner_high_ready"), sem("inner_low_ready")

        def pe_ffn(pe, use, l, f):
            block, _ = BLOCKS[f"ffn_in{f}", l]
            pe.wait_ge(act_low, KC * (JOBS["ffn", use] + 1))
            with pe.Fori(0, FF_CH // 2) as g:
                for u in range(4):
                    pe_arrived(pe, block + u, g)
                    pe.wait_ge(ups_taken if u % 2 else gates_taken, g * 2 + FF_CH * use + u // 2 + 1)
                    for k in range(KC):
                        mm = pe_tile(PS[:, u, 0:S2], block + u, k, H2_H[:, k], H2_L[:, k], k == 0, k == KC - 1)
                    mm.then_inc(blocks_done, 1)
            pe.wait_ge(inner_low, FF_CH * (use + 1))
            block, _ = BLOCKS[f"ffn_out{f}", l]

            def rows(n, k, g=None, first=False, last=False):
                pe_arrived(pe, n, g)
                for m in range(KC):
                    mm = pe_tile(PS[:, m, 0:S2], n, m, F_H[:, k], F_L[:, k], first, last)
                mm.then_inc(blocks_done, 1)

            for u in range(4):
                rows(block + u, u, first=(u == 0))
            with pe.Fori(0, 4) as g:
                for u in range(4):
                    rows(block + 4 + u, g * 4 + (4 + u), g)
            for u in range(20, 22):
                rows(block + u, u, last=(u == 21))

        def act_ffn(act, use, l, f):
            block, _ = BLOCKS[f"ffn_in{f}", l]
            with act.Fori(0, FF_CH // 2) as g:
                for u in range(2):
                    act_split(act, block + 2 * u + SPLIT, g)
                    act.wait_ge(ups_taken, g * 2 + FF_CH * use + u + 1)
                    act.wait_ge(blocks_done, g * 4 + block + 2 * u + 1)
                    nc.scalar.activation(FFN_GATE[:, u], PS[:, 2 * u, 0:S2], ACT.Silu).then_inc(gates_taken, 1)
                    act_split(act, block + 2 * u + 1 + SPLIT, g)
                    act.wait_ge(ups_taken, g * 2 + FF_CH * use + u + 3)
                    act.wait_ge(blocks_done, 1)
                    nc.scalar.activation(F_H[:, g * 2 + u], FFN_PROD[:, u], ACT.Copy).then_inc(inner_high, 1)
            split_ahead(act, act_split, *BLOCKS[f"ffn_out{f}", l])

        def dve_ffn(dve, use, l, f):
            block, _ = BLOCKS[f"ffn_in{f}", l]
            with dve.Fori(0, FF_CH // 2) as g:
                for u in range(2):
                    dve_split(dve, block + 2 * u + SPLIT, g)
                    dve.wait_ge(gates_taken, g * 2 + FF_CH * use + u + 3)
                    dve.wait_ge(blocks_done, g * 4 + block + 2 * u + 2)
                    nc.vector.tensor_tensor(FFN_PROD[:, u], FFN_GATE[:, u], PS[:, 2 * u + 1, 0:S2], ALU.mult)\
                        .then_inc(ups_taken, 1)
                    dve_split(dve, block + 2 * u + 1 + SPLIT, g)
                    dve.wait_ge(inner_high, g * 2 + FF_CH * use + u + 1)
                    nc.vector.tensor_tensor(F_L[:, g * 2 + u], FFN_PROD[:, u], F_H[:, g * 2 + u].bitcast(F32), ALU.subtract)\
                        .then_inc(inner_low, 1)
            block, count = BLOCKS[f"ffn_out{f}", l]
            split_ahead(dve, dve_split, block, count)
            dve.wait_ge(blocks_done, block + count)
            for m in range(KC):
                nc.vector.scalar_tensor_tensor(out=X[:, m], in0=PS[:, m, 0:S2], scalar=0.5, in1=X[:, m],
                                               op0=ALU.mult, op1=ALU.add)
        LEVELS = 6
        inv = {k: sem("inverse_" + k) for k in ("masked", "y_ready", "y_taken", "x_ready", "xt_ready", "new")}
        levels = const("levels", T2).rearrange("p (a b) -> p a b", a=7)

        def four(bank):
            return PS[0:T2, bank, 0:4 * T2].rearrange("p (a b) -> p a b", a=4)

        def mats(at, n=16):
            return AR[0:T2, at:at + n * T2].rearrange("p (a b) -> p a b", a=n)

        def pe_inverse(pe, use, B):
            for g in range(4):
                for j in range(4):
                    mm = nc.tensor.transpose(four(g)[:, j], B["XT"][0][:, 4 * g + j], IDENT[0:T2, 0:T2])
                mm.then_inc(inv["x_ready"], 1)
            for i in range(LEVELS):
                X_, XT_ = B["X"][i % 2], B["XT"][i % 2]
                pe.wait_ge(inv["masked"], LEVELS * use + i + 1)
                for g in range(4):
                    pe.wait_ge(inv["new"], 28 * use + 4 * i + g + 1)
                    for j in range(4):
                        mm = nc.tensor.matmul(four(g)[:, j], B["UM"][i % 2][:, 4 * g + j], X_[:, 4 * g + j],
                                              start=True, stop=True)
                    mm.then_inc(inv["y_ready"], 1)
                for g in range(4):
                    pe.wait_ge(inv["y_taken"], 24 * use + 4 * i + g + 1)
                    for j in range(4):
                        mm = nc.tensor.matmul(four(4 + g)[:, j], B["Y"][:, 4 * g + j], XT_[:, 4 * g + j],
                                              start=True, stop=True)
                    mm.then_inc(inv["xt_ready"], 1)
                    if i < LEVELS - 1:
                        for j in range(4):
                            mm = nc.tensor.matmul(four(g)[:, j], XT_[:, 4 * g + j], B["Y"][:, 4 * g + j],
                                                  start=True, stop=True)
                        mm.then_inc(inv["x_ready"], 1)

        def act_inverse(act, use, B):
            for i in range(LEVELS):
                for g in range(4):
                    act.wait_ge(inv["y_ready"], 24 * use + 4 * i + g + 1)
                    if i:
                        act.wait_ge(inv["xt_ready"], 24 * use + 4 * (i - 1) + g + 1)
                        act.wait_ge(inv["x_ready"], 24 * use + 4 * i + g + 1)
                    nc.scalar.activation(B["Y"][:, 4 * g:4 * g + 4], four(g), ACT.Copy).then_inc(inv["y_taken"], 1)

        def pool_inverse(pool, use, B):
            for i in range(LEVELS):
                if i >= 2:
                    pool.wait_ge(inv["y_ready"], 24 * use + 4 * (i - 1))
                nc.gpsimd.tensor_tensor(B["UM"][i % 2], B["U"], levels[:, i + 1:i + 2].broadcast_to([T2, 16, T2]),
                                        ALU.mult).then_inc(inv["masked"], 1)

        def dve_inverse(dve, use, B):
            for g in range(4):
                dve.wait_ge(inv["x_ready"], 24 * use + g + 1)
                nc.vector.tensor_copy(B["X"][0][:, 4 * g:4 * g + 4], four(g)).then_inc(inv["new"], 1)
            for i in range(LEVELS):
                a, b = i % 2, 1 - i % 2
                for g in range(4):
                    s = slice(4 * g, 4 * g + 4)
                    dve.wait_ge(inv["xt_ready"], 24 * use + 4 * i + g + 1)
                    step = nc.vector.tensor_tensor(B["XT"][b][:, s], B["XT"][a][:, s], four(4 + g), ALU.subtract)
                    if i < LEVELS - 1:
                        dve_chain(step)
                        dve.wait_ge(inv["x_ready"], 24 * use + 4 * (i + 1) + g + 1)
                        step = nc.vector.tensor_tensor(B["X"][b][:, s], B["X"][a][:, s], four(g), ALU.subtract)
                    step.then_inc(inv["new"], 1)

        def dve_first_level(B):
            dve_chain(nc.vector.tensor_tensor(B["XT"][0], B["U"], levels[:, 0:1].broadcast_to([T2, 16, T2]), ALU.mult))
            dve_chain(nc.vector.tensor_tensor(B["XT"][0], IDENT[0:T2, 0:T2].unsqueeze(1).broadcast_to([T2, 16, T2]),
                                              B["XT"][0], ALU.subtract))

        HP = arena(0, HYB_CH, S2)
        CO = arena(7616, 12, S2)
        FVN = AR[0:T2, 10880:12928].rearrange("p (a b) -> p a b", a=4)
        ROWS = arena(12928, 6, S2)
        FA, FB, GA, GB = (arena(14560 + 1088 * j, 4, S2) for j in range(4))
        BR = arena(18912, 4, S2)
        BETA_B, GC_B, EGC = (arena(20000 + 1088 * j, 4, S2) for j in range(3))
        KBT, KBET, QD, KDT = (arena(23264 + 1088 * j, 4, S2) for j in range(4))
        FOX = place_attention(Attn("F", 0), 27616)
        Y8 = arena(31840, 8, S2)
        GI = {"U": mats(0), "X": [mats(2176), mats(3264)], "XT": [mats(4352), mats(5440)],
              "Y": mats(27616), "UM": [mats(28704), mats(29792)]}
        ATT, DEC = mats(1088), mats(34016)
        VBN, KBEN, KDN = (AR[0:T2, at:at + 2048].rearrange("p (a b) -> p a b", a=16) for at in (10880, 14560, 20000))
        WT = arena(34016, 16, T2)
        UN = AR[0:T2, 35104:35616].rearrange("p (a b) -> p a b", a=4)
        GS = arena(36128, 4, P)
        MIX_H, MIX_L = parts("mixer", 23264, KC, S2)
        DK = 128

        def tiles(v, c):
            return v[:, :, c * T2:(c + 1) * T2]

        hs = {k: sem("hybrid_" + k) for k in (
            "small_ready", "z_ready", "rows_ready", "one_plus", "log_ready", "sigmoid_ready", "cleared", "values_turned",
            "conv_ready", "bound", "l2_ready", "l2_mean", "l2_root", "spread", "spread_taken", "prep", "grams", "decay",
            "decay_exp", "gram_taken", "turned", "turned_taken", "w_ready", "w_taken", "u_ready", "u_taken", "o_ready",
            "o_taken", "s_ready", "s_taken", "gate", "onorm", "osum", "omean", "oroot", "outputs")}

        def pe_hybrid_in(pe):
            small = vec("hyb_small").rearrange("p (k c) -> p k c", k=KC)
            for k in range(KC):
                mm = nc.tensor.matmul(PS[0:T2, 5, 0:S2], small[:, k], H[:, k], start=(k == 0), stop=(k == KC - 1))
            mm.then_inc(hs["small_ready"], 1)

        def dve_hybrid_rows(dve):
            z, t, sp, c, nc_ = (ROWS[0:36, j] for j in range(5))
            dve.wait_ge(hs["small_ready"], 1)
            dve_chain(nc.vector.tensor_scalar(z, PS[0:36, 5, 0:S2], vec("gate_b", 0, 1, 36), const("gate_sign", 36), ALU.add, ALU.mult))
            dve.sem_inc(hs["z_ready"], 1)
            for j in range(12):
                w = lambda tap: vec("conv", 4 * j + tap, 1)
                dve_chain(nc.vector.tensor_scalar(CO[:, j], HP[:, GQ + j], w(3), None, ALU.mult))
                for back in (1, 2, 3):
                    step = nc.vector.scalar_tensor_tensor(out=CO[:, j, back:], in0=HP[:, GQ + j, 0:S2 - back], scalar=w(3 - back),
                                                          in1=CO[:, j, back:], op0=ALU.mult, op1=ALU.add)
                    dve_chain(step)
            dve.sem_inc(hs["conv_ready"], 1)
            dve.wait_ge(hs["one_plus"], 1)
            dve_chain(nc.vector.tensor_scalar(t, t, 1.0, None, ALU.add))
            dve_chain(nc.vector.tensor_scalar(SM[0:36, 1:2], SM[0:36, 0:1], -1.0, None, ALU.mult))
            dve.sem_inc(hs["z_ready"], 1)
            dve.wait_ge(hs["log_ready"], 1)
            dve_chain(nc.vector.scalar_tensor_tensor(out=sp, in0=z, scalar=0.0, in1=t, op0=ALU.max, op1=ALU.add))
            dve_chain(nc.vector.tensor_scalar(sp, sp, SM[0:36, 1:2], None, ALU.mult))
            dve_chain(nc.vector.tensor_tensor_scan(ROWS[0:8, 3], const("row_one", 8), ROWS[0:8, 2], 0.0, ALU.mult, ALU.add))
            dve_chain(nc.vector.tensor_tensor_scan(ROWS[32:36, 3], C[32:36, CONST["restart"][0]:CONST["restart"][0] + S2],
                                                   ROWS[32:36, 2], 0.0, ALU.mult, ALU.add))
            dve_chain(nc.vector.tensor_scalar(ROWS[0:8, 3], ROWS[0:8, 3], 8.0, None, ALU.mult))
            dve_chain(nc.vector.tensor_scalar(ROWS[0:8, 4], ROWS[0:8, 3], -1.0, None, ALU.mult))
            dve_chain(nc.vector.tensor_scalar(ROWS[32:36, 4], ROWS[32:36, 3], -1.0, None, ALU.mult))
            dve.sem_inc(hs["rows_ready"], 1)

        def act_hybrid_rows(act):
            act.wait_ge(hs["z_ready"], 1)
            act_chain(nc.scalar.activation(ROWS[0:36, 1], ROWS[0:36, 0], ACT.Abs))
            act_chain(nc.scalar.activation(ROWS[0:36, 1], ROWS[0:36, 1], ACT.Exp, scale=-1.0))
            act_chain(nc.scalar.activation(SM[0:36, 0:1], vec("gate_b", 1, 1, 36), ACT.Exp))
            act.sem_inc(hs["one_plus"], 1)
            act.wait_ge(hs["z_ready"], 2)
            act_chain(nc.scalar.activation(ROWS[0:36, 1], ROWS[0:36, 1], ACT.Ln))
            act.sem_inc(hs["log_ready"], 1)
            act_chain(nc.scalar.activation(ROWS[64:68, 0], PS[64:68, 5, 0:S2], ACT.Sigmoid))
            act.sem_inc(hs["sigmoid_ready"], 1)
            for c in range(4):
                act.wait_ge(hs["values_turned"], c + 1)
                act_chain(nc.scalar.activation(FVN[:, c], PS[0:T2, c, 0:512], ACT.Copy))
            act.wait_ge(hs["conv_ready"], 1)
            act_chain(nc.scalar.activation(CO, CO, ACT.Silu))
            act_chain(nc.scalar.activation(HP[:, GZ:GZ + 4], HP[:, GZ:GZ + 4], ACT.Silu))

        def pool_hybrid_rows(pool):
            for j, v in enumerate((FA, FB, GA, GB)):
                nc.gpsimd.memset(v, 0.0).then_inc(hs["cleared"], 1)
            pool.wait_ge(hs["cleared"], 4)
            for j, (v, p) in enumerate(((FA, 32), (FA, 96), (FB, 0), (FB, 64), (GA, 32), (GB, 0))):
                nc.gpsimd.memset(v[p:p + 1], 1.0).then_inc(hs["cleared"], 1)

        def sp_hybrid_rows(sp):
            sp.wait_ge(hs["cleared"], 10)
            sp.wait_ge(hs["rows_ready"], 1)
            sp.wait_ge(hs["sigmoid_ready"], 1)
            for h in range(F_HEADS):
                p = 64 * (h % 2)
                sp.dma_start(FA[p:p + 1, h // 2], ROWS[h:h + 1, 3]).then_inc(hs["bound"], 16)
                sp.dma_start(FB[p + 32:p + 33, h // 2], ROWS[h:h + 1, 4]).then_inc(hs["bound"], 16)
            for h in range(G_HEADS):
                sp.dma_start(GA[0:1, h], ROWS[32 + h:33 + h, 3]).then_inc(hs["bound"], 16)
                sp.dma_start(GB[32:33, h], ROWS[32 + h:33 + h, 4]).then_inc(hs["bound"], 16)
                sp.dma_start(BR[0:1, h], ROWS[64 + h:65 + h, 0]).then_inc(hs["bound"], 16)

        N_ROW_DMAS = 2 * F_HEADS + 3 * G_HEADS

        def pe_fox_values(pe):
            for c in range(4):
                for j in range(4):
                    mm = nc.tensor.transpose(PS[0:T2, c, j * P:(j + 1) * P], HP[:, FV + j, c * T2:(c + 1) * T2], IDENT)
                mm.then_inc(hs["values_turned"], 1)

        def act_delta_prep(act):
            act_chain(nc.scalar.activation(SQ[:, :, :], CO[:, 0:8], ACT.Square))
            act.sem_inc(hs["l2_ready"], 1)
            act.wait_ge(hs["l2_mean"], 1)
            act_chain(nc.scalar.activation(H[:, :, :], H[:, :, :], ACT.Ln))
            act_chain(nc.scalar.activation(H[:, :, :], H[:, :, :], ACT.Exp, scale=-0.5))
            act.sem_inc(hs["l2_root"], 1)
            act.wait_ge(hs["spread"], 8)
            act_chain(nc.scalar.activation(GC_B, PS[:, 0:4, 0:S2], ACT.Copy))
            act_chain(nc.scalar.activation(EGC, PS[:, 0:4, 0:S2], ACT.Exp))
            act_chain(nc.scalar.activation(BETA_B, PS[:, 4:8, 0:S2], ACT.Copy))
            act.sem_inc(hs["spread_taken"], 1)
            act.wait_ge(hs["prep"], 1)
            act_chain(nc.scalar.activation(KDT, KDT, ACT.Exp))
            act.sem_inc(hs["spread_taken"], 1)

        def pe_delta_prep(pe):
            pe.wait_ge(hs["l2_ready"], 1)
            for j in range(8):
                mm = nc.tensor.matmul(PS[:, j, 0:S2], ONES, SQ[:, j], start=True, stop=True)
            mm.then_inc(hs["l2_ready"], 1)
            pe.wait_ge(hs["l2_mean"], 1)
            pe.wait_ge(hs["bound"], 16 * N_ROW_DMAS)
            for j in range(8):
                row = GA[0:1, j] if j < 4 else BR[0:1, j - 4]
                nc.tensor.matmul(PS[:, j, 0:S2], ONES[0:1, :], row, start=True, stop=True).then_inc(hs["spread"], 1)

        def dve_delta_prep(dve):
            dve.wait_ge(hs["l2_ready"], 2)
            dve_chain(nc.vector.tensor_scalar(H[:, :, :], PS[:, :, 0:S2], EPS, None, ALU.add))
            dve.sem_inc(hs["l2_mean"], 1)
            dve.wait_ge(hs["l2_root"], 1)
            q, k, v = CO[:, 0:4], CO[:, 4:8], CO[:, 8:12]
            flat = lambda a: a.rearrange("p a b -> p (a b)")
            dve_chain(nc.vector.scalar_tensor_tensor(out=flat(q), in0=flat(q), scalar=DK ** -0.5, in1=flat(H[:, 0:4]),
                                                     op0=ALU.mult, op1=ALU.mult))
            dve_chain(nc.vector.tensor_tensor(k, k, H[:, 4:8], ALU.mult))
            dve.wait_ge(hs["spread_taken"], 1)
            gc = flat(GC_B).rearrange("p (a b) -> p a b", b=T2)
            dve_chain(nc.vector.tensor_tensor(flat(KDT).rearrange("p (a b) -> p a b", b=T2),
                                              gc[:, :, T2 - 1:T2].broadcast_to([P, 16, T2]), gc, ALU.subtract))
            dve.sem_inc(hs["prep"], 1)
            dve_chain(nc.vector.tensor_tensor(KBT, k, BETA_B, ALU.mult))
            dve_chain(nc.vector.tensor_tensor(KBET, KBT, EGC, ALU.mult))
            dve_chain(nc.vector.tensor_tensor(QD, q, EGC, ALU.mult))
            dve_chain(nc.vector.tensor_tensor(v, v, BETA_B, ALU.mult))
            dve.wait_ge(hs["spread_taken"], 2)
            dve_chain(nc.vector.tensor_tensor(KDT, KDT, k, ALU.mult))

        def pe_delta_grams(pe):
            for c in range(4):
                if c >= 2:
                    pe.wait_ge(hs["gram_taken"], c - 1)
                b = 3 * (c % 2)
                for h in range(4):
                    cols = slice(c * T2, (c + 1) * T2)
                    nc.tensor.matmul(four(b)[:, h], CO[:, 4 + h, cols], KBT[:, h, cols], start=True, stop=True)
                    nc.tensor.matmul(four(b + 1)[:, h], CO[:, 4 + h, cols], CO[:, h, cols], start=True, stop=True)
                    mm = nc.tensor.matmul(four(b + 2)[:, h], GB[0:33, h, cols], GA[0:33, h, cols], start=True, stop=True)
                mm.then_inc(hs["grams"], 1)
            for j in range(12):
                src = (CO[:, 8:12], KBET, KDT)[j % 3]
                c = j // 3
                if j >= 2:
                    pe.wait_ge(hs["turned_taken"], j - 1)
                for h in range(4):
                    mm = nc.tensor.transpose(PS[0:T2, 6 + j % 2, h * P:(h + 1) * P], src[:, h, c * T2:(c + 1) * T2], IDENT)
                mm.then_inc(hs["turned"], 1)

        def act_delta_grams(act):
            for c in range(4):
                act.wait_ge(hs["decay"], c + 1)
                nc.scalar.activation(DEC[:, 4 * c:4 * c + 4], DEC[:, 4 * c:4 * c + 4], ACT.Exp).then_inc(hs["decay_exp"], 1)
            for j in range(12):
                act.wait_ge(hs["turned"], j + 1)
                dest = (VBN, KBEN, KDN)[j % 3][:, 4 * (j // 3):4 * (j // 3) + 4]
                nc.scalar.activation(dest, PS[0:T2, 6 + j % 2, :].rearrange("p (a b) -> p a b", a=4), ACT.Copy)\
                    .then_inc(hs["turned_taken"], 1)

        def dve_delta_grams(dve):
            tri = const("tri", T2).rearrange("p (a b) -> p a b", a=4)
            neg = const("neg_tri", T2).unsqueeze(1).broadcast_to([T2, 4, T2])
            for c in range(4):
                b, s = 3 * (c % 2), slice(4 * c, 4 * c + 4)
                dve.wait_ge(hs["grams"], c + 1)
                nc.vector.tensor_tensor(DEC[:, s], four(b + 2), neg, ALU.add).then_inc(hs["decay"], 1)
                dve.wait_ge(hs["decay_exp"], c + 1)
                dve_chain(nc.vector.tensor_tensor(GI["U"][:, s], four(b), DEC[:, s], ALU.mult))
                dve_chain(nc.vector.tensor_tensor(GI["U"][:, s], GI["U"][:, s], tri[:, 0:1].broadcast_to([T2, 4, T2]), ALU.mult))
                nc.vector.tensor_tensor(ATT[:, s], four(b + 1), DEC[:, s], ALU.mult).then_inc(hs["gram_taken"], 1)
            dve_first_level(GI)

        def pe_delta_scan(pe):
            XT = GI["XT"][0]
            for c in range(4):
                for h in range(4):
                    mm = nc.tensor.matmul(PS[:, c, h * T2:(h + 1) * T2], KBEN[:, 4 * c + h], XT[:, 4 * c + h], start=True, stop=True)
                mm.then_inc(hs["w_ready"], 1)
            for c in range(4):
                cols = slice(c * T2, (c + 1) * T2)
                if c == 0:
                    pe.wait_ge(hs["w_taken"], 4)
                if c:
                    pe.wait_ge(hs["s_taken"], c)
                for h in range(4):
                    mm = nc.tensor.matmul(PS[0:T2, 4, h * P:(h + 1) * P], XT[:, 4 * c + h], VBN[:, 4 * c + h], start=True, stop=(c == 0))
                    if c:
                        mm = nc.tensor.matmul(PS[0:T2, 4, h * P:(h + 1) * P], WT[:, 4 * c + h], GS[:, h], start=False, stop=True)
                mm.then_inc(hs["u_ready"], 1)
                pe.wait_ge(hs["u_taken"], c + 1)
                for h in range(4):
                    mm = nc.tensor.matmul(PS[:, 6, h * P:(h + 1) * P], KDN[:, 4 * c + h], UN[:, h], start=True, stop=True)
                mm.then_inc(hs["s_ready"], 1)
                if c:
                    pe.wait_ge(hs["o_taken"], c)
                for h in range(4):
                    if c:
                        nc.tensor.matmul(PS[:, 5, h * T2:(h + 1) * T2], GS[:, h], QD[:, h, cols], start=True, stop=False)
                    mm = nc.tensor.matmul(PS[:, 5, h * T2:(h + 1) * T2], UN[:, h], ATT[:, 4 * c + h], start=(c == 0), stop=True)
                mm.then_inc(hs["o_ready"], 1)

        def act_delta_scan(act):
            for c in range(4):
                act.wait_ge(hs["w_ready"], c + 1)
                nc.scalar.activation(WT[:, 4 * c:4 * c + 4], PS[:, c, 0:4 * T2].rearrange("p (a b) -> p a b", a=4),
                                     ACT.Copy, scale=-1.0).then_inc(hs["w_taken"], 1)
            for c in range(4):
                act.wait_ge(hs["o_ready"], c + 1)
                nc.scalar.activation(tiles(Y8[:, 4:8], c), PS[:, 5, 0:4 * T2].rearrange("p (a b) -> p a b", a=4), ACT.Copy)\
                    .then_inc(hs["o_taken"], 1)

        def dve_delta_scan(dve):
            dl = EGC.rearrange("p h (c t) -> p h c t", c=4)
            for c in range(4):
                dve.wait_ge(hs["u_ready"], c + 1)
                nc.vector.tensor_copy(UN, PS[0:T2, 4, :].rearrange("p (a b) -> p a b", a=4)).then_inc(hs["u_taken"], 1)
                dve.wait_ge(hs["s_ready"], c + 1)
                new = PS[:, 6, :].rearrange("p (a b) -> p a b", a=4)
                if c == 0:
                    nc.vector.tensor_copy(GS, new).then_inc(hs["s_taken"], 1)
                else:
                    dve.wait_ge(hs["o_ready"], c + 1)
                    dve_chain(nc.vector.tensor_tensor(GS, GS, dl[:, :, c, T2 - 1:T2].broadcast_to([P, 4, P]), ALU.mult))
                    nc.vector.tensor_tensor(GS, GS, new, ALU.add).then_inc(hs["s_taken"], 1)
                dve.wait_ge(hs["s_taken"], c + 1)

        def act_delta_out(act):
            act_chain(nc.scalar.activation(SQ[:, 0:4], Y8[:, 4:8], ACT.Square))
            act.sem_inc(hs["onorm"], 1)
            act.wait_ge(hs["omean"], 1)
            act_chain(nc.scalar.activation(SQ[:, 4:8], SQ[:, 4:8], ACT.Ln))
            act_chain(nc.scalar.activation(SQ[:, 4:8], SQ[:, 4:8], ACT.Exp, scale=-0.5))
            act.sem_inc(hs["oroot"], 1)

        def pe_delta_out(pe):
            pe.wait_ge(hs["onorm"], 1)
            for h in range(4):
                mm = nc.tensor.matmul(PS[:, 4 + h, 0:S2], ONES, SQ[:, h], start=True, stop=True)
            mm.then_inc(hs["osum"], 1)

        def dve_delta_out(dve):
            dve.wait_ge(hs["osum"], 1)
            dve_chain(nc.vector.tensor_scalar(SQ[:, 4:8], PS[:, 4:8, 0:S2], 1.0 / 128, EPS, ALU.mult, ALU.add))
            dve.sem_inc(hs["omean"], 1)
            dve.wait_ge(hs["oroot"], 1)
            flat = lambda a: a.rearrange("p a b -> p (a b)")
            y = flat(Y8[:, 4:8])
            dve_chain(nc.vector.scalar_tensor_tensor(out=y, in0=y, scalar=vec("o_gain"), in1=flat(SQ[:, 4:8]), op0=ALU.mult, op1=ALU.mult))
            dve_chain(nc.vector.tensor_tensor(y, y, flat(HP[:, GZ:GZ + 4]), ALU.mult))
            dve.sem_inc(hs["outputs"], KC)
        LI, LO = arena(0, KC, 288), arena(2304, 4, D)
        XV = [arena(6528 + 2176 * j, KC, S2) for j in range(3)]
        R_, K_, V_ = (arena(13056 + 2176 * j, KC, S2) for j in range(3))
        RKV = arena(13056, 24, S2)
        LD, A_, G_, KK, B_, AC = (arena(19584 + 2176 * j, KC, S2) for j in range(6))
        BONUS = A_
        KKT, RT, BT, KT, BH, KH = (arena(2176 * j, KC, S2) for j in range(6))
        LT = arena(34624, 4, S2)
        G4 = AR[0:T2, 26112:26112 + 64 * T2].rearrange("p (h m t) -> p h m t", h=16, m=4)
        BHN, KHN, VN = (AR[0:T2, 30464 + 1024 * j:30464 + 1024 * (j + 1)] for j in range(3))
        RI = {"U": G4[:, :, 0], "X": [mats(13056), mats(14144)], "XT": [mats(15232), mats(16320)],
              "Y": mats(19584), "UM": [mats(20672), mats(33536)]}
        RS_ = arena(34624, KC, 64)
        RS2 = arena(35136, KC, 64)
        UR = AR[0:T2, 35648:36672].rearrange("p (h v) -> p h v", h=16)
        UV = SQ[0:T2, 0:4, :].rearrange("p a b -> p (a b)")[:, 0:1024].rearrange("p (h v) -> p h v", h=16)
        YT = H
        RV = [parts("rwkv_r", 26112, KC, S2), parts("rwkv_k", 30464, KC, S2), parts("rwkv_v", 0, KC, S2)]
        RO_H, RO_L = parts("rwkv_out", 0, KC, S2)
        EC = sb("chunk_decay", [P, KC, NT2])
        MU1 = sb("one_minus_k_a", [P, KC])

        rs = {k: sem("rwkv_" + k) for k in (
            "shifted", "lora_in", "lora_act", "lora_out", "lora_taken", "lora_loaded", "mixed", "sq", "ssum", "smean", "sroot",
            "cum", "ex", "ex_used", "bonus_in", "bonus_sum", "grams", "gram_taken", "turned", "turned_taken",
            "ur_ready", "ur_taken", "u_ready", "u_taken", "y_ready", "y_taken", "s_ready", "s_taken",
            "gn_sum", "gn_centred", "gn_sq", "gn_var", "gn_mean", "gn_root", "out_ready")}

        def flat(a):
            return a.rearrange("p a b -> p (a b)")

        def dve_shift(dve):
            dve_chain(nc.vector.tensor_tensor(SQ[:, :, 1:S2], H[:, :, 0:S2 - 1], H[:, :, 1:S2], ALU.subtract))
            dve_chain(nc.vector.tensor_scalar(SQ[:, :, 0:1], H[:, :, 0:1], -1.0, None, ALU.mult))

        def dve_variant(j, dest):
            for k in range(KC):
                step = nc.vector.scalar_tensor_tensor(out=dest[:, k], in0=SQ[:, k], scalar=vec("mu", KC * j + k, 1), in1=H[:, k],
                                                      op0=ALU.mult, op1=ALU.add)
                dve_chain(step)
                dve_chain.eng.sem_inc(rs["mixed"], 1)

        def dve_lora(dve):
            dve_shift(dve)
            for j, b in ((1, 0), (4, 1), (5, 2)):
                dve_variant(j, XV[b])
            for m in range(KC):
                for q, dest in enumerate((LD, A_, G_)):
                    n = 3 * m + q
                    dve.wait_ge(rs["lora_out"], n + 1)
                    if q < 2:
                        step = nc.vector.tensor_scalar(dest[:, m], PS[:, 4 + n % 4, 0:S2], vec(("w0", "a0")[q], m, 1), None, ALU.add)
                    else:
                        step = nc.vector.tensor_copy(dest[:, m], PS[:, 4 + n % 4, 0:S2])
                    step.then_inc(rs["lora_taken"], 1)

        def pe_lora(pe):
            pe.wait_ge(rs["lora_loaded"], 32)
            spans = [(0, 0, 64), (1, 64, 64), (2, 128, 128), (2, 256, 32)]
            for j, (b, at, width) in enumerate(spans):
                pe.wait_ge(rs["mixed"], KC * (b + 1))
                for k in range(KC):
                    mm = nc.tensor.matmul(PS[0:width, j, 0:S2], LI[:, k, at:at + width], XV[b][:, k], start=(k == 0), stop=(k == KC - 1))
                mm.then_inc(rs["lora_in"], 1)
            pe.wait_ge(rs["lora_act"], 4)
            for m in range(KC):
                cols = slice(m * P, (m + 1) * P)
                for q in range(3):
                    n = 3 * m + q
                    if n >= 4:
                        pe.wait_ge(rs["lora_taken"], n - 3)
                    out_ = PS[:, 4 + n % 4, 0:S2]
                    if q < 2:
                        mm = nc.tensor.matmul(out_, LO[0:64, q, cols], LT[0:64, q], start=True, stop=True)
                    else:
                        nc.tensor.matmul(out_, LO[:, 2, cols], LT[:, 2], start=True, stop=False)
                        mm = nc.tensor.matmul(out_, LO[0:32, 3, cols], LT[0:32, 3], start=False, stop=True)
                    mm.then_inc(rs["lora_out"], 1)

        def act_lora(act):
            for j, (width, func) in enumerate(((64, ACT.Tanh), (64, ACT.Copy), (128, ACT.Sigmoid), (32, ACT.Sigmoid))):
                act.wait_ge(rs["lora_in"], j + 1)
                nc.scalar.activation(LT[0:width, j], PS[0:width, j, 0:S2], func).then_inc(rs["lora_act"], 1)

        def dve_variants(dve):
            for j, b in ((0, 0), (2, 1), (3, 2)):
                dve_variant(j, XV[b])
                dve_parts(dve, ("r", b), XV[b], *RV[b])

        def act_variants(act):
            for b in range(3):
                act_parts(act, ("r", b), XV[b], RV[b][0], rs["mixed"], KC * (3 + b))

        def act_decays(act):
            act_chain(nc.scalar.activation(LD, LD, ACT.Sigmoid))
            act_chain(nc.scalar.activation(A_, A_, ACT.Sigmoid))
            act.sem_inc(rs["cum"], 1)
            act.wait_ge(rs["sq"], 1)
            act_chain(nc.scalar.activation(H[:, :, :], KK, ACT.Square))
            act.sem_inc(rs["ssum"], 1)
            act.wait_ge(rs["smean"], 1)
            act_chain(nc.scalar.activation(H[:, :, :], H[:, :, :], ACT.Ln))
            act_chain(nc.scalar.activation(H[:, :, :], H[:, :, :], ACT.Exp, scale=-0.5))
            act.sem_inc(rs["sroot"], 1)
            act.wait_ge(rs["ex_used"], 1)
            for j, (src, scale) in enumerate(((AC, 1.0), (AC, -1.0), (SQ[:, :, :], 1.0), (SQ[:, :, :], 1.0))):
                act.wait_ge(rs["ex_used"], j + 1)
                act_chain(nc.scalar.activation(H[:, :, :], src, ACT.Exp, scale=scale))
                act.sem_inc(rs["ex"], 1)

        def pe_decays(pe):
            pe.wait_ge(rs["ssum"], 1)
            for k in range(KC):
                mm = nc.tensor.matmul(PS[:, k, 0:S2], HALF, H[:, k], start=True, stop=True)
            mm.then_inc(rs["ssum"], 1)
            pe.wait_ge(rs["bonus_in"], 1)
            for k in range(KC):
                mm = nc.tensor.matmul(PS[:, k, 0:S2], HALF, KKT[:, k], start=True, stop=True)
            mm.then_inc(rs["bonus_sum"], 1)

        def dve_decays(dve):
            def per(name, k):
                return vec(name, k, 1)
            for k in range(KC):
                dve_chain(nc.vector.tensor_scalar(KK[:, k], K_[:, k], per("k_k", k), None, ALU.mult))
            dve.sem_inc(rs["sq"], 1)
            dve_chain(nc.vector.tensor_scalar(MU1[:, :], vec("k_a"), -1.0, 1.0, ALU.mult, ALU.add))
            dve.wait_ge(rs["cum"], 1)
            for k in range(KC):
                dve_chain(nc.vector.tensor_scalar(B_[:, k], A_[:, k], per("k_a", k), MU1[:, k:k + 1], ALU.mult, ALU.add))
            dve_chain(nc.vector.tensor_tensor(K_, K_, B_, ALU.mult))
            dve_chain(nc.vector.tensor_scalar(LD, LD, -math.exp(-0.5), None, ALU.mult))
            for k in range(KC):
                dve_chain(nc.vector.tensor_tensor_scan(AC[:, k], const("restart"), LD[:, k], 0.0, ALU.mult, ALU.add))
            dve.wait_ge(rs["ssum"], 2)
            dve_chain(nc.vector.tensor_scalar(H[:, :, :], PS[:, :, 0:S2], EPS, None, ALU.add))
            dve.sem_inc(rs["smean"], 1)
            dve.wait_ge(rs["sroot"], 1)
            dve_chain(nc.vector.tensor_tensor(KK, KK, H[:, :, :], ALU.mult))
            dve_chain(nc.vector.tensor_tensor(B_, KK, A_, ALU.mult))
            for k in range(KC):
                dve_chain(nc.vector.scalar_tensor_tensor(out=KKT[:, k], in0=R_[:, k], scalar=per("r_k", k), in1=K_[:, k],
                                                         op0=ALU.mult, op1=ALU.mult))
            dve.sem_inc(rs["bonus_in"], 1)
            dve.sem_inc(rs["ex_used"], 1)
            dve_chain(nc.vector.tensor_tensor(SQ[:, :, :], AC, LD, ALU.subtract))
            dve.wait_ge(rs["bonus_sum"], 1)
            dve_chain(nc.vector.tensor_tensor(BONUS, PS[:, :, 0:S2], V_, ALU.mult))
            dve.wait_ge(rs["ex"], 1)
            dve_chain(nc.vector.tensor_tensor(RT, R_, H[:, :, :], ALU.mult))
            for c in range(NT2):
                dve_chain(nc.vector.tensor_copy(EC[:, :, c:c + 1], H[:, :, (c + 1) * T2 - 1:(c + 1) * T2]))
            dve.sem_inc(rs["ex_used"], 1)
            dve.wait_ge(rs["ex"], 2)
            dve_chain(nc.vector.tensor_tensor(BT, B_, H[:, :, :], ALU.mult))
            dve_chain(nc.vector.tensor_tensor(KT, K_, H[:, :, :], ALU.mult))
            dve.sem_inc(rs["ex_used"], 1)
            dve.wait_ge(rs["ex"], 3)
            dve_chain(nc.vector.tensor_tensor(KKT, KK, H[:, :, :], ALU.mult))
            for c in range(NT2):
                t = slice(c * T2, (c + 1) * T2)
                dve_chain(nc.vector.tensor_tensor(SQ[:, :, t], AC[:, :, (c + 1) * T2 - 1:(c + 1) * T2].broadcast_to([P, KC, T2]),
                                                  AC[:, :, t], ALU.subtract))
            dve.sem_inc(rs["ex_used"], 1)
            dve.wait_ge(rs["ex"], 4)
            dve_chain(nc.vector.tensor_tensor(BH, B_, H[:, :, :], ALU.mult))
            dve_chain(nc.vector.tensor_tensor(KH, K_, H[:, :, :], ALU.mult))

        def pe_rwkv_grams(pe, c):
            cols = slice(c * T2, (c + 1) * T2)
            for h in range(R_HEADS):
                if h >= 4:
                    pe.wait_ge(rs["gram_taken"], R_HEADS * c + h - 3)
                r, k = slice(64 * (h % 2), 64 * (h % 2) + 64), h // 2
                for m, (left, right) in enumerate(((BT, KKT), (BT, RT), (KT, KKT), (KT, RT))):
                    mm = nc.tensor.matmul(four(h % 4)[:, m], left[r, k, cols], right[r, k, cols], start=True, stop=True)
                mm.then_inc(rs["grams"], 1)
            for j in range(6):
                src = (BH, KH, V_)[j // 2]
                if j >= 4:
                    pe.wait_ge(rs["turned_taken"], 6 * c + j - 3)
                for k in range(4):
                    mm = nc.tensor.transpose(PS[0:T2, 4 + j % 4, k * P:(k + 1) * P], src[:, 4 * (j % 2) + k, cols], IDENT)
                mm.then_inc(rs["turned"], 1)

        def act_rwkv_grams(act, c):
            for j in range(6):
                act.wait_ge(rs["turned"], 6 * c + j + 1)
                nc.scalar.activation((BHN, KHN, VN)[j // 2][:, 512 * (j % 2):512 * (j % 2) + 512], PS[0:T2, 4 + j % 4, :], ACT.Copy)\
                    .then_inc(rs["turned_taken"], 1)

        def dve_rwkv_grams(dve, c):
            tri = const("tri", T2).rearrange("p (a b) -> p a b", a=4)
            for h in range(R_HEADS):
                dve.wait_ge(rs["grams"], R_HEADS * c + h + 1)
                nc.vector.tensor_tensor(G4[:, h], four(h % 4), tri, ALU.mult).then_inc(rs["gram_taken"], 1)
            dve.wait_ge(rs["gram_taken"], R_HEADS * (c + 1))
            dve_first_level(RI)

        def pe_rwkv_scan(pe, c):
            cols = slice(c * T2, (c + 1) * T2)
            XT = RI["XT"][0]

            def rows(h):
                return slice(64 * (h % 2), 64 * (h % 2) + 64), h // 2

            def head(v, h):
                return v[:, h * 64:(h + 1) * 64]
            for h in range(R_HEADS):
                r, k = rows(h)
                o = PS[0:T2, h % 2, k * 64:(k + 1) * 64]
                if c:
                    nc.tensor.matmul(o, KKT[r, k, cols], STATE[c % 2][r, k], start=True, stop=False)
                mm = nc.tensor.matmul(o, G4[:, h, 2], head(VN, h), start=(c == 0), stop=True)
            mm.then_inc(rs["ur_ready"], 1)
            pe.wait_ge(rs["ur_taken"], c + 1)
            for h in range(R_HEADS):
                mm = nc.tensor.matmul(PS[0:T2, 2 + h % 2, (h // 2) * 64:(h // 2 + 1) * 64], XT[:, h], UR[:, h], start=True, stop=True)
            mm.then_inc(rs["u_ready"], 1)
            pe.wait_ge(rs["u_taken"], c + 1)
            for h in range(R_HEADS):
                r, k = rows(h)
                o = PS[r, 6, k * 64:(k + 1) * 64]
                nc.tensor.matmul(o, head(BHN, h), UV[:, h], start=True, stop=False)
                mm = nc.tensor.matmul(o, head(KHN, h), head(VN, h), start=False, stop=True)
            mm.then_inc(rs["s_ready"], 1)
            for h in range(R_HEADS):
                r, k = rows(h)
                o = PS[r, 4 + k // 4, (k % 4) * T2:(k % 4 + 1) * T2]
                if c:
                    nc.tensor.matmul(o, STATE[c % 2][r, k], RT[r, k, cols], start=True, stop=False)
                nc.tensor.matmul(o, UV[:, h], G4[:, h, 1], start=(c == 0), stop=False)
                mm = nc.tensor.matmul(o, head(VN, h), G4[:, h, 3], start=False, stop=True)
            mm.then_inc(rs["y_ready"], 1)

        STATE = [RS_, RS2]

        def act_rwkv_scan(act, c):
            act.wait_ge(rs["u_ready"], c + 1)
            for odd in range(2):
                step = nc.scalar.activation(UV.rearrange("p (k o) v -> p o k v", o=2)[:, odd], PS[0:T2, 2 + odd, :].rearrange(
                    "p (k v) -> p k v", k=KC), ACT.Copy, scale=-1.0)
                act_chain(step)
            act.sem_inc(rs["u_taken"], 1)
            act.wait_ge(rs["y_ready"], c + 1)
            for b in range(2):
                act_chain(nc.scalar.activation(YT[:, 4 * b:4 * b + 4, c * T2:(c + 1) * T2],
                                               PS[:, 4 + b, 0:4 * T2].rearrange("p (a b) -> p a b", a=4), ACT.Copy))

        def dve_rwkv_scan(dve, c):
            dve.wait_ge(rs["ur_ready"], c + 1)
            for odd in range(2):
                dve_chain(nc.vector.tensor_copy(UR.rearrange("p (k o) v -> p o k v", o=2)[:, odd],
                                                PS[0:T2, odd, :].rearrange("p (k v) -> p k v", k=KC)))
            dve.sem_inc(rs["ur_taken"], 1)
            new, old = STATE[(c + 1) % 2], STATE[c % 2]
            if c == NT2 - 1:
                return
            dve.wait_ge(rs["s_ready"], c + 1)
            add = PS[:, 6, :].rearrange("p (k v) -> p k v", k=KC)
            if c == 0:
                dve_chain(nc.vector.tensor_copy(new, add))
            else:
                dve_chain(nc.vector.tensor_tensor(new, old, EC[:, :, c:c + 1].broadcast_to([P, KC, 64]), ALU.mult))
                dve_chain(nc.vector.tensor_tensor(new, new, add, ALU.add))

        GN_EPS = 64e-5

        def pe_rwkv_out(pe):
            for k in range(KC):
                mm = nc.tensor.matmul(PS[:, k, 0:S2], HALF, YT[:, k], start=True, stop=True)
            mm.then_inc(rs["gn_sum"], 1)
            pe.wait_ge(rs["gn_sq"], 1)
            for k in range(KC):
                mm = nc.tensor.matmul(PS[:, k, 0:S2], HALF, SQ[:, k], start=True, stop=True)
            mm.then_inc(rs["gn_var"], 1)

        def act_rwkv_out(act):
            act.wait_ge(rs["gn_centred"], 1)
            act_chain(nc.scalar.activation(SQ[:, :, :], YT[:, :, :], ACT.Square))
            act.sem_inc(rs["gn_sq"], 1)
            act.wait_ge(rs["gn_mean"], 1)
            act_chain(nc.scalar.activation(SQ[:, :, :], SQ[:, :, :], ACT.Ln))
            act_chain(nc.scalar.activation(SQ[:, :, :], SQ[:, :, :], ACT.Exp, scale=-0.5))
            act.sem_inc(rs["gn_root"], 1)

        def dve_rwkv_out(dve):
            dve.wait_ge(rs["gn_sum"], 1)
            for k in range(KC):
                dve_chain(nc.vector.scalar_tensor_tensor(out=YT[:, k], in0=PS[:, k, 0:S2], scalar=-1.0 / 64, in1=YT[:, k],
                                                         op0=ALU.mult, op1=ALU.add))
            dve.sem_inc(rs["gn_centred"], 1)
            dve.wait_ge(rs["gn_var"], 1)
            dve_chain(nc.vector.tensor_scalar(SQ[:, :, :], PS[:, :, 0:S2], 1.0 / 64, GN_EPS, ALU.mult, ALU.add))
            dve.sem_inc(rs["gn_mean"], 1)
            dve.wait_ge(rs["gn_root"], 1)
            dve_chain(nc.vector.tensor_tensor(YT[:, :, :], YT[:, :, :], SQ[:, :, :], ALU.mult))
            for k in range(KC):
                dve_chain(nc.vector.scalar_tensor_tensor(out=YT[:, k], in0=YT[:, k], scalar=vec("ln_w", k, 1), in1=BONUS[:, k],
                                                         op0=ALU.mult, op1=ALU.add))
                dve_chain(nc.vector.scalar_tensor_tensor(out=YT[:, k], in0=YT[:, k], scalar=vec("ln_bb", k, 1), in1=G_[:, k],
                                                         op0=ALU.add, op1=ALU.mult))
                dve.sem_inc(rs["out_ready"], 1)
        loaded, stored = sem("parameters_loaded"), sem("output_stored")
        final_ready = sem("final_ready")
        with nc.Block() as block:

            @block.sync
            def _(sp):
                sp.dma_start(X[:, :, :], x_in).then_inc(loaded, 16)
                sp.dma_start(V[:, :], vec_in[:, 0:VEC_W]).then_inc(loaded, 16)
                sp.dma_start(C[:, :], const_in).then_inc(loaded, 16)
                sp.dma_start(AR[:, FIRST_AT:FIRST_AT + FIRST_W], first_in).then_inc(loaded, 16)
                sp.dma_start(POS, pos_in).then_inc(loaded, 16)

                def load_block(n, slot):
                    sp.dma_start(W[:, slot], weights_in[n]).then_inc(landed[slot], 16)

                def stream(first, last):
                    n = first
                    while n < last and (n < RING or n % RING):
                        if n >= RING:
                            sp.wait_ge(weights_low, 2 * (n - RING + 1))
                        load_block(n, n % RING)
                        n += 1
                    rounds = (last - n) // RING
                    if rounds:
                        with sp.Fori(0, rounds) as g:
                            for u in range(RING):
                                sp.wait_ge(weights_low, g * (2 * RING) + 2 * (n + u - RING + 1))
                                load_block(g * RING + n + u, u)
                        n += rounds * RING
                    while n < last:
                        sp.wait_ge(weights_low, 2 * (n - RING + 1))
                        load_block(n, n % RING)
                        n += 1

                mix0 = BLOCKS["mix_out", 0][0] + SPLIT
                stream(0, mix0)
                sp_hybrid_rows(sp)
                mix1 = BLOCKS["mix_in", 1][0] + SPLIT
                stream(mix0, mix1)
                sp.wait_ge(stage_end, 4 * STAGES_BEFORE_RWKV)
                sp.dma_start(LI, vec_in[:, VEC_W:VEC_W + KC * 288].rearrange("p (k c) -> p k c", k=KC)).then_inc(rs["lora_loaded"], 16)
                sp.dma_start(LO, vec_in[:, VEC_W + KC * 288:].rearrange("p (k c) -> p k c", k=4)).then_inc(rs["lora_loaded"], 16)
                stream(mix1, N_BLOCKS)
                sp.wait_ge(final_ready, 1)
                sp.dma_start(out, H[:, :, META:S2]).then_inc(stored, 16)
                sp.wait_ge(stored, 16)

            @block.tensor
            def _(pe):
                pe.wait_ge(loaded, 80)
                end_stage(pe, "pe")
                for l in range(DEPTH):
                    pe_norm(pe, l, S1)
                    pe_project(pe, ("w_in", l), ("w_in", l), H1_H, H1_L, S1)
                    end_stage(pe, "pe")
                    pe_shape(pe, l)
                    end_stage(pe, "pe")
                    pe_attention(pe, attn["A", l], PT[:, AQ:AQ + 4], PT[:, AK:AK + 4], AVN)
                    end_stage(pe, "pe")
                    pe_attention(pe, attn["C", l], PT[:, CQ:CQ + 4], PT[:, CK:CK + 4], CVN)
                    end_stage(pe, "pe")
                    pe_diff_norm(pe, l)
                    pe_sgu(pe, l)
                    end_stage(pe, "pe")
                    pe_merge(pe, l)
                    pe_project(pe, ("w_out", l), ("w_out", l), H1_H, H1_L, S1)
                    end_stage(pe, "pe")
                pe_norm(pe, 2, S1)
                end_stage(pe, "pe")
                norm = 3
                for l in range(DEPTH):
                    for f in range(2):
                        pe_norm(pe, norm, S2)
                        norm += 1
                        pe_ffn(pe, 2 * l + f, l, f)
                        end_stage(pe, "pe")
                        if f:
                            continue
                        pe_norm(pe, norm, S2)
                        norm += 1
                        if l == 0:
                            pe.wait_ge(normed_ready, KC * norm)
                            pe_project(pe, ("mix_in", 0), ("hybrid", 0), MIX_H, MIX_L, S2)
                            pe_hybrid_in(pe)
                            end_stage(pe, "pe")
                            pe_fox_values(pe)
                            end_stage(pe, "pe")
                            pe_delta_prep(pe)
                            end_stage(pe, "pe")
                            pe_attention(pe, FOX, HP[:, FQ:FQ + 4], HP[:, FK:FK + 4], FVN, gates=(FA, FB))
                            end_stage(pe, "pe")
                            pe_delta_grams(pe)
                            end_stage(pe, "pe")
                            pe_inverse(pe, 0, GI)
                            end_stage(pe, "pe")
                            pe_delta_scan(pe)
                            end_stage(pe, "pe")
                            pe_delta_out(pe)
                            end_stage(pe, "pe")
                            pe_project(pe, ("mix_out", 0), ("hybrid", 1), MIX_H, MIX_L, S2)
                            end_stage(pe, "pe")
                        else:
                            end_stage(pe, "pe")
                            pe_lora(pe)
                            end_stage(pe, "pe")
                            for q in range(3):
                                pe_project(pe, ("mix_in", 1), ("r", q), *RV[q], S2, part=(8 * q, 8))
                            end_stage(pe, "pe")
                            pe_decays(pe)
                            end_stage(pe, "pe")
                            for c in range(NT2):
                                pe_rwkv_grams(pe, c)
                                end_stage(pe, "pe")
                                pe_inverse(pe, 1 + c, RI)
                                end_stage(pe, "pe")
                                pe_rwkv_scan(pe, c)
                                end_stage(pe, "pe")
                            pe_rwkv_out(pe)
                            pe_project(pe, ("mix_out", 1), ("r", 3), RO_H, RO_L, S2)
                            end_stage(pe, "pe")
                pe_norm(pe, norm, S2)

            @block.scalar
            def _(act):
                nonlocal act_chain
                act_chain = Chain(act, "act_chain")
                act.wait_ge(loaded, 80)
                act_setup(act)
                for n in range(SPLIT):
                    act_split(act, n)
                act.sem_inc(gates_taken, 2)
                end_stage(act, "act")
                for l in range(DEPTH):
                    act_norm(act, l, XA, S1)
                    act_parts(act, ("w_in", l), H[:, :, 0:S1], H1_H, normed_ready, KC * l)
                    take_outputs(act, act_split, ("w_in", l), (0,), act_take(PT, S1))
                    end_stage(act, "act")
                    act_shape(act, l)
                    end_stage(act, "act")
                    act_attention(act, attn["A", l])
                    end_stage(act, "act")
                    act_attention(act, attn["C", l])
                    end_stage(act, "act")
                    act_diff_norm(act, l)
                    act_sgu(act, l)
                    act_branch_parts(act, l)
                    end_stage(act, "act")
                    act_merge(act, l)
                    take_outputs(act, act_split, ("w_out", l), (), None)
                    end_stage(act, "act")
                act_norm(act, 2, XA, S1)
                end_stage(act, "act")
                norm = 3
                for l in range(DEPTH):
                    for f in range(2):
                        act_norm(act, norm, X[:, :, :], S2)
                        act_parts(act, ("ffn", 2 * l + f), H, H2_H, normed_ready, KC * norm)
                        norm += 1
                        act_ffn(act, 2 * l + f, l, f)
                        end_stage(act, "act")
                        if f:
                            continue
                        act_norm(act, norm, X[:, :, :], S2)
                        norm += 1
                        if l == 0:
                            act_parts(act, ("hybrid", 0), H, MIX_H, normed_ready, KC * (norm - 1))
                            take_outputs(act, act_split, ("mix_in", 0), (0,), act_take(HP, S2))
                            end_stage(act, "act")
                            act_hybrid_rows(act)
                            end_stage(act, "act")
                            act_delta_prep(act)
                            end_stage(act, "act")
                            act_attention(act, FOX)
                            end_stage(act, "act")
                            act_delta_grams(act)
                            end_stage(act, "act")
                            act_inverse(act, 0, GI)
                            end_stage(act, "act")
                            act_delta_scan(act)
                            end_stage(act, "act")
                            act_delta_out(act)
                            act_parts(act, ("hybrid", 1), Y8, MIX_H, hs["outputs"], 0)
                            end_stage(act, "act")
                            take_outputs(act, act_split, ("mix_out", 0), (), None)
                            end_stage(act, "act")
                        else:
                            end_stage(act, "act")
                            act_lora(act)
                            end_stage(act, "act")
                            act_variants(act)
                            take_outputs(act, act_split, ("mix_in", 1), (0,), act_take(RKV, S2))
                            end_stage(act, "act")
                            act_decays(act)
                            end_stage(act, "act")
                            for c in range(NT2):
                                act_rwkv_grams(act, c)
                                end_stage(act, "act")
                                act_inverse(act, 1 + c, RI)
                                end_stage(act, "act")
                                act_rwkv_scan(act, c)
                                end_stage(act, "act")
                            act_rwkv_out(act)
                            act_parts(act, ("r", 3), YT, RO_H, rs["out_ready"], 0)
                            take_outputs(act, act_split, ("mix_out", 1), (), None)
                            end_stage(act, "act")
                act_norm(act, norm, X[:, :, :], S2)

            @block.vector
            def _(dve):
                nonlocal dve_chain
                dve_chain = Chain(dve, "dve_chain")
                dve.wait_ge(loaded, 80)
                dve_setup(dve)
                for n in range(SPLIT):
                    dve_split(dve, n)
                dve.sem_inc(taken[0], 2)
                dve.sem_inc(taken[1], 2)
                dve.sem_inc(ups_taken, 2)
                end_stage(dve, "dve")
                for l in range(DEPTH):
                    dve_norm(dve, l, XA, S1, vec("norm_g", KC * l, KC), H)
                    dve_parts(dve, ("w_in", l), H[:, :, 0:S1], H1_H, H1_L)
                    take_outputs(dve, dve_split, ("w_in", l), (1,), dve_take(PT, S1))
                    end_stage(dve, "dve")
                    dve_shape(dve, l)
                    end_stage(dve, "dve")
                    dve_attention(dve, attn["A", l], mask_a, YS[:, 0:4], NEG_LAM[:, l:l + 1])
                    end_stage(dve, "dve")
                    dve_attention(dve, attn["C", l], mask_c, YS[:, 8:12])
                    end_stage(dve, "dve")
                    dve_diff_norm(dve, l)
                    dve_sgu(dve, l)
                    dve_branch_parts(dve, l)
                    end_stage(dve, "dve")
                    dve_merge(dve, l)
                    take_outputs(dve, dve_split, ("w_out", l), (0, 1), dve_add(XA, S1))
                    end_stage(dve, "dve")
                dve_norm(dve, 2, XA, S1, vec("final_g"), XA)
                end_stage(dve, "dve")
                norm = 3
                for l in range(DEPTH):
                    for f in range(2):
                        dve_norm(dve, norm, X, S2, vec("ffn_g", KC * (2 * l + f), KC), H)
                        dve_parts(dve, ("ffn", 2 * l + f), H, H2_H, H2_L)
                        norm += 1
                        dve_ffn(dve, 2 * l + f, l, f)
                        end_stage(dve, "dve")
                        if f:
                            continue
                        dve_norm(dve, norm, X, S2, vec("mix_g", KC * l, KC), H)
                        norm += 1
                        if l == 0:
                            dve_parts(dve, ("hybrid", 0), H, MIX_H, MIX_L)
                            take_outputs(dve, dve_split, ("mix_in", 0), (1,), dve_take(HP, S2))
                            end_stage(dve, "dve")
                            dve_hybrid_rows(dve)
                            end_stage(dve, "dve")
                            dve_delta_prep(dve)
                            end_stage(dve, "dve")
                            dve_attention(dve, FOX, const("mask_f").rearrange("p (a b) -> p a b", a=NT2), Y8[:, 0:4])
                            end_stage(dve, "dve")
                            dve_delta_grams(dve)
                            end_stage(dve, "dve")
                            dve_inverse(dve, 0, GI)
                            end_stage(dve, "dve")
                            dve_delta_scan(dve)
                            end_stage(dve, "dve")
                            dve_delta_out(dve)
                            dve_parts(dve, ("hybrid", 1), Y8, MIX_H, MIX_L)
                            end_stage(dve, "dve")
                            take_outputs(dve, dve_split, ("mix_out", 0), (0, 1), dve_add(X, S2))
                            end_stage(dve, "dve")
                        else:
                            end_stage(dve, "dve")
                            dve_lora(dve)
                            end_stage(dve, "dve")
                            dve_variants(dve)
                            take_outputs(dve, dve_split, ("mix_in", 1), (1,), dve_take(RKV, S2))
                            end_stage(dve, "dve")
                            dve_decays(dve)
                            end_stage(dve, "dve")
                            for c in range(NT2):
                                dve_rwkv_grams(dve, c)
                                end_stage(dve, "dve")
                                dve_inverse(dve, 1 + c, RI)
                                end_stage(dve, "dve")
                                dve_rwkv_scan(dve, c)
                                end_stage(dve, "dve")
                            dve_rwkv_out(dve)
                            dve_parts(dve, ("r", 3), YT, RO_H, RO_L)
                            take_outputs(dve, dve_split, ("mix_out", 1), (0, 1), dve_add(X, S2))
                            end_stage(dve, "dve")
                dve_norm(dve, norm, X, S2, vec("final2_g"), H)
                dve.sem_inc(final_ready, 1)

            @block.gpsimd
            def _(pool):
                end_stage(pool, "pool")
                for l in range(DEPTH):
                    end_stage(pool, "pool")
                    pool_shape(pool, l)
                    for _ in range(5):
                        end_stage(pool, "pool")
                end_stage(pool, "pool")
                for l in range(DEPTH):
                    for f in range(2):
                        end_stage(pool, "pool")
                        if f:
                            continue
                        if l == 0:
                            end_stage(pool, "pool")
                            pool_hybrid_rows(pool)
                            for _ in range(4):
                                end_stage(pool, "pool")
                            pool_inverse(pool, 0, GI)
                            for _ in range(4):
                                end_stage(pool, "pool")
                        else:
                            for _ in range(4):
                                end_stage(pool, "pool")
                            for c in range(NT2):
                                end_stage(pool, "pool")
                                pool_inverse(pool, 1 + c, RI)
                                end_stage(pool, "pool")
                                end_stage(pool, "pool")
                            end_stage(pool, "pool")


def kernel(**inputs):
    import concourse.bacc as bacc
    from concourse.bass_utils import run_bass_kernel_spmd

    i = {k: np.asarray(v) for k, v in inputs.items()}
    constants, first = host_constants()
    vectors, lora = host_vectors(i, first)
    x = np.concatenate([i["meta_2"], i["x"][0]], 0)
    arrays = {
        "x_in": np.ascontiguousarray(x.reshape(S2, KC, P).transpose(2, 1, 0)),
        "pos_in": np.ascontiguousarray(np.broadcast_to(i["positions"].reshape(1, S1), (P, S1))),
        "const_in": constants,
        "first_in": first,
        "vec_in": np.concatenate([vectors, lora], 1),
        "weights_in": host_weights(i),
    }
    nc = bacc.Bacc("TRN2", target_bir_lowering=False, num_devices=1,
                   dynamic_dma_scratch_size=256)
    args = {n: nc.dram_tensor(n, a.shape, mybir.dt.from_np(a.dtype), kind="ExternalInput").ap() for n, a in arrays.items()}
    out = nc.dram_tensor("out", (P, KC, S1), F32, kind="ExternalOutput").ap()
    build(nc, out=out, **args)
    result = run_bass_kernel_spmd(nc, [arrays], core_ids=[0]).results[0]["out"]
    return np.ascontiguousarray(result.transpose(2, 1, 0).reshape(1, S1, D))
```

```python
import math
from contextlib import ExitStack

import numpy as np
import concourse.bass as bass
from concourse import mybir

F32 = mybir.dt.float32
F32R = mybir.dt.float32r
I32 = mybir.dt.int32
ALU = mybir.AluOpType
ACT = mybir.ActivationFunctionType
AXX = mybir.AxisListType.X

P = 128
D = 1024
KC = D // P
DEPTH = 2
S1 = 256
META = 16
S2 = S1 + META
T1 = 128
T2 = 68
TC = 64
WIDTHS = [min(TC, S2 - t) for t in range(0, S2, TC)]
NT1, NT2 = S1 // T1, S2 // T2
RING = 4
ARENA = 36700
FIRST_AT = 31744
SPLIT = 2
LEVELS = [2, 4, 8, 16, 32]
EPS = 1e-6
NEG = -1e30

AQ, AK, AV, AZ, BU, BV, BZ, CQ, CK, CV, CZ, GL = 0, 4, 8, 12, 16, 20, 24, 28, 32, 36, 40, 44
IN_CH = 68
A_HEADS, C_HEADS, F_HEADS, G_HEADS, R_HEADS = 4, 8, 8, 4, 16
FF_CH = 22
FQ, FK, FV, GQ, GK, GV, GZ = 0, 4, 8, 12, 16, 20, 24
HYB_CH = 28

BLOCKS = {}
_n = 0
for _l in range(DEPTH):
    for _name, _count in (("w_in", IN_CH), ("w_branch", 12), ("w_out", KC)):
        BLOCKS[_name, _l] = (_n, _count)
        _n += _count
for _l in range(DEPTH):
    for _name, _count in (("ffn_in0", 2 * FF_CH), ("ffn_out0", FF_CH), ("mix_in", HYB_CH if _l == 0 else 24),
                          ("mix_out", KC), ("ffn_in1", 2 * FF_CH), ("ffn_out1", FF_CH)):
        BLOCKS[_name, _l] = (_n, _count)
        _n += _count
N_BLOCKS = _n


def _columns(table):
    at, out = 0, {}
    for name, width in table:
        out[name] = (at, width)
        at += width
    return out, at


CONST, CONST_W = _columns([
    ("ident", P), ("ones", P), ("half_ones", P), ("inv_freq", 1),
    ("mask_f", NT2 * S2),
    ("tri_pair", P), ("tri", 3 * TC), ("pairs", P), ("partners", len(LEVELS) * P), ("restart", S2), ("neg_tri", TC), ("row_one", S2), ("gate_sign", 1),
])
FIRST, FIRST_W = _columns([
    ("rope", P), ("causal_w", P), ("mask_a", 2 * S1), ("mask_c", 2 * S1), ("count_c", 2 * S1),
    ("lam", DEPTH * 4 * 64), ("sgu_w", DEPTH * 4 * P), ("sgu_b", DEPTH * 4 * P),
])
VEC, VEC_W = _columns([
    ("norm_g", DEPTH * KC), ("final_g", KC), ("subln_g", DEPTH), ("ln_g", DEPTH * 4), ("ln_b", DEPTH * 4),
    ("ffn_g", DEPTH * 2 * KC), ("mix_g", DEPTH * KC), ("final2_g", KC), ("hyb_small", KC * T2),
    ("conv", 12 * 4), ("o_gain", 1), ("mu", 6 * KC), ("w0", KC), ("a0", KC),
    ("k_k", KC), ("k_a", KC), ("r_k", KC), ("ln_w", KC), ("ln_bb", KC),
    ("gate_b", 3),
])


def host_constants():
    c, first = np.zeros((P, CONST_W), np.float32), np.zeros((P, FIRST_W), np.float32)

    def put(name, value):
        table, into = (CONST, c) if name in CONST else (FIRST, first)
        at, width = table[name]
        into[:value.shape[0], at:at + width] = value.reshape(value.shape[0], width)

    p = np.arange(P)
    put("ident", np.eye(P, dtype=np.float32))
    put("ones", np.ones((P, P), np.float32))
    put("half_ones", (p[:, None] // 64 == p[None] // 64).astype(np.float32))
    half, rot = 8, 16
    perm = np.zeros((P, P), np.float32)
    for base in (0, 64):
        for i in range(half):
            perm[base + half + i, base + i] = -1.0
            perm[base + i, base + half + i] = 1.0
    put("rope", perm)
    put("causal_w", (p[:, None] <= p[None]).astype(np.float32))
    inv = np.power(np.float32(500000.0), -np.arange(half, dtype=np.float32) * np.float32(2.0) / np.float32(rot))
    f = np.zeros((P, 1), np.float32)
    for base in (0, 64):
        f[base:base + half, 0] = inv
        f[base + half:base + rot, 0] = inv
    put("inv_freq", f)
    q = np.arange(2)[None, :, None] * T1 + p[:, None, None]
    rel = q - np.arange(S1)[None, None, :]
    put("mask_a", np.where(rel >= 0, 0.0, NEG).astype(np.float32))
    count = ((rel >= 0) & (rel <= 128)).astype(np.float32) + ((rel >= 0) & (rel % 4 == 0)) + ((rel >= 0) & (rel % 16 == 0))
    put("mask_c", np.where(count > 0, 0.0, NEG).astype(np.float32))
    put("count_c", count.astype(np.float32))
    t = np.arange(T2)
    q = np.arange(NT2)[None, :, None] * T2 + t[:, None, None]
    put("mask_f", np.where(q >= np.arange(S2)[None, None, :], 0.0, NEG).astype(np.float32))
    r, col = p[:, None] % TC, np.arange(TC)[None]
    strict, incl, same = r < col, r <= col, p[:, None] // TC == p[None] // TC
    put("tri", np.stack([incl, strict, incl], 1).astype(np.float32))
    put("tri_pair", (np.tile(strict, (1, 2)) & same).astype(np.float32))
    put("neg_tri", np.where(incl, 0.0, NEG).astype(np.float32))
    put("pairs", (np.tile(strict & (r // 2 == col // 2), (1, 2)) & same).astype(np.float32))
    partners = [(p[:, None] // (2 * b) == p[None] // (2 * b)) & (p[:, None] // b != p[None] // b) & (p[:, None] > p[None])
                for b in LEVELS]
    put("partners", np.concatenate(partners, 1).astype(np.float32))
    put("restart", np.tile((np.arange(S2) % TC != 0).astype(np.float32), (P, 1)))
    put("row_one", np.ones((P, S2), np.float32))
    put("gate_sign", np.where(p < 32, -1.0, 1.0).astype(np.float32)[:, None])
    return c, first


def host_vectors(i, first):
    v = np.zeros((P, VEC_W), np.float32)

    def put(name, value):
        table, into = (VEC, v) if name in VEC else (FIRST, first)
        at, width = table[name]
        into[:value.shape[0], at:at + width] = value.reshape(value.shape[0], width)

    def cols(a):
        a = np.asarray(a)
        return np.ascontiguousarray(a.reshape(-1, P).T)

    def every(a):
        return np.broadcast_to(np.asarray(a).reshape(1, -1), (P, np.asarray(a).size))

    put("norm_g", cols(i["norm_g"]))
    put("final_g", cols(i["final_g"]))
    put("subln_g", cols(i["subln_g"]))
    put("ln_g", cols(i["sgu_ln_g"]))
    put("ln_b", cols(i["sgu_ln_b"]))
    put("lam", every(np.stack([i[n] for n in ("lam_q1", "lam_k1", "lam_q2", "lam_k2")], 1)))
    put("sgu_w", np.ascontiguousarray(np.asarray(i["sgu_w"]).transpose(3, 0, 1, 2)).reshape(P, -1))
    put("sgu_b", every(i["sgu_b"]))
    put("ffn_g", cols(i["ffn_norm_2"]))
    put("mix_g", cols(i["mix_norm_2"]))
    put("final2_g", cols(i["final_norm_2"]))
    w = np.asarray(i["hyb_w_in_2"])[0]
    small = np.zeros((D, T2), np.float32)
    small[:, 0:8], small[:, 32:36], small[:, 64:68] = w[:, 1536:1544], w[:, 3080:3084], w[:, 3084:3088]
    put("hyb_small", small.reshape(KC, P, T2).transpose(1, 0, 2).reshape(P, -1))
    put("conv", np.asarray(i["hyb_conv_2"])[0].reshape(4, 12, P).transpose(2, 1, 0).reshape(P, -1))
    put("o_gain", cols(i["hyb_o_gain_2"]))
    put("mu", cols(i["rwkv_mu_2"][0]))
    for name, key in (("w0", "rwkv_w0_2"), ("a0", "rwkv_a0_2"), ("k_k", "rwkv_k_k_2"), ("k_a", "rwkv_k_a_2"),
                      ("r_k", "rwkv_r_k_2"), ("ln_w", "rwkv_ln_w_2"), ("ln_bb", "rwkv_ln_b_2")):
        put(name, cols(i[key]))
    b = np.zeros((P, 3), np.float32)
    b[0:8, 0] = np.asarray(i["hyb_fox_bf_2"])[0]
    b[32:36, 0] = np.asarray(i["hyb_dt_bias_2"])[0]
    b[32:36, 1] = np.asarray(i["hyb_a_log_2"])[0]
    put("gate_b", b)
    lora = np.concatenate([i[n][0] for n in ("rwkv_w1_2", "rwkv_a1_2", "rwkv_g1_2")], 1)
    lora = lora.reshape(KC, P, 288).transpose(1, 0, 2).reshape(P, -1)
    inner = np.zeros((P, 4, D), np.float32)
    inner[0:64, 0], inner[0:64, 1] = i["rwkv_w2_2"][0], i["rwkv_a2_2"][0]
    inner[:, 2], inner[0:32, 3] = i["rwkv_g2_2"][0][:P], i["rwkv_g2_2"][0][P:]
    return v, np.concatenate([lora, inner.reshape(P, -1)], 1)


def host_weights(i):
    w = np.empty((N_BLOCKS, P, D), np.float32)

    def by_output(a):
        a = np.asarray(a)
        m = a.shape[1] // P
        return a.reshape(KC, P, m, P).transpose(2, 1, 0, 3).reshape(m, P, D)

    def put(key, value):
        at, count = BLOCKS[key]
        w[at:at + count] = value

    for l in range(DEPTH):
        put(("w_in", l), by_output(i["w_in"][l]))
        wb = np.asarray(i["w_branch"][l])
        wb = wb.reshape(3, 4, P, 4, 2, P).transpose(3, 0, 2, 4, 1, 5).reshape(12, P, D)
        put(("w_branch", l), wb)
        put(("w_out", l), by_output(i["w_out"][l]))
        for f in range(2):
            a = by_output(i["ffn_w_in_2"][l, f]).reshape(2, FF_CH, P, D).transpose(1, 0, 2, 3)
            put((f"ffn_in{f}", l), a.reshape(2 * FF_CH, P, D))
            put((f"ffn_out{f}", l), np.asarray(i["ffn_w_out_2"][l, f]).reshape(FF_CH, P, D))
    h = np.asarray(i["hyb_w_in_2"])[0]
    h = np.concatenate([h[:, 0:1536], h[:, 1544:3080], h[:, 3088:3600]], 1)
    put(("mix_in", 0), by_output(h))
    put(("mix_out", 0), by_output(i["hyb_w_out_2"][0]))
    put(("mix_in", 1), np.concatenate([by_output(i[n][0]) for n in ("rwkv_w_r_2", "rwkv_w_k_2", "rwkv_w_v_2")]))
    put(("mix_out", 1), by_output(i["rwkv_w_o_2"][0]))
    return w


def build(nc, x_in, pos_in, const_in, first_in, vec_in, weights_in, out):
    ctx = ExitStack()
    with ctx:
        def sb(name, shape, dt=F32):
            return ctx.enter_context(nc.sbuf_tensor(name, shape, dt))

        sems = {}

        def sem(name):
            if name not in sems:
                sems[name] = ctx.enter_context(nc.semaphore(name))
            return sems[name]

        C = sb("consts", [P, CONST_W])
        V = sb("vectors", [P, VEC_W])
        W = sb("weight_ring", [P, RING, D])
        WH, WL = sb("weights_high", [P, SPLIT, D], F32R), sb("weights_low", [P, SPLIT, D], F32R)
        X = sb("residual", [P, KC, S2])
        H = sb("normed", [P, KC, S2])
        SQ = sb("squares", [P, KC, S2])
        RS = sb("rstd", [P, 3, S2])
        SM = sb("small", [P, 64])
        AR_BYTE = nc.sbuf_base
        AR = sb("arena", [P, ARENA])
        PS = ctx.enter_context(nc.psum_tensor("psum", [P, 8, 512], F32))

        def const(name, rows=P):
            at, width = CONST[name]
            return C[0:rows, at:at + width]

        def vec(name, at=0, width=None, rows=P):
            start, w = VEC[name]
            return V[0:rows, start + at:start + at + (w - at if width is None else width)]

        def first(name):
            at, width = FIRST[name]
            return AR[:, FIRST_AT + at:FIRST_AT + at + width]

        def part(name, at, chunks, n):
            return nc.alloc_sbuf_tensor_at(name, [P, chunks, n], F32R, offset=AR_BYTE + 4 * at)

        def parts(name, at, chunks, n):
            return part(f"{name}_high", at, chunks, n), part(f"{name}_low", at + chunks * n, chunks, n)

        def arena(at, *shape):
            n = math.prod(shape)
            v = AR[:, at:at + n]
            if len(shape) == 2:
                return v.rearrange("p (a b) -> p a b", a=shape[0])
            if len(shape) == 3:
                return v.rearrange("p (a b c) -> p a b c", a=shape[0], b=shape[1])
            return v

        STAGES_BEFORE_RWKV = 1 + 6 * DEPTH + 1 + 1 + 9 + 1 + 1 + 1
        IDENT, ONES, HALF = const("ident"), const("ones"), const("half_ones")
        XA = X[:, :, META:S2]

        class Chain:

            def __init__(self, eng, name):
                self.eng, self.sem, self.n = eng, sem(name), 0

            def __call__(self, step):
                self.n += 1
                step.then_inc(self.sem, 1)
                self.eng.wait_ge(self.sem, self.n)

        act_chain = dve_chain = None
        stage_end = sem("stage_end")
        stages = {}

        def end_stage(eng, name):
            stages[name] = stages.get(name, 0) + 1
            eng.drain().then_inc(stage_end, 1)
            eng.wait_ge(stage_end, 4 * stages[name])

        landed = [sem(f"weights_landed{u}") for u in range(RING)]
        weights_high, weights_low = sem("weights_high_ready"), sem("weights_low_ready")
        blocks_done = sem("blocks_done")

        def at_turn(value, g, step):
            return value if g is None else g * step + value

        def act_split(act, n, g=None):
            if n >= N_BLOCKS:
                return
            act.wait_ge(landed[n % RING], at_turn(16 * (n // RING + 1), g, 16))
            if n >= SPLIT:
                act.wait_ge(blocks_done, at_turn(n - SPLIT + 1, g, RING))
            for half in (slice(0, 512), slice(512, 1024)):
                nc.scalar.activation(WH[:, n % SPLIT, half], W[:, n % RING, half], ACT.Copy).then_inc(weights_high, 1)

        def dve_split(dve, n, g=None):
            if n >= N_BLOCKS:
                return
            for j, half in enumerate((slice(0, 512), slice(512, 1024))):
                dve.wait_ge(weights_high, at_turn(2 * n + j + 1, g, 2 * RING))
                nc.vector.tensor_tensor(WL[:, n % SPLIT, half], W[:, n % RING, half],
                                        WH[:, n % SPLIT, half].bitcast(F32), ALU.subtract).then_inc(weights_low, 1)

        def split_ahead(eng, split, first, count):
            if count >= RING:
                with eng.Fori(0, count // RING) as g:
                    for u in range(RING):
                        split(eng, first + u + SPLIT, g)
            for n in range(first + count // RING * RING, first + count):
                split(eng, n + SPLIT)

        def pe_arrived(pe, n, g=None):
            pe.wait_ge(weights_low, at_turn(2 * n + 2, g, 2 * RING))

        def pe_tile(psum, n, t, high, low, start, stop):
            s, cols = n % SPLIT, slice(t * P, (t + 1) * P)
            nc.tensor.matmul(psum, WH[:, s, cols], high, start=start, stop=False)
            nc.tensor.matmul(psum, WH[:, s, cols], low, start=False, stop=False)
            return nc.tensor.matmul(psum, WL[:, s, cols], high, start=False, stop=stop)

        act_high, act_low = sem("activation_high_ready"), sem("activation_low_ready")
        JOBS = {name: j for j, name in enumerate(
            [("w_in", 0), ("w_out", 0), ("w_in", 1), ("w_out", 1), ("ffn", 0), ("hybrid", 0), ("hybrid", 1), ("ffn", 1), ("ffn", 2),
             ("r", 0), ("r", 1), ("r", 2), ("r", 3), ("ffn", 3)])}

        def act_parts(act, job, source, high, ready, base):
            for k in range(KC):
                act.wait_ge(ready, base + k + 1)
                nc.scalar.activation(high[:, k], source[:, k], ACT.Copy).then_inc(act_high, 1)

        def dve_parts(dve, job, source, high, low):
            for k in range(KC):
                dve.wait_ge(act_high, KC * JOBS[job] + k + 1)
                nc.vector.tensor_tensor(low[:, k], source[:, k], high[:, k].bitcast(F32), ALU.subtract).then_inc(act_low, 1)

        taken = [sem("even_outputs_taken"), sem("odd_outputs_taken")]
        OUTS = {}
        total = 0
        for l in range(DEPTH):
            for name in ("w_in", "w_out"):
                OUTS[name, l] = total
                total += BLOCKS[name, l][1]
        for l in range(DEPTH):
            for name in ("mix_in", "mix_out"):
                OUTS[name, l] = total
                total += BLOCKS[name, l][1]
        assert all(v % 4 == 0 for v in OUTS.values())

        def pe_project(pe, key, job, high, low, n, part=(0, None)):
            block, count = BLOCKS[key]
            o = OUTS[key] + part[0]
            block += part[0]
            count = part[1] or count
            pe.wait_ge(act_low, KC * (JOBS[job] + 1))
            with pe.Fori(0, count // 4) as g:
                for u in range(4):
                    pe_arrived(pe, block + u, g)
                    pe.wait_ge(taken[u % 2], g * 2 + (o + u) // 2 + 1)
                    for k in range(KC):
                        mm = pe_tile(PS[:, u, 0:n], block + u, k, high[:, k], low[:, k], k == 0, k == KC - 1)
                    mm.then_inc(blocks_done, 1)
        def take_outputs(eng, split, key, parities, take, part=(0, None)):
            block, count = BLOCKS[key]
            block += part[0]
            count = part[1] or count
            with eng.Fori(0, count // 4) as g:
                for u in range(4):
                    split(eng, block + u + SPLIT, g)
                    if u % 2 in parities:
                        eng.wait_ge(blocks_done, g * 4 + block + u + 1)
                        take(g * 4 + (part[0] + u), u).then_inc(taken[u % 2], 1)

        def act_take(dest, n):
            def take(chunk, bank):
                nc.scalar.wait_ge(blocks_done, 1)
                return nc.scalar.activation(dest[:, chunk, 0:n], PS[:, bank, 0:n], ACT.Copy)
            return take

        def dve_take(dest, n):
            return lambda chunk, bank: nc.vector.tensor_scalar(
                dest[:, chunk, 0:n], PS[:, bank, 0:n], 1.0, None, ALU.mult)

        def dve_add(dest, n):
            return lambda chunk, bank: nc.vector.scalar_tensor_tensor(
                out=dest[:, chunk, 0:n], in0=PS[:, bank, 0:n], scalar=1.0, in1=dest[:, chunk, 0:n],
                op0=ALU.mult, op1=ALU.add)

        squares_ready, ssum_ready = sem("squares_ready"), sem("square_sum_ready")
        mean_ready, rstd_ready, normed_ready = sem("mean_square_ready"), sem("rstd_ready"), sem("normed_ready")

        def act_norm(act, use, x, n):
            nc.scalar.activation(SQ[:, :, 0:n], x, ACT.Square).then_inc(squares_ready, 1)
            act.wait_ge(mean_ready, use + 1)
            act_chain(nc.scalar.activation(RS[:, 1, 0:n], RS[:, 0, 0:n], ACT.Ln))
            nc.scalar.activation(RS[:, 2, 0:n], RS[:, 1, 0:n], ACT.Exp, scale=-0.5).then_inc(rstd_ready, 1)

        def pe_norm(pe, use, n):
            pe.wait_ge(squares_ready, use + 1)
            for k in range(KC):
                mm = nc.tensor.matmul(PS[:, 7, 0:n], ONES, SQ[:, k, 0:n], start=(k == 0), stop=(k == KC - 1))
            mm.then_inc(ssum_ready, 1)

        def dve_norm(dve, use, x, n, gain, dest):
            dve.wait_ge(ssum_ready, use + 1)
            nc.vector.tensor_scalar(RS[:, 0, 0:n], PS[:, 7, 0:n], 1.0 / D, EPS, ALU.mult, ALU.add)\
                .then_inc(mean_ready, 1)
            dve.wait_ge(rstd_ready, use + 1)
            for k in range(KC):
                nc.vector.scalar_tensor_tensor(out=dest[:, k, 0:n], in0=x[:, k], scalar=gain[:, k:k + 1],
                                               in1=RS[:, 2, 0:n], op0=ALU.mult, op1=ALU.mult)\
                    .then_inc(normed_ready, 1)
            dve.wait_ge(normed_ready, KC * (use + 1))

        class Attn:

            def __init__(self, kind, layer):
                self.kind, self.layer = kind, layer
                self.heads, self.maps = {"A": (A_HEADS, 2), "C": (C_HEADS, 1), "F": (F_HEADS, 1)}[kind]
                self.t, self.nt = (T2, NT2) if kind == "F" else (T1, NT1)
                self.n = self.t * self.nt
                self.base = layer * self.heads
                self.e = 128 if kind == "A" else 64
                name = {"A": "diff", "C": "dilated", "F": "fox"}[kind]
                self.s = {k: sem(f"{name}_{k}") for k in (
                    "scores_ready", "scores_taken", "neg_max_ready", "exp_ready", "probs_ready",
                    "turned", "turned_taken", "out_ready", "out_taken")}

            def score(self, h, m, qi):
                b, w = h % 2, self.t * (qi + 1)
                if self.kind == "A":
                    return PS[0:self.t, 2 * b + m, 256 * qi:256 * qi + w]
                if self.kind == "C":
                    return PS[0:self.t, h % 4, 256 * qi:256 * qi + w]
                bank, at = [(0, 0), (0, 68), (0, 204), (1, 0)][qi]
                return PS[0:self.t, 2 * b + bank, at:at + w]

            def rows(self, h, m):
                r = 64 * (m if self.kind == "A" else h % 2)
                return slice(r, r + 64), (h if self.kind == "A" else h // 2)

            def turn_at(self, h, kj):
                if self.kind == "F":
                    bank, at = [(4, 0), (4, 272), (5, 0), (5, 136)][kj]
                else:
                    bank, at = 4 + h % 2, 256 * kj
                return bank, at, self.n - self.t * kj

        def pe_attention(pe, A, q, k, v, gates=None):
            s = A.s

            def scores(h):
                if h >= 2:
                    pe.wait_ge(s["scores_taken"], A.base + h - 1)
                for m in range(A.maps):
                    r, c = A.rows(h, m)
                    for qi in range(A.nt):
                        w = A.t * (qi + 1)
                        mm = nc.tensor.matmul(A.score(h, m, qi), q[r, c, qi * A.t:(qi + 1) * A.t], k[r, c, 0:w],
                                              start=True, stop=gates is None)
                        if gates is not None:
                            g = slice(64 * (h % 2), 64 * (h % 2) + 33)
                            mm = nc.tensor.matmul(A.score(h, m, qi), gates[0][g, h // 2, qi * A.t:(qi + 1) * A.t],
                                                  gates[1][g, h // 2, 0:w], start=False, stop=True)
                mm.then_inc(s["scores_ready"], 1)

            def turn(h):
                pe.wait_ge(s["probs_ready"], A.base + h + 1)
                back = 1 if A.kind == "F" else 2
                if h >= back:
                    pe.wait_ge(s["turned_taken"], A.base + h - back + 1)
                for kj in range(A.nt):
                    bank, at, _ = A.turn_at(h, kj)
                    for qi in range(kj, A.nt):
                        o = at + A.t * (qi - kj)
                        mm = nc.tensor.transpose(PS[0:A.t, bank, o:o + A.t],
                                                 A.probs(h, qi)[:, kj * A.t:(kj + 1) * A.t], IDENT[0:A.t, 0:A.t])
                mm.then_inc(s["turned"], 1)

            def weigh(h):
                pe.wait_ge(s["turned_taken"], A.base + h + 1)
                if h >= 2:
                    pe.wait_ge(s["out_taken"], A.base + h - 1)
                o = 64 * (h % 2) if A.e == 64 else 0
                for kj in range(A.nt):
                    mm = nc.tensor.matmul(PS[o:o + A.e, 6 + h % 2, kj * A.t:A.n],
                                          v[0:A.t, kj, h * A.e:(h + 1) * A.e], A.probs_t(h, kj),
                                          start=(kj == 0), stop=(kj == A.nt - 1))
                mm.then_inc(s["out_ready"], 1)

            scores(0)
            scores(1)
            for h in range(A.heads):
                turn(h)
                if h + 2 < A.heads:
                    scores(h + 2)
                weigh(h)

        def act_attention(act, A):
            s = A.s
            for h in range(A.heads):
                act.wait_ge(s["neg_max_ready"], A.base + h + 1)
                for m in range(A.maps):
                    for qi in range(A.nt):
                        j = m * A.nt + qi
                        step = nc.scalar.activation(
                            A.logits(h, m, qi), A.logits(h, m, qi), ACT.Exp, bias=A.stat(h, 1, j), scale=0.125,
                            **({} if A.kind == "C" else {"accum_out": A.stat(h, 2, j)}))
                step.then_inc(s["exp_ready"], 1)
                if h >= 1:
                    act_turned(act, A, h - 1)
            act_turned(act, A, A.heads - 1)

        def act_turned(act, A, h):
            act.wait_ge(A.s["turned"], A.base + h + 1)
            if h >= 2:
                act.wait_ge(A.s["out_ready"], A.base + h - 1)
            if A.kind == "F":
                act_chain(nc.scalar.activation(A.turned(h)[:, 0:476], PS[0:A.t, 4, 0:476], ACT.Copy))
                step = nc.scalar.activation(A.turned(h)[:, 476:680], PS[0:A.t, 5, 0:204], ACT.Copy)
            else:
                step = nc.scalar.activation(A.turned(h)[:, 0:384], PS[0:A.t, 4 + h % 2, 0:384], ACT.Copy)
            step.then_inc(A.s["turned_taken"], 1)

        def dve_attention(dve, A, mask, dest, neg_lam=None):
            s = A.s

            def masked_max(h):
                dve.wait_ge(s["scores_ready"], A.base + h + 1)
                if h >= 2:
                    dve.wait_ge(s["turned"], A.base + h - 1)
                for m in range(A.maps):
                    for qi in range(A.nt):
                        w = A.t * (qi + 1)
                        dve_chain(nc.vector.tensor_tensor_reduce(
                            A.logits(h, m, qi), A.score(h, m, qi), mask[0:A.t, qi, 0:w], 1.0, -3e38,
                            ALU.add, ALU.max, A.stat(h, 0, m * A.nt + qi)))
                n = A.maps * A.nt
                dve_chain(nc.vector.tensor_scalar(A.stat(h, 1, 0, n), A.stat(h, 0, 0, n), -0.125, None, ALU.mult))
                dve.sem_inc(s["scores_taken"], 1)
                dve.sem_inc(s["neg_max_ready"], 1)

            def normalise(h):
                n = A.maps * A.nt
                dve.wait_ge(s["exp_ready"], A.base + h + 1)
                if A.kind == "C":
                    for qi in range(A.nt):
                        w = A.t * (qi + 1)
                        dve_chain(nc.vector.tensor_tensor_reduce(
                            A.logits(h, 0, qi), A.logits(h, 0, qi), first("count_c").rearrange(
                                "p (a b) -> p a b", a=2)[:, qi, 0:w], 1.0, 0.0, ALU.mult, ALU.add, A.stat(h, 2, qi)))
                dve_chain(nc.vector.reciprocal(A.stat(h, 3, 0, n), A.stat(h, 2, 0, n)))
                if A.kind == "A":
                    dve_chain(nc.vector.tensor_scalar(A.stat(h, 3, 2, 2), A.stat(h, 3, 2, 2), neg_lam, None, ALU.mult))
                    for qi in range(A.nt):
                        dve_chain(nc.vector.tensor_scalar(A.logits(h, 1, qi), A.logits(h, 1, qi),
                                                          A.stat(h, 3, 2 + qi), None, ALU.mult))
                        dve_chain(nc.vector.scalar_tensor_tensor(
                            out=A.logits(h, 0, qi), in0=A.logits(h, 0, qi), scalar=A.stat(h, 3, qi),
                            in1=A.logits(h, 1, qi), op0=ALU.mult, op1=ALU.add))
                else:
                    for qi in range(A.nt):
                        dve_chain(nc.vector.tensor_scalar(A.logits(h, 0, qi), A.logits(h, 0, qi),
                                                          A.stat(h, 3, qi), None, ALU.mult))
                dve.sem_inc(s["probs_ready"], 1)

            def take(h):
                dve.wait_ge(s["out_ready"], A.base + h + 1)
                o = 64 * (h % 2) if A.e == 64 else 0
                c = h if A.e == 128 else h // 2
                nc.vector.tensor_copy(dest[o:o + A.e, c, 0:A.n], PS[o:o + A.e, 6 + h % 2, 0:A.n])\
                    .then_inc(s["out_taken"], 1)

            masked_max(0)
            for h in range(A.heads):
                if h + 1 < A.heads:
                    masked_max(h + 1)
                normalise(h)
                if h >= 1:
                    take(h - 1)
            take(A.heads - 1)

        def place_attention(A, at):
            width = A.maps * A.nt * A.n
            base_t = at + 2 * width
            A.logits = lambda h, m, qi: AR[0:A.t, at + (h % 2) * width + (m * A.nt + qi) * A.n:][:, 0:A.t * (qi + 1)]
            A.probs = lambda h, qi: A.logits(h, 0, qi)
            A.turned = lambda h: AR[0:A.t, base_t + 1024 * (h % 2):base_t + 1024 * (h % 2) + 1024]

            def probs_t(h, kj):
                starts = [0, 272, 476, 612] if A.kind == "F" else [0, 256]
                return A.turned(h)[:, starts[kj]:starts[kj] + A.n - A.t * kj]
            A.probs_t = probs_t
            A.stat = lambda h, row, j, n=1: SM[0:A.t, 32 * (h % 2) + 8 * row + j:32 * (h % 2) + 8 * row + j + n]
            return A
        PT = arena(0, IN_CH, S1)
        AVN, CVN, BVN = (arena(17408 + 1024 * j, 2, 512) for j in range(3))
        YS = arena(20480, 12, S1)
        SCR = 23552
        NEG_LAM, SUB_G = sb("neg_lam", [P, 8]), sb("subln_gain", [P, 2])
        attn = {}
        for l in range(DEPTH):
            attn["A", l] = place_attention(Attn("A", l), SCR)
            attn["C", l] = place_attention(Attn("C", l), SCR)
        DIFF_OUT, DIFF_RS = arena(SCR, 4, S1), arena(SCR + 1024, 4, S1)
        POS = arena(2048, S1).bitcast(I32)
        COS, SIN = arena(FIRST_AT + FIRST_W, S1), arena(FIRST_AT + FIRST_W + S1, S1)
        YS_H, YS_L = part("branches_high", 17408, 12, S1), part("branches_low", SCR + 1024, 12, S1)
        H1_H, H1_L = parts("first_normed", SCR + 4096, KC, S1)
        H2_H, H2_L = parts("ffn_normed", 0, KC, S2)
        F_H, F_L = parts("ffn_inner", 2 * KC * S2, FF_CH, S2)
        FFN_GATE, FFN_PROD = (arena((2 * KC + 2 * FF_CH + 2 * j) * S2, 2, S2) for j in range(2))
        mask_a = first("mask_a").rearrange("p (a b) -> p a b", a=2)
        mask_c = first("mask_c").rearrange("p (a b) -> p a b", a=2)
        LAM_INIT = [0.8 - 0.6 * math.exp(-0.3 * l) for l in range(DEPTH)]

        inputs_ready = sem("inputs_ready")
        tables = sem("rope_tables")
        gated = sem("nonlinear_ready")
        permuted, rope_sin, rope_cos, roped = (sem(n) for n in ("rope_permuted", "rope_sin_part", "rope_cos_part", "roped"))
        values_turned, values_taken = sem("values_turned"), sem("values_taken")
        sum_ready, row_ready, stat_ready = sem("sum_ready"), sem("row_ready"), sem("stat_ready")
        norm_ready, mixed_ready = sem("norm_ready"), sem("mixed_ready")
        branches_ready, branch_parts = sem("branches_ready"), sem("branch_parts_ready")
        merged_in, merged_part, merged_ready = sem("branch_ready"), sem("branch_gated"), sem("merged_ready")
        gates_taken, ups_taken = sem("gates_taken"), sem("ups_taken")

        def dve_setup(dve):
            ang, turns, ang2 = arena(0, S1), arena(256, S1), arena(512, S1)
            dve_chain(nc.vector.tensor_copy(ang, POS))
            dve_chain(nc.vector.tensor_scalar(ang, ang, const("inv_freq"), None, ALU.mult))
            magic = 12582912.0
            for dest, shift in ((ang2, 0.0), (arena(768, S1), 0.25)):
                dve_chain(nc.vector.tensor_scalar(turns, ang, 1.0 / (2 * math.pi), shift, ALU.mult, ALU.add))
                dve_chain(nc.vector.tensor_scalar(turns, turns, magic, None, ALU.add))
                dve_chain(nc.vector.tensor_scalar(turns, turns, magic, None, ALU.subtract))
                last = ang
                for part in (-6.28125, -0.0019350051879882812, -3.0199159819567e-07):
                    dve_chain(nc.vector.scalar_tensor_tensor(out=dest, in0=turns, scalar=part, in1=last,
                                                             op0=ALU.mult, op1=ALU.add))
                    last = dest
                if shift:
                    dve_chain(nc.vector.tensor_scalar(dest, dest, math.pi / 2, None, ALU.add))
                dve_chain(nc.vector.tensor_scalar(dest, dest, 3.1415925, -3.1415925, ALU.min, ALU.max))
                dve.sem_inc(tables, 1)
            prod = arena(1024, 4, 64)
            lam = first("lam").rearrange("p (l a b) -> p l a b", l=DEPTH, a=4)
            for l in range(DEPTH):
                for j in range(2):
                    dve_chain(nc.vector.tensor_tensor_reduce(prod[:, 2 * l + j], lam[:, l, 2 * j], lam[:, l, 2 * j + 1],
                                                             1.0, 0.0, ALU.mult, ALU.add, SM[:, 2 * l + j:2 * l + j + 1]))
            dve.sem_inc(tables, 1)
            dve.wait_ge(stat_ready, 1)
            for l in range(DEPTH):
                dve_chain(nc.vector.tensor_tensor(NEG_LAM[:, l:l + 1], SM[:, 8 + 2 * l + 1:8 + 2 * l + 2],
                                                  SM[:, 8 + 2 * l:8 + 2 * l + 1], ALU.subtract))
                dve_chain(nc.vector.tensor_scalar(NEG_LAM[:, l:l + 1], NEG_LAM[:, l:l + 1], -LAM_INIT[l], None, ALU.add))
                dve_chain(nc.vector.tensor_scalar(SUB_G[:, l:l + 1], vec("subln_g", l, 1), 1.0 - LAM_INIT[l], None, ALU.mult))

        def act_setup(act):
            act.wait_ge(tables, 1)
            act_chain(nc.scalar.activation(SIN, arena(512, S1), ACT.Sin))
            act.wait_ge(tables, 2)
            act_chain(nc.scalar.activation(COS, arena(768, S1), ACT.Sin))
            act.wait_ge(tables, 3)
            act_chain(nc.scalar.activation(SM[:, 8:12], SM[:, 0:4], ACT.Exp))
            act.sem_inc(stat_ready, 1)

        ROPE_PAIRS = [AQ, AQ + 2, AK, AK + 2, CQ, CQ + 2, CK, CK + 2]

        def act_shape(act, l):
            for at, n, func in ((AZ, 4, ACT.Silu), (BZ, 4, ACT.Silu), (CZ, 4, ACT.Silu),
                                (BU, 8, ACT.Gelu_apprx_tanh), (GL, 24, ACT.Sigmoid)):
                act_chain(nc.scalar.activation(PT[:, at:at + n], PT[:, at:at + n], func))
            for j, (dest, tile) in enumerate(((AVN, 0), (AVN, 1), (CVN, 0), (CVN, 1))):
                act.wait_ge(values_turned, 4 * l + j + 1)
                nc.scalar.activation(dest[:, tile], PS[:, j, 0:512], ACT.Copy).then_inc(values_taken, 1)

        def pe_shape(pe, l):
            for j, at in enumerate(ROPE_PAIRS):
                nc.tensor.matmul(PS[:, j, 0:512], first("rope"), PT[:, at:at + 2], start=True, stop=True)\
                    .then_inc(permuted, 1)
            for j, (at, tile) in enumerate(((AV, 0), (AV, 1), (CV, 0), (CV, 1))):
                pe.wait_ge(rope_sin, 8 * l + j + 1)
                for c in range(4):
                    mm = nc.tensor.transpose(PS[:, j, c * P:(c + 1) * P], PT[:, at + c, tile * T1:(tile + 1) * T1], IDENT)
                mm.then_inc(values_turned, 1)

        def dve_shape(dve, l):
            part = arena(SCR, 8, 512)
            for j in range(8):
                dve.wait_ge(permuted, 8 * l + j + 1)
                nc.vector.tensor_tensor(part[:, j].rearrange("p (a b) -> p a b", a=2),
                                        PS[:, j, 0:512].rearrange("p (a b) -> p a b", a=2),
                                        SIN.unsqueeze(1).broadcast_to([P, 2, S1]), ALU.mult).then_inc(rope_sin, 1)
            for j, at in enumerate(ROPE_PAIRS):
                dve.wait_ge(rope_cos, 8 * l + j + 1)
                dve.wait_ge(rope_sin, 8 * l + j + 1)
                nc.vector.tensor_tensor(PT[:, at:at + 2].rearrange("p a b -> p (a b)"), PT[:, at:at + 2].rearrange("p a b -> p (a b)"),
                                        part[:, j], ALU.add).then_inc(roped, 1)

        def pool_shape(pool, l):
            for j, at in enumerate(ROPE_PAIRS):
                pool.wait_ge(permuted, 8 * l + j + 1)
                nc.gpsimd.tensor_tensor(PT[:, at:at + 2], PT[:, at:at + 2],
                                        COS.unsqueeze(1).broadcast_to([P, 2, S1]), ALU.mult).then_inc(rope_cos, 1)

        def act_diff_norm(act, l):
            act_chain(nc.scalar.activation(DIFF_RS, YS[:, 0:4], ACT.Square))
            act.sem_inc(stat_ready, 1)
            act.wait_ge(row_ready, 3 * l + 1)
            act_chain(nc.scalar.activation(DIFF_RS, DIFF_RS, ACT.Ln))
            act_chain(nc.scalar.activation(DIFF_RS, DIFF_RS, ACT.Exp, scale=-0.5))
            act.sem_inc(stat_ready, 1)

        def pe_diff_norm(pe, l):
            pe.wait_ge(stat_ready, 1 + 4 * l + 1)
            for h in range(4):
                mm = nc.tensor.matmul(PS[:, h // 2, (h % 2) * S1:(h % 2 + 1) * S1], ONES, DIFF_RS[:, h], start=True, stop=True)
            mm.then_inc(sum_ready, 1)

        def dve_diff_norm(dve, l):
            dve.wait_ge(sum_ready, 3 * l + 1)
            dve_chain(nc.vector.tensor_scalar(DIFF_RS.rearrange("p (a b) c -> p a (b c)", a=2), PS[:, 0:2, :],
                                              1.0 / 128, EPS, ALU.mult, ALU.add))
            dve.sem_inc(row_ready, 1)
            dve.wait_ge(stat_ready, 1 + 4 * l + 2)
            y = YS[:, 0:4].rearrange("p a b -> p (a b)")
            dve_chain(nc.vector.scalar_tensor_tensor(out=y, in0=y, scalar=SUB_G[:, l:l + 1],
                                                     in1=DIFF_RS.rearrange("p a b -> p (a b)"), op0=ALU.mult, op1=ALU.mult))
            dve_chain(nc.vector.tensor_tensor(y, y, PT[:, AZ:AZ + 4].rearrange("p a b -> p (a b)"), ALU.mult))
            y = YS[:, 8:12].rearrange("p a b -> p (a b)")
            dve_chain(nc.vector.tensor_tensor(y, y, PT[:, CZ:CZ + 4].rearrange("p a b -> p (a b)"), ALU.mult))

        B_SQ, B_MEAN, B_WC = arena(SCR + 2048, 4, S1), arena(SCR + 3072, 2, S1), arena(SCR + 3584, 4, P)
        B_V = PT[:, BV:BV + 4]

        def pe_sgu(pe, l):
            for k in range(4):
                mm = nc.tensor.matmul(PS[:, 4, 0:S1], ONES, B_V[:, k], start=(k == 0), stop=(k == 3))
            mm.then_inc(sum_ready, 1)
            pe.wait_ge(stat_ready, 1 + 4 * l + 3)
            for k in range(4):
                mm = nc.tensor.matmul(PS[:, 5, 0:S1], ONES, B_SQ[:, k], start=(k == 0), stop=(k == 3))
            mm.then_inc(sum_ready, 1)
            pe.wait_ge(norm_ready, 2 * l + 1)
            for tile in range(2):
                for c in range(4):
                    mm = nc.tensor.transpose(PS[:, 6 + tile, c * P:(c + 1) * P], B_V[:, c, tile * T1:(tile + 1) * T1], IDENT)
                mm.then_inc(mixed_ready, 1)
            pe.wait_ge(norm_ready, 2 * l + 2)
            for tile in range(2):
                pe.wait_ge(merged_in, 2 * l + tile + 1)
                for g in range(4):
                    mm = nc.tensor.matmul(PS[:, 2 + tile, g * P:(g + 1) * P], BVN[:, tile, g * P:(g + 1) * P],
                                          B_WC[:, g], start=True, stop=True)
                mm.then_inc(mixed_ready, 1)

        def act_sgu(act, l):
            act.wait_ge(row_ready, 3 * l + 2)
            act_chain(nc.scalar.activation(B_SQ, B_V, ACT.Square))
            act.sem_inc(stat_ready, 1)
            act.wait_ge(row_ready, 3 * l + 3)
            act_chain(nc.scalar.activation(B_MEAN[:, 1], B_MEAN[:, 1], ACT.Ln))
            act_chain(nc.scalar.activation(B_MEAN[:, 1], B_MEAN[:, 1], ACT.Exp, scale=-0.5))
            act.sem_inc(stat_ready, 1)
            for tile in range(2):
                act.wait_ge(mixed_ready, 4 * l + tile + 1)
                nc.scalar.activation(BVN[:, tile], PS[:, 6 + tile, 0:512], ACT.Copy).then_inc(merged_in, 1)

        def dve_sgu(dve, l):
            dve.wait_ge(sum_ready, 3 * l + 2)
            dve_chain(nc.vector.tensor_scalar(B_MEAN[:, 0], PS[:, 4, 0:S1], 1.0 / 512, None, ALU.mult))
            dve_chain(nc.vector.tensor_tensor(B_V, B_V, B_MEAN[:, 0:1].broadcast_to([P, 4, S1]), ALU.subtract))
            dve.sem_inc(row_ready, 1)
            dve_chain(nc.vector.tensor_tensor(B_WC, first("sgu_w")[:, l * 512:(l + 1) * 512].rearrange("p (a b) -> p a b", a=4),
                                              first("causal_w").unsqueeze(1).broadcast_to([P, 4, P]), ALU.mult))
            dve.wait_ge(sum_ready, 3 * l + 3)
            dve_chain(nc.vector.tensor_scalar(B_MEAN[:, 1], PS[:, 5, 0:S1], 1.0 / 512, EPS, ALU.mult, ALU.add))
            dve.sem_inc(row_ready, 1)
            dve.wait_ge(stat_ready, 1 + 4 * l + 4)
            dve_chain(nc.vector.tensor_tensor(B_V, B_V, B_MEAN[:, 1:2].broadcast_to([P, 4, S1]), ALU.mult))
            for k in range(4):
                dve_chain(nc.vector.tensor_scalar(B_V[:, k], B_V[:, k], vec("ln_g", 4 * l + k, 1), vec("ln_b", 4 * l + k, 1),
                                                  ALU.mult, ALU.add))
            dve.sem_inc(norm_ready, 2)
            bias = first("sgu_b")[:, l * 512:(l + 1) * 512].rearrange("p (a b) -> p a b", a=4)
            y = YS[:, 4:8]
            for tile in range(2):
                dve.wait_ge(mixed_ready, 4 * l + 3 + tile)
                ts = slice(tile * T1, (tile + 1) * T1)
                dve_chain(nc.vector.tensor_tensor(y[:, :, ts], PS[:, 2 + tile, :].rearrange("p (a b) -> p a b", a=4),
                                                  bias, ALU.add))
            y = y.rearrange("p a b -> p (a b)")
            dve_chain(nc.vector.tensor_tensor(y, y, PT[:, BU:BU + 4].rearrange("p a b -> p (a b)"), ALU.mult))
            dve_chain(nc.vector.tensor_tensor(y, y, PT[:, BZ:BZ + 4].rearrange("p a b -> p (a b)"), ALU.mult))

        def pe_merge(pe, l):
            block, _ = BLOCKS["w_branch", l]
            pe.wait_ge(branch_parts, 2 * l + 2)
            for j in range(12):
                pe_arrived(pe, block + j)
                if j >= 4:
                    pe.wait_ge(merged_part, 12 * l + j - 3)
                for c in range(2):
                    for k in range(4):
                        y = 4 * (j % 3) + k
                        mm = pe_tile(PS[:, j % 4, c * S1:(c + 1) * S1], block + j, c * 4 + k, YS_H[:, y], YS_L[:, y],
                                     k == 0, k == 3)
                mm.then_inc(blocks_done, 1)

        def act_branch_parts(act, l):
            act.wait_ge(branches_ready, l + 1)
            nc.scalar.activation(YS_H[:, :, :], YS, ACT.Copy).then_inc(branch_parts, 1)

        def dve_branch_parts(dve, l):
            dve.sem_inc(branches_ready, 1)
            dve.wait_ge(branch_parts, 2 * l + 1)
            nc.vector.tensor_tensor(YS_L[:, :, :], YS, YS_H[:, :, :].bitcast(F32), ALU.subtract).then_inc(branch_parts, 1)

        def act_merge(act, l):
            block, _ = BLOCKS["w_branch", l]
            for j in range(12):
                act_split(act, block + j + SPLIT)
                if j % 3 == 2:
                    act.wait_ge(merged_ready, KC * l + 2 * (j // 3) + 2)
                    for k in (2 * (j // 3), 2 * (j // 3) + 1):
                        nc.scalar.activation(H1_H[:, k], H[:, k, 0:S1], ACT.Copy).then_inc(act_high, 1)

        def dve_merge(dve, l):
            block, _ = BLOCKS["w_branch", l]
            product = arena(SCR, 2, 512)
            for j in range(12):
                dve_split(dve, block + j + SPLIT)
                dve.wait_ge(blocks_done, block + j + 1)
                pair, n = divmod(j, 3)
                gate = PT[:, GL + 8 * n + 2 * pair:GL + 8 * n + 2 * pair + 2]
                dest = H[:, 2 * pair:2 * pair + 2, 0:S1]
                psum = PS[:, j % 4, :].rearrange("p (a b) -> p a b", a=2)
                to = dest if n == 0 else product[:, n - 1].rearrange("p (a b) -> p a b", a=2)
                nc.vector.tensor_tensor(to, psum, gate, ALU.mult).then_inc(merged_part, 1)
                dve.wait_ge(merged_part, 12 * l + j + 1)
                if n:
                    dve_chain(nc.vector.tensor_tensor(dest, dest, to, ALU.add))
                if n == 2:
                    dve.sem_inc(merged_ready, 2)
            dve_parts(dve, ("w_out", l), H[:, :, 0:S1], H1_H, H1_L)

        inner_high, inner_low = sem("inner_high_ready"), sem("inner_low_ready")

        def pe_ffn(pe, use, l, f):
            block, _ = BLOCKS[f"ffn_in{f}", l]
            pe.wait_ge(act_low, KC * (JOBS["ffn", use] + 1))
            with pe.Fori(0, FF_CH // 2) as g:
                for u in range(4):
                    pe_arrived(pe, block + u, g)
                    pe.wait_ge(ups_taken if u % 2 else gates_taken, g * 2 + FF_CH * use + u // 2 + 1)
                    for k in range(KC):
                        mm = pe_tile(PS[:, u, 0:S2], block + u, k, H2_H[:, k], H2_L[:, k], k == 0, k == KC - 1)
                    mm.then_inc(blocks_done, 1)
            pe.wait_ge(inner_low, FF_CH * (use + 1))
            block, _ = BLOCKS[f"ffn_out{f}", l]

            def rows(n, k, g=None, first=False, last=False):
                pe_arrived(pe, n, g)
                for m in range(KC):
                    mm = pe_tile(PS[:, m, 0:S2], n, m, F_H[:, k], F_L[:, k], first, last)
                mm.then_inc(blocks_done, 1)

            for u in range(4):
                rows(block + u, u, first=(u == 0))
            with pe.Fori(0, 4) as g:
                for u in range(4):
                    rows(block + 4 + u, g * 4 + (4 + u), g)
            for u in range(20, 22):
                rows(block + u, u, last=(u == 21))

        def act_ffn(act, use, l, f):
            block, _ = BLOCKS[f"ffn_in{f}", l]
            with act.Fori(0, FF_CH // 2) as g:
                for u in range(2):
                    act_split(act, block + 2 * u + SPLIT, g)
                    act.wait_ge(ups_taken, g * 2 + FF_CH * use + u + 1)
                    act.wait_ge(blocks_done, g * 4 + block + 2 * u + 1)
                    nc.scalar.activation(FFN_GATE[:, u], PS[:, 2 * u, 0:S2], ACT.Silu).then_inc(gates_taken, 1)
                    act_split(act, block + 2 * u + 1 + SPLIT, g)
                    act.wait_ge(ups_taken, g * 2 + FF_CH * use + u + 3)
                    act.wait_ge(blocks_done, 1)
                    nc.scalar.activation(F_H[:, g * 2 + u], FFN_PROD[:, u], ACT.Copy).then_inc(inner_high, 1)
            split_ahead(act, act_split, *BLOCKS[f"ffn_out{f}", l])

        def dve_ffn(dve, use, l, f):
            block, _ = BLOCKS[f"ffn_in{f}", l]
            with dve.Fori(0, FF_CH // 2) as g:
                for u in range(2):
                    dve_split(dve, block + 2 * u + SPLIT, g)
                    dve.wait_ge(gates_taken, g * 2 + FF_CH * use + u + 3)
                    dve.wait_ge(blocks_done, g * 4 + block + 2 * u + 2)
                    nc.vector.tensor_tensor(FFN_PROD[:, u], FFN_GATE[:, u], PS[:, 2 * u + 1, 0:S2], ALU.mult)\
                        .then_inc(ups_taken, 1)
                    dve_split(dve, block + 2 * u + 1 + SPLIT, g)
                    dve.wait_ge(inner_high, g * 2 + FF_CH * use + u + 1)
                    nc.vector.tensor_tensor(F_L[:, g * 2 + u], FFN_PROD[:, u], F_H[:, g * 2 + u].bitcast(F32), ALU.subtract)\
                        .then_inc(inner_low, 1)
            block, count = BLOCKS[f"ffn_out{f}", l]
            split_ahead(dve, dve_split, block, count)
            dve.wait_ge(blocks_done, block + count)
            for m in range(KC):
                nc.vector.scalar_tensor_tensor(out=X[:, m], in0=PS[:, m, 0:S2], scalar=0.5, in1=X[:, m],
                                               op0=ALU.mult, op1=ALU.add)
        ROUNDS = [len(LEVELS)] + [sum(2 * b <= w for b in LEVELS) for w in WIDTHS]
        FIRST_TURN = [4 * (sum(ROUNDS[:u]) + u) for u in range(len(ROUNDS))]
        FIRST_ROUND = [4 * sum(ROUNDS[:u]) for u in range(len(ROUNDS))]
        inv = {k: sem("inverse_" + k) for k in ("y_ready", "y_taken", "xy_ready", "x_new", "turned", "turned_taken")}

        def span(c):
            return slice(c * TC, c * TC + WIDTHS[c])

        def half(odd):
            return slice(odd * TC, odd * TC + TC)

        def firsts(v, b):
            return v.rearrange("p m (k two b) -> p m k two b", two=2, b=b)[:, :, :, 0]

        def halves(bank, n):
            return PS[:, bank, 0:n * TC].rearrange("p (a b) -> p a b", a=n)

        def wholes(bank, n):
            return PS[:, bank, 0:n * P].rearrange("p (a b) -> p a b", a=n)

        def by_parity(v):
            return v.rearrange("p (q o) t -> p o q t", o=2)

        def pe_inverse(pe, use, B):
            U, X_, XT, Y = B["U"], B["X"], B["XT"], B["Y"]
            turn, first_round = FIRST_TURN[use], FIRST_ROUND[use]
            for g, (m0, n) in enumerate(B["groups"]):
                for j in range(n):
                    mm = nc.tensor.transpose(wholes(4 + g, n)[:, j], XT[:, m0 + j], IDENT)
                mm.then_inc(inv["turned"], 1)
            for i in range(ROUNDS[use] + 1):
                for g, (m0, n) in enumerate(B["groups"]):
                    if i == ROUNDS[use]:
                        break
                    if i == 0:
                        pe.wait_ge(inv["turned_taken"], turn + g + 1)
                    else:
                        pe.wait_ge(inv["x_new"], first_round + 4 * (i - 1) + g + 1)
                    for j in range(n):
                        mm = nc.tensor.matmul(wholes(g, n)[:, j], U[:, m0 + j], X_[:, m0 + j], start=True, stop=True)
                    mm.then_inc(inv["y_ready"], 1)
                for g, (m0, n) in enumerate(B["groups"]):
                    if i == 0:
                        break
                    pe.wait_ge(inv["x_new"], first_round + 4 * (i - 1) + g + 1)
                    pe.wait_ge(inv["turned_taken"], turn + 4 * (i - 1) + g + 1)
                    for j in range(n):
                        mm = nc.tensor.transpose(wholes(4 + g, n)[:, j], X_[:, m0 + j], IDENT)
                    mm.then_inc(inv["turned"], 1)
                for g, (m0, n) in enumerate(B["groups"]):
                    if i == ROUNDS[use]:
                        break
                    pe.wait_ge(inv["y_taken"], first_round + 4 * i + g + 1)
                    pe.wait_ge(inv["turned_taken"], turn + 4 * i + g + 1)
                    for j in range(n):
                        mm = nc.tensor.matmul(wholes(g, n)[:, j], XT[:, m0 + j], Y[:, m0 + j], start=True, stop=True)
                    mm.then_inc(inv["xy_ready"], 1)

        def act_inverse(act, use, B):
            for i in range(ROUNDS[use] + 1):
                for g, (m0, n) in enumerate(B["groups"]):
                    act.wait_ge(inv["turned"], FIRST_TURN[use] + 4 * i + g + 1)
                    nc.scalar.activation((B["XT"] if i else B["X"])[:, m0:m0 + n], wholes(4 + g, n), ACT.Copy)\
                        .then_inc(inv["turned_taken"], 1)

        def dve_inverse(dve, use, B):
            X_, Y = B["X"], B["Y"]
            for i in range(ROUNDS[use]):
                base, b = FIRST_ROUND[use] + 4 * i, LEVELS[i]
                for g, (m0, n) in enumerate(B["groups"]):
                    dve.wait_ge(inv["y_ready"], base + g + 1)
                    mask = const("partners")[:, i * P:(i + 1) * P].unsqueeze(1).broadcast_to([P, n, P])
                    nc.vector.tensor_tensor(Y[:, m0:m0 + n], wholes(g, n), mask, ALU.mult).then_inc(inv["y_taken"], 1)
                for g, (m0, n) in enumerate(B["groups"]):
                    dve.wait_ge(inv["xy_ready"], base + g + 1)
                    if i:
                        dve.wait_ge(inv["x_new"], base - 4 + g + 1)
                    x = firsts(X_[:, m0:m0 + n], b)
                    nc.vector.tensor_tensor(x, x, firsts(wholes(g, n), b), ALU.subtract)\
                        .then_inc(inv["x_new"], 1)

        def dve_first_level(B, n):
            dve_chain(nc.vector.tensor_tensor(B["XT"], B["U"], const("pairs").unsqueeze(1).broadcast_to([P, n, P]), ALU.mult))
            dve_chain(nc.vector.tensor_tensor(B["XT"], IDENT.unsqueeze(1).broadcast_to([P, n, P]), B["XT"], ALU.subtract))

        HP = arena(0, HYB_CH, S2)
        CO = arena(7616, 12, S2)
        FVN = AR[0:T2, 10880:12928].rearrange("p (a b) -> p a b", a=4)
        ROWS = arena(12928, 6, S2)
        FA, FB, GA, GB = (arena(14560 + 1088 * j, 4, S2) for j in range(4))
        BR = arena(18912, 4, S2)
        BETA_B, GC_B, EGC = (arena(20000 + 1088 * j, 4, S2) for j in range(3))
        KBT, KBET, QD, KDT = (arena(23264 + 1088 * j, 4, S2) for j in range(4))
        FOX = place_attention(Attn("F", 0), 27616)
        Y8 = arena(31840, 8, S2)
        GP = 2 * len(WIDTHS)
        GI = {"U": arena(0, GP, P), "X": arena(1280, GP, P), "XT": arena(2560, GP, P), "Y": arena(3840, GP, P),
              "groups": [(0, 3), (3, 3), (6, 2), (8, 2)]}
        ATT, DEC = arena(5120, GP, TC), arena(34016, GP, TC)
        VBN, KBEN, KDN = (arena(at, GP, P) for at in (10880, 14560, 20000))
        WT = arena(34016, 2 * GP, TC)
        UN = arena(35296, 2, P)
        GS = arena(36128, 4, P)
        MIX_H, MIX_L = parts("mixer", 23264, KC, S2)
        DK = 128

        hs = {k: sem("hybrid_" + k) for k in (
            "small_ready", "z_ready", "rows_ready", "one_plus", "log_ready", "sigmoid_ready", "cleared", "values_turned",
            "conv_ready", "bound", "l2_ready", "l2_mean", "l2_root", "spread", "spread_taken", "prep", "grams", "decay",
            "decay_exp", "gram_taken", "turned", "turned_taken", "w_ready", "w_taken", "u_ready", "u_taken", "o_ready",
            "o_taken", "s_ready", "s_taken", "gate", "onorm", "osum", "omean", "oroot", "outputs")}

        def pe_hybrid_in(pe):
            small = vec("hyb_small").rearrange("p (k c) -> p k c", k=KC)
            for k in range(KC):
                mm = nc.tensor.matmul(PS[0:T2, 5, 0:S2], small[:, k], H[:, k], start=(k == 0), stop=(k == KC - 1))
            mm.then_inc(hs["small_ready"], 1)

        def dve_hybrid_rows(dve):
            z, t, sp, c, nc_ = (ROWS[0:36, j] for j in range(5))
            dve.wait_ge(hs["small_ready"], 1)
            dve_chain(nc.vector.tensor_scalar(z, PS[0:36, 5, 0:S2], vec("gate_b", 0, 1, 36), const("gate_sign", 36), ALU.add, ALU.mult))
            dve.sem_inc(hs["z_ready"], 1)
            for j in range(12):
                w = lambda tap: vec("conv", 4 * j + tap, 1)
                dve_chain(nc.vector.tensor_scalar(CO[:, j], HP[:, GQ + j], w(3), None, ALU.mult))
                for back in (1, 2, 3):
                    step = nc.vector.scalar_tensor_tensor(out=CO[:, j, back:], in0=HP[:, GQ + j, 0:S2 - back], scalar=w(3 - back),
                                                          in1=CO[:, j, back:], op0=ALU.mult, op1=ALU.add)
                    dve_chain(step)
            dve.sem_inc(hs["conv_ready"], 1)
            dve.wait_ge(hs["one_plus"], 1)
            dve_chain(nc.vector.tensor_scalar(t, t, 1.0, None, ALU.add))
            dve_chain(nc.vector.tensor_scalar(SM[0:36, 1:2], SM[0:36, 0:1], -1.0, None, ALU.mult))
            dve.sem_inc(hs["z_ready"], 1)
            dve.wait_ge(hs["log_ready"], 1)
            dve_chain(nc.vector.scalar_tensor_tensor(out=sp, in0=z, scalar=0.0, in1=t, op0=ALU.max, op1=ALU.add))
            dve_chain(nc.vector.tensor_scalar(sp, sp, SM[0:36, 1:2], None, ALU.mult))
            dve_chain(nc.vector.tensor_tensor_scan(ROWS[0:8, 3], const("row_one", 8), ROWS[0:8, 2], 0.0, ALU.mult, ALU.add))
            dve_chain(nc.vector.tensor_tensor_scan(ROWS[32:36, 3], C[32:36, CONST["restart"][0]:CONST["restart"][0] + S2],
                                                   ROWS[32:36, 2], 0.0, ALU.mult, ALU.add))
            dve_chain(nc.vector.tensor_scalar(ROWS[0:8, 3], ROWS[0:8, 3], 8.0, None, ALU.mult))
            dve_chain(nc.vector.tensor_scalar(ROWS[0:8, 4], ROWS[0:8, 3], -1.0, None, ALU.mult))
            dve_chain(nc.vector.tensor_scalar(ROWS[32:36, 4], ROWS[32:36, 3], -1.0, None, ALU.mult))
            dve.sem_inc(hs["rows_ready"], 1)

        def act_hybrid_rows(act):
            act.wait_ge(hs["z_ready"], 1)
            act_chain(nc.scalar.activation(ROWS[0:36, 1], ROWS[0:36, 0], ACT.Abs))
            act_chain(nc.scalar.activation(ROWS[0:36, 1], ROWS[0:36, 1], ACT.Exp, scale=-1.0))
            act_chain(nc.scalar.activation(SM[0:36, 0:1], vec("gate_b", 1, 1, 36), ACT.Exp))
            act.sem_inc(hs["one_plus"], 1)
            act.wait_ge(hs["z_ready"], 2)
            act_chain(nc.scalar.activation(ROWS[0:36, 1], ROWS[0:36, 1], ACT.Ln))
            act.sem_inc(hs["log_ready"], 1)
            act_chain(nc.scalar.activation(ROWS[64:68, 0], PS[64:68, 5, 0:S2], ACT.Sigmoid))
            act.sem_inc(hs["sigmoid_ready"], 1)
            for c in range(4):
                act.wait_ge(hs["values_turned"], c + 1)
                act_chain(nc.scalar.activation(FVN[:, c], PS[0:T2, c, 0:512], ACT.Copy))
            act.wait_ge(hs["conv_ready"], 1)
            act_chain(nc.scalar.activation(CO, CO, ACT.Silu))
            act_chain(nc.scalar.activation(HP[:, GZ:GZ + 4], HP[:, GZ:GZ + 4], ACT.Silu))

        def pool_hybrid_rows(pool):
            for j, v in enumerate((FA, FB, GA, GB)):
                nc.gpsimd.memset(v, 0.0).then_inc(hs["cleared"], 1)
            pool.wait_ge(hs["cleared"], 4)
            for j, (v, p) in enumerate(((FA, 32), (FA, 96), (FB, 0), (FB, 64), (GA, 32), (GB, 0))):
                nc.gpsimd.memset(v[p:p + 1], 1.0).then_inc(hs["cleared"], 1)

        def sp_hybrid_rows(sp):
            sp.wait_ge(hs["cleared"], 10)
            sp.wait_ge(hs["rows_ready"], 1)
            sp.wait_ge(hs["sigmoid_ready"], 1)
            for h in range(F_HEADS):
                p = 64 * (h % 2)
                sp.dma_start(FA[p:p + 1, h // 2], ROWS[h:h + 1, 3]).then_inc(hs["bound"], 16)
                sp.dma_start(FB[p + 32:p + 33, h // 2], ROWS[h:h + 1, 4]).then_inc(hs["bound"], 16)
            for h in range(G_HEADS):
                sp.dma_start(GA[0:1, h], ROWS[32 + h:33 + h, 3]).then_inc(hs["bound"], 16)
                sp.dma_start(GB[32:33, h], ROWS[32 + h:33 + h, 4]).then_inc(hs["bound"], 16)
                sp.dma_start(BR[0:1, h], ROWS[64 + h:65 + h, 0]).then_inc(hs["bound"], 16)

        N_ROW_DMAS = 2 * F_HEADS + 3 * G_HEADS

        def pe_fox_values(pe):
            for c in range(4):
                for j in range(4):
                    mm = nc.tensor.transpose(PS[0:T2, c, j * P:(j + 1) * P], HP[:, FV + j, c * T2:(c + 1) * T2], IDENT)
                mm.then_inc(hs["values_turned"], 1)

        def act_delta_prep(act):
            act_chain(nc.scalar.activation(SQ[:, :, :], CO[:, 0:8], ACT.Square))
            act.sem_inc(hs["l2_ready"], 1)
            act.wait_ge(hs["l2_mean"], 1)
            act_chain(nc.scalar.activation(H[:, :, :], H[:, :, :], ACT.Ln))
            act_chain(nc.scalar.activation(H[:, :, :], H[:, :, :], ACT.Exp, scale=-0.5))
            act.sem_inc(hs["l2_root"], 1)
            act.wait_ge(hs["spread"], 8)
            act_chain(nc.scalar.activation(GC_B, PS[:, 0:4, 0:S2], ACT.Copy))
            act_chain(nc.scalar.activation(EGC, PS[:, 0:4, 0:S2], ACT.Exp))
            act_chain(nc.scalar.activation(BETA_B, PS[:, 4:8, 0:S2], ACT.Copy))
            act.sem_inc(hs["spread_taken"], 1)
            act.wait_ge(hs["prep"], 1)
            act_chain(nc.scalar.activation(KDT, KDT, ACT.Exp))
            act.sem_inc(hs["spread_taken"], 1)

        def pe_delta_prep(pe):
            pe.wait_ge(hs["l2_ready"], 1)
            for j in range(8):
                mm = nc.tensor.matmul(PS[:, j, 0:S2], ONES, SQ[:, j], start=True, stop=True)
            mm.then_inc(hs["l2_ready"], 1)
            pe.wait_ge(hs["l2_mean"], 1)
            pe.wait_ge(hs["bound"], 16 * N_ROW_DMAS)
            for j in range(8):
                row = GA[0:1, j] if j < 4 else BR[0:1, j - 4]
                nc.tensor.matmul(PS[:, j, 0:S2], ONES[0:1, :], row, start=True, stop=True).then_inc(hs["spread"], 1)

        def dve_delta_prep(dve):
            dve.wait_ge(hs["l2_ready"], 2)
            dve_chain(nc.vector.tensor_scalar(H[:, :, :], PS[:, :, 0:S2], EPS, None, ALU.add))
            dve.sem_inc(hs["l2_mean"], 1)
            dve.wait_ge(hs["l2_root"], 1)
            q, k, v = CO[:, 0:4], CO[:, 4:8], CO[:, 8:12]
            flat = lambda a: a.rearrange("p a b -> p (a b)")
            dve_chain(nc.vector.scalar_tensor_tensor(out=flat(q), in0=flat(q), scalar=DK ** -0.5, in1=flat(H[:, 0:4]),
                                                     op0=ALU.mult, op1=ALU.mult))
            dve_chain(nc.vector.tensor_tensor(k, k, H[:, 4:8], ALU.mult))
            dve.wait_ge(hs["spread_taken"], 1)
            for c, w in enumerate(WIDTHS):
                t = span(c)
                dve_chain(nc.vector.tensor_tensor(KDT[:, :, t], GC_B[:, :, t.stop - 1:t.stop].broadcast_to([P, 4, w]), GC_B[:, :, t],
                                                  ALU.subtract))
            dve.sem_inc(hs["prep"], 1)
            dve_chain(nc.vector.tensor_tensor(KBT, k, BETA_B, ALU.mult))
            dve_chain(nc.vector.tensor_tensor(KBET, KBT, EGC, ALU.mult))
            dve_chain(nc.vector.tensor_tensor(QD, q, EGC, ALU.mult))
            dve_chain(nc.vector.tensor_tensor(v, v, BETA_B, ALU.mult))
            dve.wait_ge(hs["spread_taken"], 2)
            dve_chain(nc.vector.tensor_tensor(KDT, KDT, k, ALU.mult))

        def gram(c):
            return PS[:, c, 0:6 * TC].rearrange("p (m q t) -> p m q t", m=3, q=2)

        def pe_delta_grams(pe):
            for c, w in enumerate(WIDTHS):
                cols = span(c)
                for h in range(4):
                    q, o = divmod(h, 2)
                    out_ = gram(c)[o * TC:o * TC + w]
                    nc.tensor.matmul(out_[:, 0, q, 0:w], CO[:, 4 + h, cols], KBT[:, h, cols], start=True, stop=True)
                    nc.tensor.matmul(out_[:, 1, q, 0:w], CO[:, 4 + h, cols], CO[:, h, cols], start=True, stop=True)
                    mm = nc.tensor.matmul(out_[:, 2, q, 0:w], GB[0:33, h, cols], GA[0:33, h, cols], start=True, stop=True)
                mm.then_inc(hs["grams"], 1)
            for j in range(3 * len(WIDTHS)):
                src, c = (CO[:, 8:12], KBET, KDT)[j % 3], j // 3
                if j >= 3:
                    pe.wait_ge(hs["turned_taken"], j - 2)
                for h in range(4):
                    mm = nc.tensor.transpose(PS[0:WIDTHS[c], 5 + j % 3, h * P:(h + 1) * P], src[:, h, span(c)], IDENT)
                mm.then_inc(hs["turned"], 1)

        def act_delta_grams(act):
            for c, w in enumerate(WIDTHS):
                act.wait_ge(hs["decay"], c + 1)
                d = DEC[:, 2 * c:2 * c + 2, 0:w]
                nc.scalar.activation(d, d, ACT.Exp).then_inc(hs["decay_exp"], 1)
            for j in range(3 * len(WIDTHS)):
                act.wait_ge(hs["turned"], j + 1)
                dest = (VBN, KBEN, KDN)[j % 3][:, 2 * (j // 3):2 * (j // 3) + 2]
                for o in range(2):
                    step = nc.scalar.activation(dest[half(o)], by_parity(wholes(5 + j % 3, 4))[half(0), o], ACT.Copy)
                step.then_inc(hs["turned_taken"], 1)

        def dve_delta_grams(dve):
            dve_chain(nc.vector.memset(GI["U"][:, GP - 2:GP], 0.0))
            u4 = GI["U"].rearrange("p m (two t) -> p m two t", two=2)
            for c, w in enumerate(WIDTHS):
                s = slice(2 * c, 2 * c + 2)
                dve.wait_ge(hs["grams"], c + 1)
                nc.vector.tensor_tensor(DEC[:, s, 0:w], gram(c)[:, 2, :, 0:w], const("neg_tri")[:, 0:w].unsqueeze(1).broadcast_to([P, 2, w]),
                                        ALU.add).then_inc(hs["decay"], 1)
            for c, w in enumerate(WIDTHS):
                s = slice(2 * c, 2 * c + 2)
                dve.wait_ge(hs["decay_exp"], c + 1)
                nc.vector.tensor_tensor(ATT[:, s, 0:w], gram(c)[:, 1, :, 0:w], DEC[:, s, 0:w], ALU.mult)
                dve_chain(nc.vector.tensor_tensor(DEC[:, s, 0:w], gram(c)[:, 0, :, 0:w], DEC[:, s, 0:w], ALU.mult))
                tri = const("tri_pair").rearrange("p (two t) -> p two t", two=2)
                dve_chain(nc.vector.tensor_tensor(u4[:, s, :, 0:w], DEC[:, s, 0:w].unsqueeze(2).broadcast_to([P, 2, 2, w]),
                                                  tri[:, :, 0:w].unsqueeze(1).broadcast_to([P, 2, 2, w]), ALU.mult))
            dve_first_level(GI, GP)

        def two_banks(bank, n):
            return PS[:, bank:bank + 2, 0:2 * n].rearrange("p o (q t) -> p o q t", q=2)

        def pe_delta_scan(pe):
            XT = GI["XT"]
            for c, w in enumerate(WIDTHS):
                if c >= 4:
                    pe.wait_ge(hs["w_taken"], c - 3)
                for h in range(4):
                    q, o = divmod(h, 2)
                    mm = nc.tensor.matmul(two_banks(2 * (c % 4), TC)[:, o, q, 0:w], KBEN[half(o), 2 * c + q], XT[half(o), 2 * c + q, o * TC:o * TC + w],
                                          start=True, stop=True)
                mm.then_inc(hs["w_ready"], 1)
            for c, w in enumerate(WIDTHS):
                if c == 0:
                    pe.wait_ge(hs["w_taken"], len(WIDTHS))
                if c:
                    pe.wait_ge(hs["s_taken"], c)
                for q in range(2):
                    for o in range(2):
                        out_, rows = PS[o * TC:o * TC + w, 5, q * P:(q + 1) * P], slice(o * TC, o * TC + w)
                        if c:
                            nc.tensor.matmul(out_, WT[:, 4 * c + 2 * q + o, 0:w], GS[:, 2 * q + o], start=True, stop=False)
                        mm = nc.tensor.matmul(out_, XT[:, 2 * c + q, rows], VBN[:, 2 * c + q], start=(c == 0), stop=True)
                mm.then_inc(hs["u_ready"], 1)
                pe.wait_ge(hs["u_taken"], c + 1)
                for h in range(4):
                    if c == len(WIDTHS) - 1:
                        break
                    q, o = divmod(h, 2)
                    mm = nc.tensor.matmul(two_banks(6, P)[:, o, q], KDN[half(o), 2 * c + q], UN[half(o), q], start=True, stop=True)
                    if h == 3:
                        mm.then_inc(hs["s_ready"], 1)
                if c:
                    pe.wait_ge(hs["o_taken"], c)
                for h in range(4):
                    q, o = divmod(h, 2)
                    out_ = two_banks(3, TC)[:, o, q, 0:w]
                    if c:
                        nc.tensor.matmul(out_, GS[:, h], QD[:, h, span(c)], start=True, stop=False)
                    mm = nc.tensor.matmul(out_, UN[half(o), q], ATT[half(o), 2 * c + q, 0:w], start=(c == 0), stop=True)
                mm.then_inc(hs["o_ready"], 1)

        def act_delta_scan(act):
            for c, w in enumerate(WIDTHS):
                act.wait_ge(hs["w_ready"], c + 1)
                nc.scalar.activation(by_parity(WT[:, 4 * c:4 * c + 4, 0:w]), two_banks(2 * (c % 4), TC)[:, :, :, 0:w], ACT.Copy, scale=-1.0).then_inc(hs["w_taken"], 1)
            for c, w in enumerate(WIDTHS):
                act.wait_ge(hs["o_ready"], c + 1)
                nc.scalar.activation(by_parity(Y8[:, 4:8, span(c)]), two_banks(3, TC)[:, :, :, 0:w], ACT.Copy).then_inc(hs["o_taken"], 1)

        def dve_delta_scan(dve):
            for c in range(len(WIDTHS)):
                dve.wait_ge(hs["u_ready"], c + 1)
                if c:
                    dve.wait_ge(hs["o_ready"], c)
                nc.vector.tensor_copy(UN, wholes(5, 2)).then_inc(hs["u_taken"], 1)
                if c == len(WIDTHS) - 1:
                    break
                dve.wait_ge(hs["s_ready"], c + 1)
                if c == 0:
                    nc.vector.tensor_copy(by_parity(GS), two_banks(6, P)).then_inc(hs["s_taken"], 1)
                else:
                    dve.wait_ge(hs["o_ready"], c + 1)
                    end = span(c).stop
                    dve_chain(nc.vector.tensor_tensor(GS, GS, EGC[:, :, end - 1:end].broadcast_to([P, 4, P]), ALU.mult))
                    nc.vector.tensor_tensor(by_parity(GS), by_parity(GS), two_banks(6, P), ALU.add).then_inc(hs["s_taken"], 1)
                dve.wait_ge(hs["s_taken"], c + 1)

        def act_delta_out(act):
            act_chain(nc.scalar.activation(SQ[:, 0:4], Y8[:, 4:8], ACT.Square))
            act.sem_inc(hs["onorm"], 1)
            act.wait_ge(hs["omean"], 1)
            act_chain(nc.scalar.activation(SQ[:, 4:8], SQ[:, 4:8], ACT.Ln))
            act_chain(nc.scalar.activation(SQ[:, 4:8], SQ[:, 4:8], ACT.Exp, scale=-0.5))
            act.sem_inc(hs["oroot"], 1)

        def pe_delta_out(pe):
            pe.wait_ge(hs["onorm"], 1)
            for h in range(4):
                mm = nc.tensor.matmul(PS[:, 4 + h, 0:S2], ONES, SQ[:, h], start=True, stop=True)
            mm.then_inc(hs["osum"], 1)

        def dve_delta_out(dve):
            dve.wait_ge(hs["osum"], 1)
            dve_chain(nc.vector.tensor_scalar(SQ[:, 4:8], PS[:, 4:8, 0:S2], 1.0 / 128, EPS, ALU.mult, ALU.add))
            dve.sem_inc(hs["omean"], 1)
            dve.wait_ge(hs["oroot"], 1)
            flat = lambda a: a.rearrange("p a b -> p (a b)")
            y = flat(Y8[:, 4:8])
            dve_chain(nc.vector.scalar_tensor_tensor(out=y, in0=y, scalar=vec("o_gain"), in1=flat(SQ[:, 4:8]), op0=ALU.mult, op1=ALU.mult))
            dve_chain(nc.vector.tensor_tensor(y, y, flat(HP[:, GZ:GZ + 4]), ALU.mult))
            dve.sem_inc(hs["outputs"], KC)
        LI, LO = arena(0, KC, 288), arena(2304, 4, D)
        XV = [arena(6528 + 2176 * j, KC, S2) for j in range(3)]
        R_, K_, V_ = (arena(13056 + 2176 * j, KC, S2) for j in range(3))
        RKV = arena(13056, 24, S2)
        LD, A_, G_, KK, B_, AC = (arena(19584 + 2176 * j, KC, S2) for j in range(6))
        BONUS = A_
        KKT, RT, BT, KT, BH, KH = (arena(2176 * j, KC, S2) for j in range(6))
        KKT_RT = arena(0, 2, KC, S2)
        LT = arena(34624, 4, S2)
        G3 = AR[:, 27136:27136 + KC * 3 * TC].rearrange("p (k m t) -> p k m t", k=KC, m=3)
        BHN, KHN, VN = (arena(30464 + 512 * j, KC, TC) for j in range(3))
        RI = {"U": arena(26112, KC, P), "X": arena(13056, KC, P), "XT": arena(14080, KC, P), "Y": arena(15104, KC, P),
              "groups": [(0, 2), (2, 2), (4, 2), (6, 2)]}
        RS_, RS2 = arena(34624, KC, 64), arena(35136, KC, 64)
        UR, UV = arena(35648, KC, 64), arena(36160, KC, 64)
        YT = H
        RV = [parts("rwkv_r", 26112, KC, S2), parts("rwkv_k", 30464, KC, S2), parts("rwkv_v", 0, KC, S2)]
        RO_H, RO_L = parts("rwkv_out", 0, KC, S2)
        EC = sb("chunk_decay", [P, KC, len(WIDTHS)])
        MU1 = sb("one_minus_k_a", [P, KC])

        rs = {k: sem("rwkv_" + k) for k in (
            "shifted", "lora_in", "lora_act", "lora_out", "lora_taken", "lora_loaded", "mixed", "sq", "ssum", "smean", "sroot",
            "cum", "ex", "ex_used", "bonus_in", "bonus_sum", "grams", "gram_taken", "turned", "turned_taken",
            "ur_ready", "ur_taken", "u_ready", "u_taken", "y_ready", "y_taken", "s_ready", "s_taken",
            "gn_sum", "gn_centred", "gn_sq", "gn_var", "gn_mean", "gn_root", "out_ready")}

        def flat(a):
            return a.rearrange("p a b -> p (a b)")

        def dve_shift(dve):
            dve_chain(nc.vector.tensor_tensor(SQ[:, :, 1:S2], H[:, :, 0:S2 - 1], H[:, :, 1:S2], ALU.subtract))
            dve_chain(nc.vector.tensor_scalar(SQ[:, :, 0:1], H[:, :, 0:1], -1.0, None, ALU.mult))

        def dve_variant(j, dest):
            for k in range(KC):
                step = nc.vector.scalar_tensor_tensor(out=dest[:, k], in0=SQ[:, k], scalar=vec("mu", KC * j + k, 1), in1=H[:, k],
                                                      op0=ALU.mult, op1=ALU.add)
                dve_chain(step)
                dve_chain.eng.sem_inc(rs["mixed"], 1)

        def dve_lora(dve):
            dve_shift(dve)
            for j, b in ((1, 0), (4, 1), (5, 2)):
                dve_variant(j, XV[b])
            for m in range(KC):
                for q, dest in enumerate((LD, A_, G_)):
                    n = 3 * m + q
                    dve.wait_ge(rs["lora_out"], n + 1)
                    if q < 2:
                        step = nc.vector.tensor_scalar(dest[:, m], PS[:, 4 + n % 4, 0:S2], vec(("w0", "a0")[q], m, 1), None, ALU.add)
                    else:
                        step = nc.vector.tensor_copy(dest[:, m], PS[:, 4 + n % 4, 0:S2])
                    step.then_inc(rs["lora_taken"], 1)

        def pe_lora(pe):
            pe.wait_ge(rs["lora_loaded"], 32)
            spans = [(0, 0, 64), (1, 64, 64), (2, 128, 128), (2, 256, 32)]
            for j, (b, at, width) in enumerate(spans):
                pe.wait_ge(rs["mixed"], KC * (b + 1))
                for k in range(KC):
                    mm = nc.tensor.matmul(PS[0:width, j, 0:S2], LI[:, k, at:at + width], XV[b][:, k], start=(k == 0), stop=(k == KC - 1))
                mm.then_inc(rs["lora_in"], 1)
            pe.wait_ge(rs["lora_act"], 4)
            for m in range(KC):
                cols = slice(m * P, (m + 1) * P)
                for q in range(3):
                    n = 3 * m + q
                    if n >= 4:
                        pe.wait_ge(rs["lora_taken"], n - 3)
                    out_ = PS[:, 4 + n % 4, 0:S2]
                    if q < 2:
                        mm = nc.tensor.matmul(out_, LO[0:64, q, cols], LT[0:64, q], start=True, stop=True)
                    else:
                        nc.tensor.matmul(out_, LO[:, 2, cols], LT[:, 2], start=True, stop=False)
                        mm = nc.tensor.matmul(out_, LO[0:32, 3, cols], LT[0:32, 3], start=False, stop=True)
                    mm.then_inc(rs["lora_out"], 1)

        def act_lora(act):
            for j, (width, func) in enumerate(((64, ACT.Tanh), (64, ACT.Copy), (128, ACT.Sigmoid), (32, ACT.Sigmoid))):
                act.wait_ge(rs["lora_in"], j + 1)
                nc.scalar.activation(LT[0:width, j], PS[0:width, j, 0:S2], func).then_inc(rs["lora_act"], 1)

        def dve_variants(dve):
            for j, b in ((0, 0), (2, 1), (3, 2)):
                dve_variant(j, XV[b])
                dve_parts(dve, ("r", b), XV[b], *RV[b])

        def act_variants(act):
            for b in range(3):
                act_parts(act, ("r", b), XV[b], RV[b][0], rs["mixed"], KC * (3 + b))

        def act_decays(act):
            act_chain(nc.scalar.activation(LD, LD, ACT.Sigmoid))
            act_chain(nc.scalar.activation(A_, A_, ACT.Sigmoid))
            act.sem_inc(rs["cum"], 1)
            act.wait_ge(rs["sq"], 1)
            act_chain(nc.scalar.activation(H[:, :, :], KK, ACT.Square))
            act.sem_inc(rs["ssum"], 1)
            act.wait_ge(rs["smean"], 1)
            act_chain(nc.scalar.activation(H[:, :, :], H[:, :, :], ACT.Ln))
            act_chain(nc.scalar.activation(H[:, :, :], H[:, :, :], ACT.Exp, scale=-0.5))
            act.sem_inc(rs["sroot"], 1)
            act.wait_ge(rs["ex_used"], 1)
            for j, (src, scale) in enumerate(((AC, 1.0), (AC, -1.0), (SQ[:, :, :], 1.0), (SQ[:, :, :], 1.0))):
                act.wait_ge(rs["ex_used"], j + 1)
                act_chain(nc.scalar.activation(H[:, :, :], src, ACT.Exp, scale=scale))
                act.sem_inc(rs["ex"], 1)

        def pe_decays(pe):
            pe.wait_ge(rs["ssum"], 1)
            for k in range(KC):
                mm = nc.tensor.matmul(PS[:, k, 0:S2], HALF, H[:, k], start=True, stop=True)
            mm.then_inc(rs["ssum"], 1)
            pe.wait_ge(rs["bonus_in"], 1)
            for k in range(KC):
                mm = nc.tensor.matmul(PS[:, k, 0:S2], HALF, KKT[:, k], start=True, stop=True)
            mm.then_inc(rs["bonus_sum"], 1)

        def dve_decays(dve):
            def per(name, k):
                return vec(name, k, 1)
            for k in range(KC):
                dve_chain(nc.vector.tensor_scalar(KK[:, k], K_[:, k], per("k_k", k), None, ALU.mult))
            dve.sem_inc(rs["sq"], 1)
            dve_chain(nc.vector.tensor_scalar(MU1[:, :], vec("k_a"), -1.0, 1.0, ALU.mult, ALU.add))
            dve.wait_ge(rs["cum"], 1)
            for k in range(KC):
                dve_chain(nc.vector.tensor_scalar(B_[:, k], A_[:, k], per("k_a", k), MU1[:, k:k + 1], ALU.mult, ALU.add))
            dve_chain(nc.vector.tensor_tensor(K_, K_, B_, ALU.mult))
            dve_chain(nc.vector.tensor_scalar(LD, LD, -math.exp(-0.5), None, ALU.mult))
            for k in range(KC):
                dve_chain(nc.vector.tensor_tensor_scan(AC[:, k], const("restart"), LD[:, k], 0.0, ALU.mult, ALU.add))
            dve.wait_ge(rs["ssum"], 2)
            dve_chain(nc.vector.tensor_scalar(H[:, :, :], PS[:, :, 0:S2], EPS, None, ALU.add))
            dve.sem_inc(rs["smean"], 1)
            dve.wait_ge(rs["sroot"], 1)
            dve_chain(nc.vector.tensor_tensor(KK, KK, H[:, :, :], ALU.mult))
            dve_chain(nc.vector.tensor_tensor(B_, KK, A_, ALU.mult))
            for k in range(KC):
                dve_chain(nc.vector.scalar_tensor_tensor(out=KKT[:, k], in0=R_[:, k], scalar=per("r_k", k), in1=K_[:, k],
                                                         op0=ALU.mult, op1=ALU.mult))
            dve.sem_inc(rs["bonus_in"], 1)
            dve.sem_inc(rs["ex_used"], 1)
            dve_chain(nc.vector.tensor_tensor(SQ[:, :, :], AC, LD, ALU.subtract))
            dve.wait_ge(rs["bonus_sum"], 1)
            dve_chain(nc.vector.tensor_tensor(BONUS, PS[:, :, 0:S2], V_, ALU.mult))
            dve.wait_ge(rs["ex"], 1)
            dve_chain(nc.vector.tensor_tensor(RT, R_, H[:, :, :], ALU.mult))
            for c in range(len(WIDTHS)):
                end = span(c).stop
                dve_chain(nc.vector.tensor_copy(EC[:, :, c:c + 1], H[:, :, end - 1:end]))
            dve.sem_inc(rs["ex_used"], 1)
            dve.wait_ge(rs["ex"], 2)
            dve_chain(nc.vector.tensor_tensor(BT, B_, H[:, :, :], ALU.mult))
            dve_chain(nc.vector.tensor_tensor(KT, K_, H[:, :, :], ALU.mult))
            dve.sem_inc(rs["ex_used"], 1)
            dve.wait_ge(rs["ex"], 3)
            dve_chain(nc.vector.tensor_tensor(KKT, KK, H[:, :, :], ALU.mult))
            for c, w in enumerate(WIDTHS):
                t = span(c)
                dve_chain(nc.vector.tensor_tensor(SQ[:, :, t], AC[:, :, t.stop - 1:t.stop].broadcast_to([P, KC, w]),
                                                  AC[:, :, t], ALU.subtract))
            dve.sem_inc(rs["ex_used"], 1)
            dve.wait_ge(rs["ex"], 4)
            dve_chain(nc.vector.tensor_tensor(BH, B_, H[:, :, :], ALU.mult))
            dve_chain(nc.vector.tensor_tensor(KH, K_, H[:, :, :], ALU.mult))

        def pe_rwkv_grams(pe, c):
            cols, w = span(c), WIDTHS[c]
            for k in range(KC):
                for m, left in enumerate((BT, KT)):
                    for o in range(2):
                        out_ = PS[o * TC:o * TC + w, k // 2, 256 * (k % 2) + 128 * m:][:, 0:P].rearrange("p (a t) -> p a t", a=2)
                        mm = nc.tensor.matmul(out_[:, :, 0:w], left[half(o), k, cols], KKT_RT[half(o), :, k, cols], start=True, stop=True)
                if k % 2:
                    mm.then_inc(rs["grams"], 1)
            for j, src in enumerate((BH, KH, V_)):
                if j == 2:
                    pe.wait_ge(rs["turned_taken"], 3 * c + 1)
                for k in range(KC):
                    mm = nc.tensor.transpose(PS[0:w, 4 + 2 * (j % 2) + k // 4, (k % 4) * P:(k % 4 + 1) * P], src[:, k, cols], IDENT)
                mm.then_inc(rs["turned"], 1)

        def act_rwkv_grams(act, c):
            for j, dest in enumerate((BHN, KHN, VN)):
                act.wait_ge(rs["turned"], 3 * c + j + 1)
                for o in range(2):
                    step = nc.scalar.activation(dest[half(o)], PS[half(0), 4 + 2 * (j % 2):6 + 2 * (j % 2), :].rearrange(
                        "p a (b v) -> p (a b) v", b=4)[:, :, o * 64:(o + 1) * 64], ACT.Copy)
                step.then_inc(rs["turned_taken"], 1)

        def dve_rwkv_grams(dve, c):
            w = WIDTHS[c]
            u4 = RI["U"].rearrange("p k (two t) -> p k two t", two=2)
            tri_pair = const("tri_pair").rearrange("p (two t) -> p two t", two=2)[:, :, 0:w].unsqueeze(1).broadcast_to([P, 2, 2, w])
            tri = const("tri").rearrange("p (m t) -> p m t", m=3)[:, :, 0:w].unsqueeze(1).broadcast_to([P, 2, 3, w])
            for b in range(4):
                s = slice(2 * b, 2 * b + 2)
                psum = PS[:, b, :].rearrange("p (k m t) -> p k m t", k=2, m=4)[:, :, :, 0:w]
                dve.wait_ge(rs["grams"], 4 * c + b + 1)
                nc.vector.tensor_tensor(u4[:, s, :, 0:w], psum[:, :, 0:1].broadcast_to([P, 2, 2, w]), tri_pair, ALU.mult)
                nc.vector.tensor_tensor(G3[:, s, :, 0:w], psum[:, :, 1:4], tri, ALU.mult).then_inc(rs["gram_taken"], 1)
            dve.wait_ge(rs["gram_taken"], 4 * (c + 1))
            dve_first_level(RI, KC)

        HEADS = [(k, half(o), o * TC) for k in range(KC) for o in range(2)]

        def pe_rwkv_scan(pe, c):
            cols, w = span(c), WIDTHS[c]
            for k, r, at in HEADS:
                o = PS[at:at + w, 0, k * 64:(k + 1) * 64]
                if c:
                    nc.tensor.matmul(o, KKT[r, k, cols], STATE[c % 2][r, k], start=True, stop=False)
                mm = nc.tensor.matmul(o, G3[r, k, 1, 0:w], VN[r, k], start=(c == 0), stop=True)
            mm.then_inc(rs["ur_ready"], 1)
            pe.wait_ge(rs["ur_taken"], c + 1)
            for k in range(KC):
                mm = nc.tensor.matmul(PS[:, 1, k * 64:(k + 1) * 64], RI["XT"][:, k], UR[:, k], start=True, stop=True)
            mm.then_inc(rs["u_ready"], 1)
            pe.wait_ge(rs["u_taken"], c + 1)
            if c < len(WIDTHS) - 1:
                for k, r, at in HEADS:
                    o = PS[r, 2, k * 64:(k + 1) * 64]
                    nc.tensor.matmul(o, BHN[r, k], UV[r, k], start=True, stop=False)
                    mm = nc.tensor.matmul(o, KHN[r, k], VN[r, k], start=False, stop=True)
                mm.then_inc(rs["s_ready"], 1)
            for k, r, at in HEADS:
                o = PS[r, 3, k * TC:k * TC + w]
                if c:
                    nc.tensor.matmul(o, STATE[c % 2][r, k], RT[r, k, cols], start=True, stop=False)
                nc.tensor.matmul(o, UV[r, k], G3[r, k, 0, 0:w], start=(c == 0), stop=False)
                mm = nc.tensor.matmul(o, VN[r, k], G3[r, k, 2, 0:w], start=False, stop=True)
            mm.then_inc(rs["y_ready"], 1)

        STATE = [RS_, RS2]

        def act_rwkv_scan(act, c):
            act.wait_ge(rs["u_ready"], c + 1)
            nc.scalar.activation(UV, halves(1, KC), ACT.Copy, scale=-1.0).then_inc(rs["u_taken"], 1)
            act.wait_ge(rs["y_ready"], c + 1)
            act_chain(nc.scalar.activation(YT[:, :, span(c)], halves(3, KC)[:, :, 0:WIDTHS[c]], ACT.Copy))

        def dve_rwkv_scan(dve, c):
            dve.wait_ge(rs["ur_ready"], c + 1)
            nc.vector.tensor_copy(UR, halves(0, KC)).then_inc(rs["ur_taken"], 1)
            if c == len(WIDTHS) - 1:
                return
            new, old = STATE[(c + 1) % 2], STATE[c % 2]
            if c:
                dve_chain(nc.vector.tensor_tensor(new, old, EC[:, :, c:c + 1].broadcast_to([P, KC, 64]), ALU.mult))
            dve.wait_ge(rs["s_ready"], c + 1)
            if c:
                dve_chain(nc.vector.tensor_tensor(new, new, halves(2, KC), ALU.add))
            else:
                dve_chain(nc.vector.tensor_copy(new, halves(2, KC)))

        GN_EPS = 64e-5

        def pe_rwkv_out(pe):
            for k in range(KC):
                mm = nc.tensor.matmul(PS[:, k, 0:S2], HALF, YT[:, k], start=True, stop=True)
            mm.then_inc(rs["gn_sum"], 1)
            pe.wait_ge(rs["gn_sq"], 1)
            for k in range(KC):
                mm = nc.tensor.matmul(PS[:, k, 0:S2], HALF, SQ[:, k], start=True, stop=True)
            mm.then_inc(rs["gn_var"], 1)

        def act_rwkv_out(act):
            act.wait_ge(rs["gn_centred"], 1)
            act_chain(nc.scalar.activation(SQ[:, :, :], YT[:, :, :], ACT.Square))
            act.sem_inc(rs["gn_sq"], 1)
            act.wait_ge(rs["gn_mean"], 1)
            act_chain(nc.scalar.activation(SQ[:, :, :], SQ[:, :, :], ACT.Ln))
            act_chain(nc.scalar.activation(SQ[:, :, :], SQ[:, :, :], ACT.Exp, scale=-0.5))
            act.sem_inc(rs["gn_root"], 1)

        def dve_rwkv_out(dve):
            dve.wait_ge(rs["gn_sum"], 1)
            for k in range(KC):
                dve_chain(nc.vector.scalar_tensor_tensor(out=YT[:, k], in0=PS[:, k, 0:S2], scalar=-1.0 / 64, in1=YT[:, k],
                                                         op0=ALU.mult, op1=ALU.add))
            dve.sem_inc(rs["gn_centred"], 1)
            dve.wait_ge(rs["gn_var"], 1)
            dve_chain(nc.vector.tensor_scalar(SQ[:, :, :], PS[:, :, 0:S2], 1.0 / 64, GN_EPS, ALU.mult, ALU.add))
            dve.sem_inc(rs["gn_mean"], 1)
            dve.wait_ge(rs["gn_root"], 1)
            dve_chain(nc.vector.tensor_tensor(YT[:, :, :], YT[:, :, :], SQ[:, :, :], ALU.mult))
            for k in range(KC):
                dve_chain(nc.vector.scalar_tensor_tensor(out=YT[:, k], in0=YT[:, k], scalar=vec("ln_w", k, 1), in1=BONUS[:, k],
                                                         op0=ALU.mult, op1=ALU.add))
                dve_chain(nc.vector.scalar_tensor_tensor(out=YT[:, k], in0=YT[:, k], scalar=vec("ln_bb", k, 1), in1=G_[:, k],
                                                         op0=ALU.add, op1=ALU.mult))
                dve.sem_inc(rs["out_ready"], 1)
        loaded, stored = sem("parameters_loaded"), sem("output_stored")
        final_ready = sem("final_ready")
        with nc.Block() as block:

            @block.sync
            def _(sp):
                sp.dma_start(X[:, :, :], x_in).then_inc(loaded, 16)
                sp.dma_start(V[:, :], vec_in[:, 0:VEC_W]).then_inc(loaded, 16)
                sp.dma_start(C[:, :], const_in).then_inc(loaded, 16)
                sp.dma_start(AR[:, FIRST_AT:FIRST_AT + FIRST_W], first_in).then_inc(loaded, 16)
                sp.dma_start(POS, pos_in).then_inc(loaded, 16)

                def load_block(n, slot):
                    sp.dma_start(W[:, slot], weights_in[n]).then_inc(landed[slot], 16)

                def stream(first, last):
                    n = first
                    while n < last and (n < RING or n % RING):
                        if n >= RING:
                            sp.wait_ge(weights_low, 2 * (n - RING + 1))
                        load_block(n, n % RING)
                        n += 1
                    rounds = (last - n) // RING
                    if rounds:
                        with sp.Fori(0, rounds) as g:
                            for u in range(RING):
                                sp.wait_ge(weights_low, g * (2 * RING) + 2 * (n + u - RING + 1))
                                load_block(g * RING + n + u, u)
                        n += rounds * RING
                    while n < last:
                        sp.wait_ge(weights_low, 2 * (n - RING + 1))
                        load_block(n, n % RING)
                        n += 1

                mix0 = BLOCKS["mix_out", 0][0] + SPLIT
                stream(0, mix0)
                sp_hybrid_rows(sp)
                mix1 = BLOCKS["mix_in", 1][0] + SPLIT
                stream(mix0, mix1)
                sp.wait_ge(stage_end, 4 * STAGES_BEFORE_RWKV)
                sp.dma_start(LI, vec_in[:, VEC_W:VEC_W + KC * 288].rearrange("p (k c) -> p k c", k=KC)).then_inc(rs["lora_loaded"], 16)
                sp.dma_start(LO, vec_in[:, VEC_W + KC * 288:].rearrange("p (k c) -> p k c", k=4)).then_inc(rs["lora_loaded"], 16)
                stream(mix1, N_BLOCKS)
                sp.wait_ge(final_ready, 1)
                sp.dma_start(out, H[:, :, META:S2]).then_inc(stored, 16)
                sp.wait_ge(stored, 16)

            @block.tensor
            def _(pe):
                pe.wait_ge(loaded, 80)
                end_stage(pe, "pe")
                for l in range(DEPTH):
                    pe_norm(pe, l, S1)
                    pe_project(pe, ("w_in", l), ("w_in", l), H1_H, H1_L, S1)
                    end_stage(pe, "pe")
                    pe_shape(pe, l)
                    end_stage(pe, "pe")
                    pe_attention(pe, attn["A", l], PT[:, AQ:AQ + 4], PT[:, AK:AK + 4], AVN)
                    end_stage(pe, "pe")
                    pe_attention(pe, attn["C", l], PT[:, CQ:CQ + 4], PT[:, CK:CK + 4], CVN)
                    end_stage(pe, "pe")
                    pe_diff_norm(pe, l)
                    pe_sgu(pe, l)
                    end_stage(pe, "pe")
                    pe_merge(pe, l)
                    pe_project(pe, ("w_out", l), ("w_out", l), H1_H, H1_L, S1)
                    end_stage(pe, "pe")
                pe_norm(pe, 2, S1)
                end_stage(pe, "pe")
                norm = 3
                for l in range(DEPTH):
                    for f in range(2):
                        pe_norm(pe, norm, S2)
                        norm += 1
                        pe_ffn(pe, 2 * l + f, l, f)
                        end_stage(pe, "pe")
                        if f:
                            continue
                        pe_norm(pe, norm, S2)
                        norm += 1
                        if l == 0:
                            pe.wait_ge(normed_ready, KC * norm)
                            pe_project(pe, ("mix_in", 0), ("hybrid", 0), MIX_H, MIX_L, S2)
                            pe_hybrid_in(pe)
                            end_stage(pe, "pe")
                            pe_fox_values(pe)
                            end_stage(pe, "pe")
                            pe_delta_prep(pe)
                            end_stage(pe, "pe")
                            pe_attention(pe, FOX, HP[:, FQ:FQ + 4], HP[:, FK:FK + 4], FVN, gates=(FA, FB))
                            end_stage(pe, "pe")
                            pe_delta_grams(pe)
                            end_stage(pe, "pe")
                            pe_inverse(pe, 0, GI)
                            end_stage(pe, "pe")
                            pe_delta_scan(pe)
                            end_stage(pe, "pe")
                            pe_delta_out(pe)
                            end_stage(pe, "pe")
                            pe_project(pe, ("mix_out", 0), ("hybrid", 1), MIX_H, MIX_L, S2)
                            end_stage(pe, "pe")
                        else:
                            end_stage(pe, "pe")
                            pe_lora(pe)
                            end_stage(pe, "pe")
                            for q in range(3):
                                pe_project(pe, ("mix_in", 1), ("r", q), *RV[q], S2, part=(8 * q, 8))
                            end_stage(pe, "pe")
                            pe_decays(pe)
                            end_stage(pe, "pe")
                            for c in range(len(WIDTHS)):
                                pe_rwkv_grams(pe, c)
                                end_stage(pe, "pe")
                                pe_inverse(pe, 1 + c, RI)
                                end_stage(pe, "pe")
                                pe_rwkv_scan(pe, c)
                                end_stage(pe, "pe")
                            pe_rwkv_out(pe)
                            pe_project(pe, ("mix_out", 1), ("r", 3), RO_H, RO_L, S2)
                            end_stage(pe, "pe")
                pe_norm(pe, norm, S2)

            @block.scalar
            def _(act):
                nonlocal act_chain
                act_chain = Chain(act, "act_chain")
                act.wait_ge(loaded, 80)
                act_setup(act)
                for n in range(SPLIT):
                    act_split(act, n)
                act.sem_inc(gates_taken, 2)
                end_stage(act, "act")
                for l in range(DEPTH):
                    act_norm(act, l, XA, S1)
                    act_parts(act, ("w_in", l), H[:, :, 0:S1], H1_H, normed_ready, KC * l)
                    take_outputs(act, act_split, ("w_in", l), (0,), act_take(PT, S1))
                    end_stage(act, "act")
                    act_shape(act, l)
                    end_stage(act, "act")
                    act_attention(act, attn["A", l])
                    end_stage(act, "act")
                    act_attention(act, attn["C", l])
                    end_stage(act, "act")
                    act_diff_norm(act, l)
                    act_sgu(act, l)
                    act_branch_parts(act, l)
                    end_stage(act, "act")
                    act_merge(act, l)
                    take_outputs(act, act_split, ("w_out", l), (), None)
                    end_stage(act, "act")
                act_norm(act, 2, XA, S1)
                end_stage(act, "act")
                norm = 3
                for l in range(DEPTH):
                    for f in range(2):
                        act_norm(act, norm, X[:, :, :], S2)
                        act_parts(act, ("ffn", 2 * l + f), H, H2_H, normed_ready, KC * norm)
                        norm += 1
                        act_ffn(act, 2 * l + f, l, f)
                        end_stage(act, "act")
                        if f:
                            continue
                        act_norm(act, norm, X[:, :, :], S2)
                        norm += 1
                        if l == 0:
                            act_parts(act, ("hybrid", 0), H, MIX_H, normed_ready, KC * (norm - 1))
                            take_outputs(act, act_split, ("mix_in", 0), (0,), act_take(HP, S2))
                            end_stage(act, "act")
                            act_hybrid_rows(act)
                            end_stage(act, "act")
                            act_delta_prep(act)
                            end_stage(act, "act")
                            act_attention(act, FOX)
                            end_stage(act, "act")
                            act_delta_grams(act)
                            end_stage(act, "act")
                            act_inverse(act, 0, GI)
                            end_stage(act, "act")
                            act_delta_scan(act)
                            end_stage(act, "act")
                            act_delta_out(act)
                            act_parts(act, ("hybrid", 1), Y8, MIX_H, hs["outputs"], 0)
                            end_stage(act, "act")
                            take_outputs(act, act_split, ("mix_out", 0), (), None)
                            end_stage(act, "act")
                        else:
                            end_stage(act, "act")
                            act_lora(act)
                            end_stage(act, "act")
                            act_variants(act)
                            take_outputs(act, act_split, ("mix_in", 1), (0,), act_take(RKV, S2))
                            end_stage(act, "act")
                            act_decays(act)
                            end_stage(act, "act")
                            for c in range(len(WIDTHS)):
                                act_rwkv_grams(act, c)
                                end_stage(act, "act")
                                act_inverse(act, 1 + c, RI)
                                end_stage(act, "act")
                                act_rwkv_scan(act, c)
                                end_stage(act, "act")
                            act_rwkv_out(act)
                            act_parts(act, ("r", 3), YT, RO_H, rs["out_ready"], 0)
                            take_outputs(act, act_split, ("mix_out", 1), (), None)
                            end_stage(act, "act")
                act_norm(act, norm, X[:, :, :], S2)

            @block.vector
            def _(dve):
                nonlocal dve_chain
                dve_chain = Chain(dve, "dve_chain")
                dve.wait_ge(loaded, 80)
                dve_setup(dve)
                for n in range(SPLIT):
                    dve_split(dve, n)
                dve.sem_inc(taken[0], 2)
                dve.sem_inc(taken[1], 2)
                dve.sem_inc(ups_taken, 2)
                end_stage(dve, "dve")
                for l in range(DEPTH):
                    dve_norm(dve, l, XA, S1, vec("norm_g", KC * l, KC), H)
                    dve_parts(dve, ("w_in", l), H[:, :, 0:S1], H1_H, H1_L)
                    take_outputs(dve, dve_split, ("w_in", l), (1,), dve_take(PT, S1))
                    end_stage(dve, "dve")
                    dve_shape(dve, l)
                    end_stage(dve, "dve")
                    dve_attention(dve, attn["A", l], mask_a, YS[:, 0:4], NEG_LAM[:, l:l + 1])
                    end_stage(dve, "dve")
                    dve_attention(dve, attn["C", l], mask_c, YS[:, 8:12])
                    end_stage(dve, "dve")
                    dve_diff_norm(dve, l)
                    dve_sgu(dve, l)
                    dve_branch_parts(dve, l)
                    end_stage(dve, "dve")
                    dve_merge(dve, l)
                    take_outputs(dve, dve_split, ("w_out", l), (0, 1), dve_add(XA, S1))
                    end_stage(dve, "dve")
                dve_norm(dve, 2, XA, S1, vec("final_g"), XA)
                end_stage(dve, "dve")
                norm = 3
                for l in range(DEPTH):
                    for f in range(2):
                        dve_norm(dve, norm, X, S2, vec("ffn_g", KC * (2 * l + f), KC), H)
                        dve_parts(dve, ("ffn", 2 * l + f), H, H2_H, H2_L)
                        norm += 1
                        dve_ffn(dve, 2 * l + f, l, f)
                        end_stage(dve, "dve")
                        if f:
                            continue
                        dve_norm(dve, norm, X, S2, vec("mix_g", KC * l, KC), H)
                        norm += 1
                        if l == 0:
                            dve_parts(dve, ("hybrid", 0), H, MIX_H, MIX_L)
                            take_outputs(dve, dve_split, ("mix_in", 0), (1,), dve_take(HP, S2))
                            end_stage(dve, "dve")
                            dve_hybrid_rows(dve)
                            end_stage(dve, "dve")
                            dve_delta_prep(dve)
                            end_stage(dve, "dve")
                            dve_attention(dve, FOX, const("mask_f").rearrange("p (a b) -> p a b", a=NT2), Y8[:, 0:4])
                            end_stage(dve, "dve")
                            dve_delta_grams(dve)
                            end_stage(dve, "dve")
                            dve_inverse(dve, 0, GI)
                            end_stage(dve, "dve")
                            dve_delta_scan(dve)
                            end_stage(dve, "dve")
                            dve_delta_out(dve)
                            dve_parts(dve, ("hybrid", 1), Y8, MIX_H, MIX_L)
                            end_stage(dve, "dve")
                            take_outputs(dve, dve_split, ("mix_out", 0), (0, 1), dve_add(X, S2))
                            end_stage(dve, "dve")
                        else:
                            end_stage(dve, "dve")
                            dve_lora(dve)
                            end_stage(dve, "dve")
                            dve_variants(dve)
                            take_outputs(dve, dve_split, ("mix_in", 1), (1,), dve_take(RKV, S2))
                            end_stage(dve, "dve")
                            dve_decays(dve)
                            end_stage(dve, "dve")
                            for c in range(len(WIDTHS)):
                                dve_rwkv_grams(dve, c)
                                end_stage(dve, "dve")
                                dve_inverse(dve, 1 + c, RI)
                                end_stage(dve, "dve")
                                dve_rwkv_scan(dve, c)
                                end_stage(dve, "dve")
                            dve_rwkv_out(dve)
                            dve_parts(dve, ("r", 3), YT, RO_H, RO_L)
                            take_outputs(dve, dve_split, ("mix_out", 1), (0, 1), dve_add(X, S2))
                            end_stage(dve, "dve")
                dve_norm(dve, norm, X, S2, vec("final2_g"), H)
                dve.sem_inc(final_ready, 1)

            @block.gpsimd
            def _(pool):
                end_stage(pool, "pool")
                for l in range(DEPTH):
                    end_stage(pool, "pool")
                    pool_shape(pool, l)
                    for _ in range(5):
                        end_stage(pool, "pool")
                end_stage(pool, "pool")
                for l in range(DEPTH):
                    for f in range(2):
                        end_stage(pool, "pool")
                        if f:
                            continue
                        if l == 0:
                            end_stage(pool, "pool")
                            pool_hybrid_rows(pool)
                            for _ in range(4):
                                end_stage(pool, "pool")
                            for _ in range(4):
                                end_stage(pool, "pool")
                        else:
                            for _ in range(4):
                                end_stage(pool, "pool")
                            for _ in range(3 * len(WIDTHS)):
                                end_stage(pool, "pool")
                            end_stage(pool, "pool")


def kernel(**inputs):
    import concourse.bacc as bacc
    from concourse.bass_utils import run_bass_kernel_spmd

    i = {k: np.asarray(v) for k, v in inputs.items()}
    constants, first = host_constants()
    vectors, lora = host_vectors(i, first)
    x = np.concatenate([i["meta_2"], i["x"][0]], 0)
    arrays = {
        "x_in": np.ascontiguousarray(x.reshape(S2, KC, P).transpose(2, 1, 0)),
        "pos_in": np.ascontiguousarray(np.broadcast_to(i["positions"].reshape(1, S1), (P, S1))),
        "const_in": constants,
        "first_in": first,
        "vec_in": np.concatenate([vectors, lora], 1),
        "weights_in": host_weights(i),
    }
    nc = bacc.Bacc("TRN2", target_bir_lowering=False, num_devices=1,
                   dynamic_dma_scratch_size=256)
    args = {n: nc.dram_tensor(n, a.shape, mybir.dt.from_np(a.dtype), kind="ExternalInput").ap() for n, a in arrays.items()}
    out = nc.dram_tensor("out", (P, KC, S1), F32, kind="ExternalOutput").ap()
    build(nc, out=out, **args)
    result = run_bass_kernel_spmd(nc, [arrays], core_ids=[0]).results[0]["out"]
    return np.ascontiguousarray(result.transpose(2, 1, 0).reshape(1, S1, D))
```

```python
import math
from contextlib import ExitStack

import numpy as np
import concourse.bass as bass
from concourse import mybir

F32 = mybir.dt.float32
F32R = mybir.dt.float32r
I32 = mybir.dt.int32
ALU = mybir.AluOpType
ACT = mybir.ActivationFunctionType
AXX = mybir.AxisListType.X

P = 128
D = 1024
KC = D // P
DEPTH = 2
S1 = 256
META = 16
S2 = S1 + META
T1 = 128
T2 = 68
TC = 64
WIDTHS = [min(TC, S2 - t) for t in range(0, S2, TC)]
NT1, NT2 = S1 // T1, S2 // T2
RING = 4
ARENA = 36700
FIRST_AT = 31744
SPLIT = 2
LEVELS = [2, 4, 8, 16, 32]
EPS = 1e-6
NEG = -1e30

AQ, AK, AV, AZ, BU, BV, BZ, CQ, CK, CV, CZ, GL = 0, 4, 8, 12, 16, 20, 24, 28, 32, 36, 40, 44
IN_CH = 68
A_HEADS, C_HEADS, F_HEADS, G_HEADS, R_HEADS = 4, 8, 8, 4, 16
FF_CH = 22
FQ, FK, FV, GQ, GK, GV, GZ = 0, 4, 8, 12, 16, 20, 24
HYB_CH = 28

BLOCKS = {}
_n = 0
for _l in range(DEPTH):
    for _name, _count in (("w_in", IN_CH), ("w_branch", 12), ("w_out", KC)):
        BLOCKS[_name, _l] = (_n, _count)
        _n += _count
for _l in range(DEPTH):
    for _name, _count in (("ffn_in0", 2 * FF_CH), ("ffn_out0", FF_CH), ("mix_in", HYB_CH if _l == 0 else 24),
                          ("mix_out", KC), ("ffn_in1", 2 * FF_CH), ("ffn_out1", FF_CH)):
        BLOCKS[_name, _l] = (_n, _count)
        _n += _count
N_BLOCKS = _n


def _columns(table):
    at, out = 0, {}
    for name, width in table:
        out[name] = (at, width)
        at += width
    return out, at


CONST, CONST_W = _columns([
    ("ident", P), ("ones", P), ("half_ones", P), ("inv_freq", 1),
    ("mask_f", NT2 * S2),
    ("tri_pair", P), ("tri", 3 * TC), ("pairs", P), ("partners", len(LEVELS) * P), ("restart", S2), ("neg_tri", TC), ("row_one", S2), ("gate_sign", 1),
])
FIRST, FIRST_W = _columns([
    ("rope", P), ("causal_w", P), ("mask_a", 2 * S1), ("mask_c", 2 * S1), ("count_c", 2 * S1),
    ("lam", DEPTH * 4 * 64), ("sgu_w", DEPTH * 4 * P), ("sgu_b", DEPTH * 4 * P),
])
VEC, VEC_W = _columns([
    ("norm_g", DEPTH * KC), ("final_g", KC), ("subln_g", DEPTH), ("ln_g", DEPTH * 4), ("ln_b", DEPTH * 4),
    ("ffn_g", DEPTH * 2 * KC), ("mix_g", DEPTH * KC), ("final2_g", KC), ("hyb_small", KC * T2),
    ("conv", 12 * 4), ("o_gain", 1), ("mu", 6 * KC), ("w0", KC), ("a0", KC),
    ("k_k", KC), ("k_a", KC), ("r_k", KC), ("ln_w", KC), ("ln_bb", KC),
    ("gate_b", 3),
])


def host_constants():
    c, first = np.zeros((P, CONST_W), np.float32), np.zeros((P, FIRST_W), np.float32)

    def put(name, value):
        table, into = (CONST, c) if name in CONST else (FIRST, first)
        at, width = table[name]
        into[:value.shape[0], at:at + width] = value.reshape(value.shape[0], width)

    p = np.arange(P)
    put("ident", np.eye(P, dtype=np.float32))
    put("ones", np.ones((P, P), np.float32))
    put("half_ones", (p[:, None] // 64 == p[None] // 64).astype(np.float32))
    half, rot = 8, 16
    perm = np.zeros((P, P), np.float32)
    for base in (0, 64):
        for i in range(half):
            perm[base + half + i, base + i] = -1.0
            perm[base + i, base + half + i] = 1.0
    put("rope", perm)
    put("causal_w", (p[:, None] <= p[None]).astype(np.float32))
    inv = np.power(np.float32(500000.0), -np.arange(half, dtype=np.float32) * np.float32(2.0) / np.float32(rot))
    f = np.zeros((P, 1), np.float32)
    for base in (0, 64):
        f[base:base + half, 0] = inv
        f[base + half:base + rot, 0] = inv
    put("inv_freq", f)
    q = np.arange(2)[None, :, None] * T1 + p[:, None, None]
    rel = q - np.arange(S1)[None, None, :]
    put("mask_a", np.where(rel >= 0, 0.0, NEG).astype(np.float32))
    count = ((rel >= 0) & (rel <= 128)).astype(np.float32) + ((rel >= 0) & (rel % 4 == 0)) + ((rel >= 0) & (rel % 16 == 0))
    put("mask_c", np.where(count > 0, 0.0, NEG).astype(np.float32))
    put("count_c", count.astype(np.float32))
    t = np.arange(T2)
    q = np.arange(NT2)[None, :, None] * T2 + t[:, None, None]
    put("mask_f", np.where(q >= np.arange(S2)[None, None, :], 0.0, NEG).astype(np.float32))
    r, col = p[:, None] % TC, np.arange(TC)[None]
    strict, incl, same = r < col, r <= col, p[:, None] // TC == p[None] // TC
    put("tri", np.stack([incl, strict, incl], 1).astype(np.float32))
    put("tri_pair", (np.tile(strict, (1, 2)) & same).astype(np.float32))
    put("neg_tri", np.where(incl, 0.0, NEG).astype(np.float32))
    put("pairs", (np.tile(strict & (r // 2 == col // 2), (1, 2)) & same).astype(np.float32))
    partners = [(p[:, None] // (2 * b) == p[None] // (2 * b)) & (p[:, None] // b != p[None] // b) & (p[:, None] > p[None])
                for b in LEVELS]
    put("partners", np.concatenate(partners, 1).astype(np.float32))
    put("restart", np.tile((np.arange(S2) % TC != 0).astype(np.float32), (P, 1)))
    put("row_one", np.ones((P, S2), np.float32))
    put("gate_sign", np.where(p < 32, -1.0, 1.0).astype(np.float32)[:, None])
    return c, first


def host_vectors(i, first):
    v = np.zeros((P, VEC_W), np.float32)

    def put(name, value):
        table, into = (VEC, v) if name in VEC else (FIRST, first)
        at, width = table[name]
        into[:value.shape[0], at:at + width] = value.reshape(value.shape[0], width)

    def cols(a):
        a = np.asarray(a)
        return np.ascontiguousarray(a.reshape(-1, P).T)

    def every(a):
        return np.broadcast_to(np.asarray(a).reshape(1, -1), (P, np.asarray(a).size))

    put("norm_g", cols(i["norm_g"]))
    put("final_g", cols(i["final_g"]))
    put("subln_g", cols(i["subln_g"]))
    put("ln_g", cols(i["sgu_ln_g"]))
    put("ln_b", cols(i["sgu_ln_b"]))
    put("lam", every(np.stack([i[n] for n in ("lam_q1", "lam_k1", "lam_q2", "lam_k2")], 1)))
    put("sgu_w", np.ascontiguousarray(np.asarray(i["sgu_w"]).transpose(3, 0, 1, 2)).reshape(P, -1))
    put("sgu_b", every(i["sgu_b"]))
    put("ffn_g", cols(i["ffn_norm_2"]))
    put("mix_g", cols(i["mix_norm_2"]))
    put("final2_g", cols(i["final_norm_2"]))
    w = np.asarray(i["hyb_w_in_2"])[0]
    small = np.zeros((D, T2), np.float32)
    small[:, 0:8], small[:, 32:36], small[:, 64:68] = w[:, 1536:1544], w[:, 3080:3084], w[:, 3084:3088]
    put("hyb_small", small.reshape(KC, P, T2).transpose(1, 0, 2).reshape(P, -1))
    put("conv", np.asarray(i["hyb_conv_2"])[0].reshape(4, 12, P).transpose(2, 1, 0).reshape(P, -1))
    put("o_gain", cols(i["hyb_o_gain_2"]))
    put("mu", cols(i["rwkv_mu_2"][0]))
    for name, key in (("w0", "rwkv_w0_2"), ("a0", "rwkv_a0_2"), ("k_k", "rwkv_k_k_2"), ("k_a", "rwkv_k_a_2"),
                      ("r_k", "rwkv_r_k_2"), ("ln_w", "rwkv_ln_w_2"), ("ln_bb", "rwkv_ln_b_2")):
        put(name, cols(i[key]))
    b = np.zeros((P, 3), np.float32)
    b[0:8, 0] = np.asarray(i["hyb_fox_bf_2"])[0]
    b[32:36, 0] = np.asarray(i["hyb_dt_bias_2"])[0]
    b[32:36, 1] = np.asarray(i["hyb_a_log_2"])[0]
    put("gate_b", b)
    lora = np.concatenate([i[n][0] for n in ("rwkv_w1_2", "rwkv_a1_2", "rwkv_g1_2")], 1)
    lora = lora.reshape(KC, P, 288).transpose(1, 0, 2).reshape(P, -1)
    inner = np.zeros((P, 4, D), np.float32)
    inner[0:64, 0], inner[0:64, 1] = i["rwkv_w2_2"][0], i["rwkv_a2_2"][0]
    inner[:, 2], inner[0:32, 3] = i["rwkv_g2_2"][0][:P], i["rwkv_g2_2"][0][P:]
    return v, np.concatenate([lora, inner.reshape(P, -1)], 1)


def host_weights(i):
    w = np.empty((N_BLOCKS, P, D), np.float32)

    def by_output(a):
        a = np.asarray(a)
        m = a.shape[1] // P
        return a.reshape(KC, P, m, P).transpose(2, 1, 0, 3).reshape(m, P, D)

    def put(key, value):
        at, count = BLOCKS[key]
        w[at:at + count] = value

    for l in range(DEPTH):
        put(("w_in", l), by_output(i["w_in"][l]))
        wb = np.asarray(i["w_branch"][l])
        wb = wb.reshape(3, 4, P, 4, 2, P).transpose(3, 0, 2, 4, 1, 5).reshape(12, P, D)
        put(("w_branch", l), wb)
        put(("w_out", l), by_output(i["w_out"][l]))
        for f in range(2):
            a = by_output(i["ffn_w_in_2"][l, f]).reshape(2, FF_CH, P, D).transpose(1, 0, 2, 3)
            put((f"ffn_in{f}", l), a.reshape(2 * FF_CH, P, D))
            put((f"ffn_out{f}", l), np.asarray(i["ffn_w_out_2"][l, f]).reshape(FF_CH, P, D))
    h = np.asarray(i["hyb_w_in_2"])[0]
    h = np.concatenate([h[:, 0:1536], h[:, 1544:3080], h[:, 3088:3600]], 1)
    put(("mix_in", 0), by_output(h))
    put(("mix_out", 0), by_output(i["hyb_w_out_2"][0]))
    put(("mix_in", 1), np.concatenate([by_output(i[n][0]) for n in ("rwkv_w_r_2", "rwkv_w_k_2", "rwkv_w_v_2")]))
    put(("mix_out", 1), by_output(i["rwkv_w_o_2"][0]))
    return w


def build(nc, x_in, pos_in, const_in, first_in, vec_in, weights_in, out):
    ctx = ExitStack()
    with ctx:
        def sb(name, shape, dt=F32):
            return ctx.enter_context(nc.sbuf_tensor(name, shape, dt))

        sems = {}

        def sem(name):
            if name not in sems:
                sems[name] = ctx.enter_context(nc.semaphore(name))
            return sems[name]

        C = sb("consts", [P, CONST_W])
        V = sb("vectors", [P, VEC_W])
        W = sb("weight_ring", [P, RING, D])
        WH, WL = sb("weights_high", [P, SPLIT, D], F32R), sb("weights_low", [P, SPLIT, D], F32R)
        X = sb("residual", [P, KC, S2])
        H = sb("normed", [P, KC, S2])
        SQ = sb("squares", [P, KC, S2])
        RS = sb("rstd", [P, 3, S2])
        SM = sb("small", [P, 64])
        AR_BYTE = nc.sbuf_base
        AR = sb("arena", [P, ARENA])
        PS = ctx.enter_context(nc.psum_tensor("psum", [P, 8, 512], F32))

        def const(name, rows=P):
            at, width = CONST[name]
            return C[0:rows, at:at + width]

        def vec(name, at=0, width=None, rows=P):
            start, w = VEC[name]
            return V[0:rows, start + at:start + at + (w - at if width is None else width)]

        def first(name):
            at, width = FIRST[name]
            return AR[:, FIRST_AT + at:FIRST_AT + at + width]

        def part(name, at, chunks, n):
            return nc.alloc_sbuf_tensor_at(name, [P, chunks, n], F32R, offset=AR_BYTE + 4 * at)

        def parts(name, at, chunks, n):
            return part(f"{name}_high", at, chunks, n), part(f"{name}_low", at + chunks * n, chunks, n)

        def arena(at, *shape):
            n = math.prod(shape)
            v = AR[:, at:at + n]
            if len(shape) == 2:
                return v.rearrange("p (a b) -> p a b", a=shape[0])
            if len(shape) == 3:
                return v.rearrange("p (a b c) -> p a b c", a=shape[0], b=shape[1])
            return v

        STAGES_BEFORE_RWKV = 6 * DEPTH + 1 + 9 + 1
        IDENT, ONES, HALF = const("ident"), const("ones"), const("half_ones")
        XA = X[:, :, META:S2]

        class Chain:

            def __init__(self, eng, name):
                self.eng, self.sem, self.n = eng, sem(name), 0

            def __call__(self, step):
                self.later(step)
                self.settle()

            def later(self, step):
                self.n += 1
                step.then_inc(self.sem, 1)

            def settle(self):
                self.eng.wait_ge(self.sem, self.n)

        act_chain = dve_chain = None
        stage_end = sem("stage_end")
        stages = {}

        def end_stage(eng, name):
            stages[name] = stages.get(name, 0) + 1
            eng.drain().then_inc(stage_end, 1)
            eng.wait_ge(stage_end, 4 * stages[name])

        landed = [sem(f"weights_landed{u}") for u in range(RING)]
        weights_high, weights_low = sem("weights_high_ready"), sem("weights_low_ready")
        blocks_done = sem("blocks_done")

        def at_turn(value, g, step):
            return value if g is None else g * step + value

        def act_split(act, n, g=None):
            if n >= N_BLOCKS:
                return
            act.wait_ge(landed[n % RING], at_turn(16 * (n // RING + 1), g, 16))
            if n >= SPLIT:
                act.wait_ge(blocks_done, at_turn(n - SPLIT + 1, g, RING))
            for half in (slice(0, 512), slice(512, 1024)):
                nc.scalar.activation(WH[:, n % SPLIT, half], W[:, n % RING, half], ACT.Copy).then_inc(weights_high, 1)

        def dve_split(dve, n, g=None):
            if n >= N_BLOCKS:
                return
            for j, half in enumerate((slice(0, 512), slice(512, 1024))):
                dve.wait_ge(weights_high, at_turn(2 * n + j + 1, g, 2 * RING))
                nc.vector.tensor_tensor(WL[:, n % SPLIT, half], W[:, n % RING, half],
                                        WH[:, n % SPLIT, half].bitcast(F32), ALU.subtract).then_inc(weights_low, 1)

        def split_ahead(eng, split, first, count):
            if count >= RING:
                with eng.Fori(0, count // RING) as g:
                    for u in range(RING):
                        split(eng, first + u + SPLIT, g)
            for n in range(first + count // RING * RING, first + count):
                split(eng, n + SPLIT)

        def pe_arrived(pe, n, g=None):
            pe.wait_ge(weights_low, at_turn(2 * n + 2, g, 2 * RING))

        def pe_tile(psum, n, t, high, low, start, stop):
            s, cols = n % SPLIT, slice(t * P, (t + 1) * P)
            nc.tensor.matmul(psum, WH[:, s, cols], high, start=start, stop=False)
            nc.tensor.matmul(psum, WH[:, s, cols], low, start=False, stop=False)
            return nc.tensor.matmul(psum, WL[:, s, cols], high, start=False, stop=stop)

        act_high, act_low = sem("activation_high_ready"), sem("activation_low_ready")
        JOBS = {name: j for j, name in enumerate(
            [("w_in", 0), ("w_out", 0), ("w_in", 1), ("w_out", 1), ("ffn", 0), ("hybrid", 0), ("hybrid", 1), ("ffn", 1), ("ffn", 2),
             ("r", 0), ("r", 1), ("r", 2), ("r", 3), ("ffn", 3)])}

        def act_parts(act, job, source, high, ready, base):
            for k in range(KC):
                act.wait_ge(ready, base + k + 1)
                nc.scalar.activation(high[:, k], source[:, k], ACT.Copy).then_inc(act_high, 1)

        def dve_parts(dve, job, source, high, low):
            for k in range(KC):
                dve.wait_ge(act_high, KC * JOBS[job] + k + 1)
                nc.vector.tensor_tensor(low[:, k], source[:, k], high[:, k].bitcast(F32), ALU.subtract).then_inc(act_low, 1)

        taken = [sem("even_outputs_taken"), sem("odd_outputs_taken")]
        OUTS = {}
        total = 0
        for l in range(DEPTH):
            for name in ("w_in", "w_out"):
                OUTS[name, l] = total
                total += BLOCKS[name, l][1]
        for l in range(DEPTH):
            for name in ("mix_in", "mix_out"):
                OUTS[name, l] = total
                total += BLOCKS[name, l][1]
        assert all(v % 4 == 0 for v in OUTS.values())

        def pe_project(pe, key, job, high, low, n, part=(0, None)):
            block, count = BLOCKS[key]
            o = OUTS[key] + part[0]
            block += part[0]
            count = part[1] or count
            with pe.Fori(0, count // 4) as g:
                for u in range(4):
                    pe_arrived(pe, block + u, g)
                    pe.wait_ge(taken[u % 2], g * 2 + (o + u) // 2 + 1)
                    for k in range(KC):
                        if u == 0:
                            pe.wait_ge(act_low, KC * JOBS[job] + k + 1)
                        mm = pe_tile(PS[:, u, 0:n], block + u, k, high[:, k], low[:, k], k == 0, k == KC - 1)
                    mm.then_inc(blocks_done, 1)
        def take_outputs(eng, split, key, parities, take, part=(0, None)):
            block, count = BLOCKS[key]
            block += part[0]
            count = part[1] or count
            with eng.Fori(0, count // 4) as g:
                for u in range(4):
                    split(eng, block + u + SPLIT, g)
                    if u % 2 in parities:
                        eng.wait_ge(blocks_done, g * 4 + block + u + 1)
                        take(g * 4 + (part[0] + u), u).then_inc(taken[u % 2], 1)

        def act_take(dest, n):
            def take(chunk, bank):
                nc.scalar.wait_ge(blocks_done, 1)
                return nc.scalar.activation(dest[:, chunk, 0:n], PS[:, bank, 0:n], ACT.Copy)
            return take

        def dve_take(dest, n):
            return lambda chunk, bank: nc.vector.tensor_scalar(
                dest[:, chunk, 0:n], PS[:, bank, 0:n], 1.0, None, ALU.mult)

        def dve_add(dest, n):
            return lambda chunk, bank: nc.vector.scalar_tensor_tensor(
                out=dest[:, chunk, 0:n], in0=PS[:, bank, 0:n], scalar=1.0, in1=dest[:, chunk, 0:n],
                op0=ALU.mult, op1=ALU.add)

        residual_ready = sem("residual_chunk_ready")
        squares_ready, ssum_ready = sem("squares_ready"), sem("square_sum_ready")
        mean_ready, rstd_ready, normed_ready = sem("mean_square_ready"), sem("rstd_ready"), sem("normed_ready")

        def load_log_exp(act):
            act.preload_act_table_set("natural_log_exp_and_others")

        def act_norm(act, use, x, n):
            for k in range(KC):
                act.wait_ge(residual_ready, KC * use + k + 1)
                nc.scalar.activation(SQ[:, k, 0:n], x[:, k], ACT.Square).then_inc(squares_ready, 1)
            if use == 0:
                for b in range(SPLIT):
                    act_split(act, b)
            act.wait_ge(mean_ready, use + 1)
            act_chain(nc.scalar.activation(RS[:, 1, 0:n], RS[:, 0, 0:n], ACT.Ln))
            nc.scalar.activation(RS[:, 2, 0:n], RS[:, 1, 0:n], ACT.Exp, scale=-0.5).then_inc(rstd_ready, 1)

        def pe_norm(pe, use, n):
            for k in range(KC):
                pe.wait_ge(squares_ready, KC * use + k + 1)
                mm = nc.tensor.matmul(PS[:, 0, 0:n], ONES, SQ[:, k, 0:n], start=(k == 0), stop=(k == KC - 1))
            mm.then_inc(ssum_ready, 1)

        def dve_norm(dve, use, x, n, gain, dest):
            dve.wait_ge(ssum_ready, use + 1)
            nc.vector.tensor_scalar(RS[:, 0, 0:n], PS[:, 0, 0:n], 1.0 / D, EPS, ALU.mult, ALU.add)\
                .then_inc(mean_ready, 1)
            dve.wait_ge(rstd_ready, use + 1)
            for k in range(KC):
                nc.vector.scalar_tensor_tensor(out=dest[:, k, 0:n], in0=x[:, k], scalar=gain[:, k:k + 1],
                                               in1=RS[:, 2, 0:n], op0=ALU.mult, op1=ALU.mult)\
                    .then_inc(normed_ready, 1)
            dve.wait_ge(normed_ready, KC * (use + 1))

        class Attn:

            def __init__(self, kind, layer):
                self.kind, self.layer = kind, layer
                self.heads, self.maps = {"A": (A_HEADS, 2), "C": (C_HEADS, 1), "F": (F_HEADS, 1)}[kind]
                self.t, self.nt = (T2, NT2) if kind == "F" else (T1, NT1)
                self.n = self.t * self.nt
                self.base = layer * self.heads
                self.e = 128 if kind == "A" else 64
                name = {"A": "diff", "C": "dilated", "F": "fox"}[kind]
                self.s = {k: sem(f"{name}_{k}") for k in (
                    "scores_ready", "scores_taken", "neg_max_ready", "exp_ready", "probs_ready",
                    "turned", "turned_taken", "out_ready", "out_taken")}

            def score(self, h, m, qi):
                b, w = h % 2, self.t * (qi + 1)
                if self.kind == "A":
                    return PS[0:self.t, 2 * b + m, 256 * qi:256 * qi + w]
                if self.kind == "C":
                    return PS[0:self.t, h % 4, 256 * qi:256 * qi + w]
                bank, at = [(0, 0), (0, 68), (0, 204), (1, 0)][qi]
                return PS[0:self.t, 2 * b + bank, at:at + w]

            def rows(self, h, m):
                r = 64 * (m if self.kind == "A" else h % 2)
                return slice(r, r + 64), (h if self.kind == "A" else h // 2)

            def turn_at(self, h, kj):
                if self.kind == "F":
                    bank, at = [(4, 0), (4, 272), (5, 0), (5, 136)][kj]
                else:
                    bank, at = 4 + h % 2, 256 * kj
                return bank, at, self.n - self.t * kj

        def pe_attention(pe, A, q, k, v, gates=None):
            s = A.s

            def scores(h):
                if h >= 2:
                    pe.wait_ge(s["scores_taken"], A.base + h - 1)
                for m in range(A.maps):
                    r, c = A.rows(h, m)
                    for qi in range(A.nt):
                        w = A.t * (qi + 1)
                        mm = nc.tensor.matmul(A.score(h, m, qi), q[r, c, qi * A.t:(qi + 1) * A.t], k[r, c, 0:w],
                                              start=True, stop=gates is None)
                        if gates is not None:
                            g = slice(64 * (h % 2), 64 * (h % 2) + 33)
                            mm = nc.tensor.matmul(A.score(h, m, qi), gates[0][g, h // 2, qi * A.t:(qi + 1) * A.t],
                                                  gates[1][g, h // 2, 0:w], start=False, stop=True)
                mm.then_inc(s["scores_ready"], 1)

            def turn(h):
                pe.wait_ge(s["probs_ready"], A.base + h + 1)
                back = 1 if A.kind == "F" else 2
                if h >= back:
                    pe.wait_ge(s["turned_taken"], A.base + h - back + 1)
                for kj in range(A.nt):
                    bank, at, _ = A.turn_at(h, kj)
                    for qi in range(kj, A.nt):
                        o = at + A.t * (qi - kj)
                        mm = nc.tensor.transpose(PS[0:A.t, bank, o:o + A.t],
                                                 A.probs(h, qi)[:, kj * A.t:(kj + 1) * A.t], IDENT[0:A.t, 0:A.t])
                mm.then_inc(s["turned"], 1)

            def weigh(h):
                pe.wait_ge(s["turned_taken"], A.base + h + 1)
                if h >= 2:
                    pe.wait_ge(s["out_taken"], A.base + h - 1)
                o = 64 * (h % 2) if A.e == 64 else 0
                for kj in range(A.nt):
                    mm = nc.tensor.matmul(PS[o:o + A.e, 6 + h % 2, kj * A.t:A.n],
                                          v[0:A.t, kj, h * A.e:(h + 1) * A.e], A.probs_t(h, kj),
                                          start=(kj == 0), stop=(kj == A.nt - 1))
                mm.then_inc(s["out_ready"], 1)

            scores(0)
            scores(1)
            for h in range(A.heads):
                if h + 2 < A.heads:
                    scores(h + 2)
                turn(h)
                weigh(h)

        def act_attention(act, A):
            s = A.s
            for h in range(A.heads):
                act.wait_ge(s["neg_max_ready"], A.base + h + 1)
                for m in range(A.maps):
                    for qi in range(A.nt):
                        j = m * A.nt + qi
                        step = nc.scalar.activation(
                            A.logits(h, m, qi), A.logits(h, m, qi), ACT.Exp, bias=A.stat(h, 1, j), scale=0.125,
                            **({} if A.kind == "C" else {"accum_out": A.stat(h, 2, j)}))
                step.then_inc(s["exp_ready"], 1)
                if h >= 1:
                    act_turned(act, A, h - 1)
            act_turned(act, A, A.heads - 1)

        def act_turned(act, A, h):
            act.wait_ge(A.s["turned"], A.base + h + 1)
            if h >= 2:
                act.wait_ge(A.s["out_ready"], A.base + h - 1)
            if A.kind == "F":
                act_chain.later(nc.scalar.activation(A.turned(h)[:, 0:476], PS[0:A.t, 4, 0:476], ACT.Copy))
                step = nc.scalar.activation(A.turned(h)[:, 476:680], PS[0:A.t, 5, 0:204], ACT.Copy)
            else:
                step = nc.scalar.activation(A.turned(h)[:, 0:384], PS[0:A.t, 4 + h % 2, 0:384], ACT.Copy)
            step.then_inc(A.s["turned_taken"], 1)

        def dve_attention(dve, A, mask, dest, neg_lam=None, beside=None):
            s = A.s

            def masked_max(h):
                dve.wait_ge(s["scores_ready"], A.base + h + 1)
                if h >= 2:
                    dve.wait_ge(s["turned"], A.base + h - 1)
                for m in range(A.maps):
                    for qi in range(A.nt):
                        w = A.t * (qi + 1)
                        dve_chain.later(nc.vector.tensor_tensor_reduce(
                            A.logits(h, m, qi), A.score(h, m, qi), mask[0:A.t, qi, 0:w], 1.0, -3e38,
                            ALU.add, ALU.max, A.stat(h, 0, m * A.nt + qi)))
                dve_chain.settle()
                n = A.maps * A.nt
                dve_chain(nc.vector.tensor_scalar(A.stat(h, 1, 0, n), A.stat(h, 0, 0, n), -0.125, None, ALU.mult))
                dve.sem_inc(s["scores_taken"], 1)
                dve.sem_inc(s["neg_max_ready"], 1)

            def normalise(h):
                n = A.maps * A.nt
                dve.wait_ge(s["exp_ready"], A.base + h + 1)
                if A.kind == "C":
                    for qi in range(A.nt):
                        w = A.t * (qi + 1)
                        dve_chain.later(nc.vector.tensor_tensor_reduce(
                            A.logits(h, 0, qi), A.logits(h, 0, qi), first("count_c").rearrange(
                                "p (a b) -> p a b", a=2)[:, qi, 0:w], 1.0, 0.0, ALU.mult, ALU.add, A.stat(h, 2, qi)))
                    dve_chain.settle()
                dve_chain(nc.vector.reciprocal(A.stat(h, 3, 0, n), A.stat(h, 2, 0, n)))
                if A.kind == "A":
                    dve_chain(nc.vector.tensor_scalar(A.stat(h, 3, 2, 2), A.stat(h, 3, 2, 2), neg_lam, None, ALU.mult))
                    for qi in range(A.nt):
                        dve_chain.later(nc.vector.tensor_scalar(A.logits(h, 1, qi), A.logits(h, 1, qi),
                                                                A.stat(h, 3, 2 + qi), None, ALU.mult))
                    dve_chain.settle()
                    for qi in range(A.nt):
                        dve_chain.later(nc.vector.scalar_tensor_tensor(
                            out=A.logits(h, 0, qi), in0=A.logits(h, 0, qi), scalar=A.stat(h, 3, qi),
                            in1=A.logits(h, 1, qi), op0=ALU.mult, op1=ALU.add))
                else:
                    for qi in range(A.nt):
                        dve_chain.later(nc.vector.tensor_scalar(A.logits(h, 0, qi), A.logits(h, 0, qi),
                                                                A.stat(h, 3, qi), None, ALU.mult))
                dve_chain.settle()
                dve.sem_inc(s["probs_ready"], 1)

            def take(h):
                dve.wait_ge(s["out_ready"], A.base + h + 1)
                o = 64 * (h % 2) if A.e == 64 else 0
                c = h if A.e == 128 else h // 2
                nc.vector.tensor_copy(dest[o:o + A.e, c, 0:A.n], PS[o:o + A.e, 6 + h % 2, 0:A.n])\
                    .then_inc(s["out_taken"], 1)

            masked_max(0)
            for h in range(A.heads):
                if h + 1 < A.heads:
                    masked_max(h + 1)
                normalise(h)
                if h >= 1:
                    take(h - 1)
                if beside is not None:
                    beside(h)
            take(A.heads - 1)

        def place_attention(A, at):
            width = A.maps * A.nt * A.n
            base_t = at + 2 * width
            A.logits = lambda h, m, qi: AR[0:A.t, at + (h % 2) * width + (m * A.nt + qi) * A.n:][:, 0:A.t * (qi + 1)]
            A.probs = lambda h, qi: A.logits(h, 0, qi)
            A.turned = lambda h: AR[0:A.t, base_t + 1024 * (h % 2):base_t + 1024 * (h % 2) + 1024]

            def probs_t(h, kj):
                starts = [0, 272, 476, 612] if A.kind == "F" else [0, 256]
                return A.turned(h)[:, starts[kj]:starts[kj] + A.n - A.t * kj]
            A.probs_t = probs_t
            A.stat = lambda h, row, j, n=1: SM[0:A.t, 32 * (h % 2) + 8 * row + j:32 * (h % 2) + 8 * row + j + n]
            return A
        PT = arena(0, IN_CH, S1)
        AVN, CVN, BVN = (arena(17408 + 1024 * j, 2, 512) for j in range(3))
        YS = arena(20480, 12, S1)
        SCR = 23552
        NEG_LAM, SUB_G = sb("neg_lam", [P, 8]), sb("subln_gain", [P, 2])
        attn = {}
        for l in range(DEPTH):
            attn["A", l] = place_attention(Attn("A", l), SCR)
            attn["C", l] = place_attention(Attn("C", l), SCR)
        DIFF_OUT, DIFF_RS = arena(SCR, 4, S1), arena(SCR + 1024, 4, S1)
        POS = arena(SCR + 2048, S1).bitcast(I32)
        COS, SIN = arena(FIRST_AT + FIRST_W, S1), arena(FIRST_AT + FIRST_W + S1, S1)
        YS_H, YS_L = part("branches_high", 17408, 12, S1), part("branches_low", SCR + 1024, 12, S1)
        H1_H, H1_L = parts("first_normed", SCR + 4096, KC, S1)
        H2_H, H2_L = parts("ffn_normed", 0, KC, S2)
        F_H, F_L = parts("ffn_inner", 2 * KC * S2, FF_CH, S2)
        FFN_GATE, FFN_PROD = (arena((2 * KC + 2 * FF_CH + 2 * j) * S2, 2, S2) for j in range(2))
        mask_a = first("mask_a").rearrange("p (a b) -> p a b", a=2)
        mask_c = first("mask_c").rearrange("p (a b) -> p a b", a=2)
        LAM_INIT = [0.8 - 0.6 * math.exp(-0.3 * l) for l in range(DEPTH)]

        inputs_ready = sem("inputs_ready")
        tables = sem("rope_tables")
        gated = sem("nonlinear_ready")
        permuted, rope_sin, rope_cos, roped = (sem(n) for n in ("rope_permuted", "rope_sin_part", "rope_cos_part", "roped"))
        values_turned, values_taken = sem("values_turned"), sem("values_taken")
        sum_ready, row_ready, stat_ready = sem("sum_ready"), sem("row_ready"), sem("stat_ready")
        norm_ready, mixed_ready = sem("norm_ready"), sem("mixed_ready")
        branches_ready, branch_parts = sem("branches_ready"), sem("branch_parts_ready")
        merged_in, merged_part, merged_ready = sem("branch_ready"), sem("branch_gated"), sem("merged_ready")
        gates_taken, ups_taken = sem("gates_taken"), sem("ups_taken")

        def dve_setup(dve):
            ang, turns, ang2 = arena(SCR, S1), arena(SCR + 256, S1), arena(SCR + 512, S1)
            dve_chain(nc.vector.tensor_copy(ang, POS))
            dve_chain(nc.vector.tensor_scalar(ang, ang, const("inv_freq"), None, ALU.mult))
            magic = 12582912.0
            for dest, shift in ((ang2, 0.0), (arena(SCR + 768, S1), 0.25)):
                dve_chain(nc.vector.tensor_scalar(turns, ang, 1.0 / (2 * math.pi), shift, ALU.mult, ALU.add))
                dve_chain(nc.vector.tensor_scalar(turns, turns, magic, None, ALU.add))
                dve_chain(nc.vector.tensor_scalar(turns, turns, magic, None, ALU.subtract))
                last = ang
                for part in (-6.28125, -0.0019350051879882812, -3.0199159819567e-07):
                    dve_chain(nc.vector.scalar_tensor_tensor(out=dest, in0=turns, scalar=part, in1=last,
                                                             op0=ALU.mult, op1=ALU.add))
                    last = dest
                if shift:
                    dve_chain(nc.vector.tensor_scalar(dest, dest, math.pi / 2, None, ALU.add))
                dve_chain(nc.vector.tensor_scalar(dest, dest, 3.1415925, -3.1415925, ALU.min, ALU.max))
                dve.sem_inc(tables, 1)
            prod = arena(SCR + 1024, 4, 64)
            lam = first("lam").rearrange("p (l a b) -> p l a b", l=DEPTH, a=4)
            for l in range(DEPTH):
                for j in range(2):
                    dve_chain(nc.vector.tensor_tensor_reduce(prod[:, 2 * l + j], lam[:, l, 2 * j], lam[:, l, 2 * j + 1],
                                                             1.0, 0.0, ALU.mult, ALU.add, SM[:, 2 * l + j:2 * l + j + 1]))
            dve.sem_inc(tables, 1)
            dve.wait_ge(stat_ready, 1)
            for l in range(DEPTH):
                dve_chain(nc.vector.tensor_tensor(NEG_LAM[:, l:l + 1], SM[:, 8 + 2 * l + 1:8 + 2 * l + 2],
                                                  SM[:, 8 + 2 * l:8 + 2 * l + 1], ALU.subtract))
                dve_chain(nc.vector.tensor_scalar(NEG_LAM[:, l:l + 1], NEG_LAM[:, l:l + 1], -LAM_INIT[l], None, ALU.add))
                dve_chain(nc.vector.tensor_scalar(SUB_G[:, l:l + 1], vec("subln_g", l, 1), 1.0 - LAM_INIT[l], None, ALU.mult))

        def act_setup(act):
            act.wait_ge(tables, 1)
            act_chain(nc.scalar.activation(SIN, arena(SCR + 512, S1), ACT.Sin))
            act.wait_ge(tables, 2)
            act_chain(nc.scalar.activation(COS, arena(SCR + 768, S1), ACT.Sin))
            act.wait_ge(tables, 3)
            act_chain(nc.scalar.activation(SM[:, 8:12], SM[:, 0:4], ACT.Exp))
            act.sem_inc(stat_ready, 1)

        ROPE_PAIRS = [AQ, AQ + 2, AK, AK + 2, CQ, CQ + 2, CK, CK + 2]

        def act_shape(act, l):
            for at, n, func in ((AZ, 4, ACT.Silu), (BZ, 4, ACT.Silu), (CZ, 4, ACT.Silu),
                                (BU, 8, ACT.Gelu_apprx_tanh), (GL, 24, ACT.Sigmoid)):
                act_chain(nc.scalar.activation(PT[:, at:at + n], PT[:, at:at + n], func))
            for j, (dest, tile) in enumerate(((AVN, 0), (AVN, 1), (CVN, 0), (CVN, 1))):
                act.wait_ge(values_turned, 4 * l + j + 1)
                nc.scalar.activation(dest[:, tile], PS[:, j, 0:512], ACT.Copy).then_inc(values_taken, 1)
            load_log_exp(act)

        def pe_shape(pe, l):
            for j, at in enumerate(ROPE_PAIRS):
                nc.tensor.matmul(PS[:, j, 0:512], first("rope"), PT[:, at:at + 2], start=True, stop=True)\
                    .then_inc(permuted, 1)
            for j, (at, tile) in enumerate(((AV, 0), (AV, 1), (CV, 0), (CV, 1))):
                pe.wait_ge(rope_sin, 8 * l + j + 1)
                for c in range(4):
                    mm = nc.tensor.transpose(PS[:, j, c * P:(c + 1) * P], PT[:, at + c, tile * T1:(tile + 1) * T1], IDENT)
                mm.then_inc(values_turned, 1)

        def dve_shape(dve, l):
            part = arena(SCR, 8, 512)
            for j in range(8):
                dve.wait_ge(permuted, 8 * l + j + 1)
                nc.vector.tensor_tensor(part[:, j].rearrange("p (a b) -> p a b", a=2),
                                        PS[:, j, 0:512].rearrange("p (a b) -> p a b", a=2),
                                        SIN.unsqueeze(1).broadcast_to([P, 2, S1]), ALU.mult).then_inc(rope_sin, 1)
            for j, at in enumerate(ROPE_PAIRS):
                dve.wait_ge(rope_cos, 8 * l + j + 1)
                dve.wait_ge(rope_sin, 8 * l + j + 1)
                nc.vector.tensor_tensor(PT[:, at:at + 2].rearrange("p a b -> p (a b)"), PT[:, at:at + 2].rearrange("p a b -> p (a b)"),
                                        part[:, j], ALU.add).then_inc(roped, 1)

        def pool_shape(pool, l):
            for j, at in enumerate(ROPE_PAIRS):
                pool.wait_ge(permuted, 8 * l + j + 1)
                nc.gpsimd.tensor_tensor(PT[:, at:at + 2], PT[:, at:at + 2],
                                        COS.unsqueeze(1).broadcast_to([P, 2, S1]), ALU.mult).then_inc(rope_cos, 1)

        def act_diff_norm(act, l):
            act_chain(nc.scalar.activation(DIFF_RS, YS[:, 0:4], ACT.Square))
            act.sem_inc(stat_ready, 1)
            act.wait_ge(row_ready, 3 * l + 1)
            act_chain(nc.scalar.activation(DIFF_RS, DIFF_RS, ACT.Ln))
            act_chain(nc.scalar.activation(DIFF_RS, DIFF_RS, ACT.Exp, scale=-0.5))
            act.sem_inc(stat_ready, 1)

        def pe_diff_norm(pe, l):
            pe.wait_ge(stat_ready, 1 + 4 * l + 1)
            for h in range(4):
                mm = nc.tensor.matmul(PS[:, h // 2, (h % 2) * S1:(h % 2 + 1) * S1], ONES, DIFF_RS[:, h], start=True, stop=True)
            mm.then_inc(sum_ready, 1)

        def dve_diff_norm(dve, l):
            dve.wait_ge(sum_ready, 3 * l + 1)
            dve_chain(nc.vector.tensor_scalar(DIFF_RS.rearrange("p (a b) c -> p a (b c)", a=2), PS[:, 0:2, :],
                                              1.0 / 128, EPS, ALU.mult, ALU.add))
            dve.sem_inc(row_ready, 1)
            dve.wait_ge(stat_ready, 1 + 4 * l + 2)
            y = YS[:, 0:4].rearrange("p a b -> p (a b)")
            dve_chain(nc.vector.scalar_tensor_tensor(out=y, in0=y, scalar=SUB_G[:, l:l + 1],
                                                     in1=DIFF_RS.rearrange("p a b -> p (a b)"), op0=ALU.mult, op1=ALU.mult))
            dve_chain(nc.vector.tensor_tensor(y, y, PT[:, AZ:AZ + 4].rearrange("p a b -> p (a b)"), ALU.mult))
            y = YS[:, 8:12].rearrange("p a b -> p (a b)")
            dve_chain(nc.vector.tensor_tensor(y, y, PT[:, CZ:CZ + 4].rearrange("p a b -> p (a b)"), ALU.mult))

        B_SQ, B_MEAN, B_WC = arena(SCR + 2048, 4, S1), arena(SCR + 3072, 2, S1), arena(SCR + 3584, 4, P)
        B_V = PT[:, BV:BV + 4]

        def pe_sgu(pe, l):
            for k in range(4):
                mm = nc.tensor.matmul(PS[:, 4, 0:S1], ONES, B_V[:, k], start=(k == 0), stop=(k == 3))
            mm.then_inc(sum_ready, 1)
            pe.wait_ge(stat_ready, 1 + 4 * l + 3)
            for k in range(4):
                mm = nc.tensor.matmul(PS[:, 5, 0:S1], ONES, B_SQ[:, k], start=(k == 0), stop=(k == 3))
            mm.then_inc(sum_ready, 1)
            pe.wait_ge(norm_ready, 2 * l + 1)
            for tile in range(2):
                for c in range(4):
                    mm = nc.tensor.transpose(PS[:, 6 + tile, c * P:(c + 1) * P], B_V[:, c, tile * T1:(tile + 1) * T1], IDENT)
                mm.then_inc(mixed_ready, 1)
            pe.wait_ge(norm_ready, 2 * l + 2)
            for tile in range(2):
                pe.wait_ge(merged_in, 2 * l + tile + 1)
                for g in range(4):
                    mm = nc.tensor.matmul(PS[:, 2 + tile, g * P:(g + 1) * P], BVN[:, tile, g * P:(g + 1) * P],
                                          B_WC[:, g], start=True, stop=True)
                mm.then_inc(mixed_ready, 1)

        def act_sgu(act, l):
            act.wait_ge(row_ready, 3 * l + 2)
            act_chain(nc.scalar.activation(B_SQ, B_V, ACT.Square))
            act.sem_inc(stat_ready, 1)
            act.wait_ge(row_ready, 3 * l + 3)
            act_chain(nc.scalar.activation(B_MEAN[:, 1], B_MEAN[:, 1], ACT.Ln))
            act_chain(nc.scalar.activation(B_MEAN[:, 1], B_MEAN[:, 1], ACT.Exp, scale=-0.5))
            act.sem_inc(stat_ready, 1)
            for tile in range(2):
                act.wait_ge(mixed_ready, 4 * l + tile + 1)
                nc.scalar.activation(BVN[:, tile], PS[:, 6 + tile, 0:512], ACT.Copy).then_inc(merged_in, 1)

        def dve_sgu(dve, l):
            dve.wait_ge(sum_ready, 3 * l + 2)
            dve_chain(nc.vector.tensor_scalar(B_MEAN[:, 0], PS[:, 4, 0:S1], 1.0 / 512, None, ALU.mult))
            dve_chain(nc.vector.tensor_tensor(B_V, B_V, B_MEAN[:, 0:1].broadcast_to([P, 4, S1]), ALU.subtract))
            dve.sem_inc(row_ready, 1)
            dve_chain(nc.vector.tensor_tensor(B_WC, first("sgu_w")[:, l * 512:(l + 1) * 512].rearrange("p (a b) -> p a b", a=4),
                                              first("causal_w").unsqueeze(1).broadcast_to([P, 4, P]), ALU.mult))
            dve.wait_ge(sum_ready, 3 * l + 3)
            dve_chain(nc.vector.tensor_scalar(B_MEAN[:, 1], PS[:, 5, 0:S1], 1.0 / 512, EPS, ALU.mult, ALU.add))
            dve.sem_inc(row_ready, 1)
            dve.wait_ge(stat_ready, 1 + 4 * l + 4)
            dve_chain(nc.vector.tensor_tensor(B_V, B_V, B_MEAN[:, 1:2].broadcast_to([P, 4, S1]), ALU.mult))
            for k in range(4):
                dve_chain.later(nc.vector.tensor_scalar(B_V[:, k], B_V[:, k], vec("ln_g", 4 * l + k, 1), vec("ln_b", 4 * l + k, 1),
                                                        ALU.mult, ALU.add))
            dve_chain.settle()
            dve.sem_inc(norm_ready, 2)
            bias = first("sgu_b")[:, l * 512:(l + 1) * 512].rearrange("p (a b) -> p a b", a=4)
            y = YS[:, 4:8]
            for tile in range(2):
                dve.wait_ge(mixed_ready, 4 * l + 3 + tile)
                ts = slice(tile * T1, (tile + 1) * T1)
                dve_chain(nc.vector.tensor_tensor(y[:, :, ts], PS[:, 2 + tile, :].rearrange("p (a b) -> p a b", a=4),
                                                  bias, ALU.add))
            y = y.rearrange("p a b -> p (a b)")
            dve_chain(nc.vector.tensor_tensor(y, y, PT[:, BU:BU + 4].rearrange("p a b -> p (a b)"), ALU.mult))
            dve_chain(nc.vector.tensor_tensor(y, y, PT[:, BZ:BZ + 4].rearrange("p a b -> p (a b)"), ALU.mult))

        def pe_merge(pe, l):
            block, _ = BLOCKS["w_branch", l]
            pe.wait_ge(branch_parts, 2 * l + 2)
            for j in range(12):
                pe_arrived(pe, block + j)
                if j >= 4:
                    pe.wait_ge(merged_part, 12 * l + j - 3)
                for c in range(2):
                    for k in range(4):
                        y = 4 * (j % 3) + k
                        mm = pe_tile(PS[:, j % 4, c * S1:(c + 1) * S1], block + j, c * 4 + k, YS_H[:, y], YS_L[:, y],
                                     k == 0, k == 3)
                mm.then_inc(blocks_done, 1)

        def act_branch_parts(act, l):
            act.wait_ge(branches_ready, l + 1)
            nc.scalar.activation(YS_H[:, :, :], YS, ACT.Copy).then_inc(branch_parts, 1)

        def dve_branch_parts(dve, l):
            dve.sem_inc(branches_ready, 1)
            dve.wait_ge(branch_parts, 2 * l + 1)
            nc.vector.tensor_tensor(YS_L[:, :, :], YS, YS_H[:, :, :].bitcast(F32), ALU.subtract).then_inc(branch_parts, 1)

        def act_merge(act, l):
            block, _ = BLOCKS["w_branch", l]
            for j in range(12):
                act_split(act, block + j + SPLIT)
                if j % 3 == 2:
                    act.wait_ge(merged_ready, KC * l + 2 * (j // 3) + 2)
                    for k in (2 * (j // 3), 2 * (j // 3) + 1):
                        nc.scalar.activation(H1_H[:, k], H[:, k, 0:S1], ACT.Copy).then_inc(act_high, 1)

        def dve_merge(dve, l):
            block, _ = BLOCKS["w_branch", l]
            product = arena(SCR, 2, 512)
            for j in range(12):
                dve_split(dve, block + j + SPLIT)
                dve.wait_ge(blocks_done, block + j + 1)
                pair, n = divmod(j, 3)
                gate = PT[:, GL + 8 * n + 2 * pair:GL + 8 * n + 2 * pair + 2]
                dest = H[:, 2 * pair:2 * pair + 2, 0:S1]
                psum = PS[:, j % 4, :].rearrange("p (a b) -> p a b", a=2)
                to = dest if n == 0 else product[:, n - 1].rearrange("p (a b) -> p a b", a=2)
                nc.vector.tensor_tensor(to, psum, gate, ALU.mult).then_inc(merged_part, 1)
                dve.wait_ge(merged_part, 12 * l + j + 1)
                if n:
                    dve_chain(nc.vector.tensor_tensor(dest, dest, to, ALU.add))
                if n == 2:
                    dve.sem_inc(merged_ready, 2)
            dve_parts(dve, ("w_out", l), H[:, :, 0:S1], H1_H, H1_L)

        inner_high, inner_low = sem("inner_high_ready"), sem("inner_low_ready")

        def pe_ffn(pe, use, l, f):
            block, _ = BLOCKS[f"ffn_in{f}", l]
            with pe.Fori(0, FF_CH // 2) as g:
                for u in range(4):
                    pe_arrived(pe, block + u, g)
                    pe.wait_ge(ups_taken if u % 2 else gates_taken, g * 2 + FF_CH * use + u // 2 + 1)
                    for k in range(KC):
                        if u == 0:
                            pe.wait_ge(act_low, KC * JOBS["ffn", use] + k + 1)
                        mm = pe_tile(PS[:, u, 0:S2], block + u, k, H2_H[:, k], H2_L[:, k], k == 0, k == KC - 1)
                    mm.then_inc(blocks_done, 1)
            pe.wait_ge(inner_low, FF_CH * (use + 1) - 2)
            block, _ = BLOCKS[f"ffn_out{f}", l]

            def rows(n, k, g=None, first=False, last=False):
                pe_arrived(pe, n, g)
                for m in (4, 5, 6, 7, 0, 1, 2, 3):
                    if first and m in (0, 2):
                        pe.wait_ge(ups_taken, FF_CH * (use + 1) + 1 + m // 2)
                    mm = pe_tile(PS[:, m, 0:S2], n, m, F_H[:, k], F_L[:, k], first, last)
                mm.then_inc(blocks_done, 1)

            for u in range(4):
                rows(block + u, u, first=(u == 0))
            with pe.Fori(0, 4) as g:
                for u in range(4):
                    rows(block + 4 + u, g * 4 + (4 + u), g)
            pe.wait_ge(inner_low, FF_CH * (use + 1))
            for u in range(20, 22):
                rows(block + u, u, last=(u == 21))

        def act_ffn(act, use, l, f):
            block, _ = BLOCKS[f"ffn_in{f}", l]
            act.preload_act_table(ACT.Silu)
            with act.Fori(0, FF_CH // 2) as g:
                for u in range(2):
                    act_split(act, block + 2 * u + SPLIT, g)
                    act.wait_ge(ups_taken, g * 2 + FF_CH * use + u + 1)
                    act.wait_ge(blocks_done, g * 4 + block + 2 * u + 1)
                    nc.scalar.activation(FFN_GATE[:, u], PS[:, 2 * u, 0:S2], ACT.Silu).then_inc(gates_taken, 1)
                    act_split(act, block + 2 * u + 1 + SPLIT, g)
                    act.wait_ge(ups_taken, g * 2 + FF_CH * use + u + 3)
                    act.wait_ge(blocks_done, 1)
                    nc.scalar.activation(F_H[:, g * 2 + u], FFN_PROD[:, u], ACT.Copy).then_inc(inner_high, 1)
            load_log_exp(act)
            split_ahead(act, act_split, *BLOCKS[f"ffn_out{f}", l])

        def dve_ffn(dve, use, l, f):
            block, _ = BLOCKS[f"ffn_in{f}", l]
            with dve.Fori(0, FF_CH // 2) as g:
                for u in range(2):
                    dve_split(dve, block + 2 * u + SPLIT, g)
                    dve.wait_ge(gates_taken, g * 2 + FF_CH * use + u + 3)
                    dve.wait_ge(blocks_done, g * 4 + block + 2 * u + 2)
                    nc.vector.tensor_tensor(FFN_PROD[:, u], FFN_GATE[:, u], PS[:, 2 * u + 1, 0:S2], ALU.mult)\
                        .then_inc(ups_taken, 1)
                    dve_split(dve, block + 2 * u + 1 + SPLIT, g)
                    dve.wait_ge(inner_high, g * 2 + FF_CH * use + u + 1)
                    nc.vector.tensor_tensor(F_L[:, g * 2 + u], FFN_PROD[:, u], F_H[:, g * 2 + u].bitcast(F32), ALU.subtract)\
                        .then_inc(inner_low, 1)
            block, count = BLOCKS[f"ffn_out{f}", l]
            split_ahead(dve, dve_split, block, count)
            dve.wait_ge(blocks_done, block + count)
            for m in range(KC):
                nc.vector.scalar_tensor_tensor(out=X[:, m], in0=PS[:, m, 0:S2], scalar=0.5, in1=X[:, m],
                                               op0=ALU.mult, op1=ALU.add).then_inc(residual_ready, 1)
        ROUNDS = [len(LEVELS)] + [sum(2 * b <= w for b in LEVELS) for w in WIDTHS]
        FIRST_TURN = [4 * (sum(ROUNDS[:u]) + u) for u in range(len(ROUNDS))]
        FIRST_ROUND = [4 * sum(ROUNDS[:u]) for u in range(len(ROUNDS))]
        inv = {k: sem("inverse_" + k) for k in ("y_ready", "y_taken", "xy_ready", "x_new", "turned", "turned_taken")}

        def span(c):
            return slice(c * TC, c * TC + WIDTHS[c])

        def half(odd):
            return slice(odd * TC, odd * TC + TC)

        def firsts(v, b):
            return v.rearrange("p m (k two b) -> p m k two b", two=2, b=b)[:, :, :, 0]

        def halves(bank, n):
            return PS[:, bank, 0:n * TC].rearrange("p (a b) -> p a b", a=n)

        def wholes(bank, n):
            return PS[:, bank, 0:n * P].rearrange("p (a b) -> p a b", a=n)

        def by_parity(v):
            return v.rearrange("p (q o) t -> p o q t", o=2)

        def pe_inverse(pe, use, B):
            U, X_, XT, Y = B["U"], B["X"], B["XT"], B["Y"]
            turn, first_round = FIRST_TURN[use], FIRST_ROUND[use]
            for g, (m0, n) in enumerate(B["groups"]):
                for j in range(n):
                    mm = nc.tensor.transpose(wholes(4 + g, n)[:, j], XT[:, m0 + j], IDENT)
                mm.then_inc(inv["turned"], 1)
            for i in range(ROUNDS[use] + 1):
                for g, (m0, n) in enumerate(B["groups"]):
                    if i == ROUNDS[use]:
                        break
                    if i == 0:
                        pe.wait_ge(inv["turned_taken"], turn + g + 1)
                    else:
                        pe.wait_ge(inv["x_new"], first_round + 4 * (i - 1) + g + 1)
                    for j in range(n):
                        mm = nc.tensor.matmul(wholes(g, n)[:, j], U[:, m0 + j], X_[:, m0 + j], start=True, stop=True)
                    mm.then_inc(inv["y_ready"], 1)
                for g, (m0, n) in enumerate(B["groups"]):
                    if i == 0:
                        break
                    pe.wait_ge(inv["x_new"], first_round + 4 * (i - 1) + g + 1)
                    pe.wait_ge(inv["turned_taken"], turn + 4 * (i - 1) + g + 1)
                    for j in range(n):
                        mm = nc.tensor.transpose(wholes(4 + g, n)[:, j], X_[:, m0 + j], IDENT)
                    mm.then_inc(inv["turned"], 1)
                for g, (m0, n) in enumerate(B["groups"]):
                    if i == ROUNDS[use]:
                        break
                    pe.wait_ge(inv["y_taken"], first_round + 4 * i + g + 1)
                    pe.wait_ge(inv["turned_taken"], turn + 4 * i + g + 1)
                    for j in range(n):
                        mm = nc.tensor.matmul(wholes(g, n)[:, j], XT[:, m0 + j], Y[:, m0 + j], start=True, stop=True)
                    mm.then_inc(inv["xy_ready"], 1)

        def act_inverse(act, use, B):
            for i in range(ROUNDS[use] + 1):
                for g, (m0, n) in enumerate(B["groups"]):
                    act.wait_ge(inv["turned"], FIRST_TURN[use] + 4 * i + g + 1)
                    nc.scalar.activation((B["XT"] if i else B["X"])[:, m0:m0 + n], wholes(4 + g, n), ACT.Copy)\
                        .then_inc(inv["turned_taken"], 1)

        def dve_inverse(dve, use, B):
            X_, Y = B["X"], B["Y"]
            for i in range(ROUNDS[use]):
                base, b = FIRST_ROUND[use] + 4 * i, LEVELS[i]
                for g, (m0, n) in enumerate(B["groups"]):
                    dve.wait_ge(inv["y_ready"], base + g + 1)
                    mask = const("partners")[:, i * P:(i + 1) * P].unsqueeze(1).broadcast_to([P, n, P])
                    nc.vector.tensor_tensor(Y[:, m0:m0 + n], wholes(g, n), mask, ALU.mult).then_inc(inv["y_taken"], 1)
                for g, (m0, n) in enumerate(B["groups"]):
                    dve.wait_ge(inv["xy_ready"], base + g + 1)
                    if i:
                        dve.wait_ge(inv["x_new"], base - 4 + g + 1)
                    x = firsts(X_[:, m0:m0 + n], b)
                    nc.vector.tensor_tensor(x, x, firsts(wholes(g, n), b), ALU.subtract)\
                        .then_inc(inv["x_new"], 1)

        def dve_first_level(B, n):
            dve_chain(nc.vector.tensor_tensor(B["XT"], B["U"], const("pairs").unsqueeze(1).broadcast_to([P, n, P]), ALU.mult))
            dve_chain(nc.vector.tensor_tensor(B["XT"], IDENT.unsqueeze(1).broadcast_to([P, n, P]), B["XT"], ALU.subtract))

        HP = arena(0, HYB_CH, S2)
        CO = arena(7616, 12, S2)
        FVN = AR[0:T2, 10880:12928].rearrange("p (a b) -> p a b", a=4)
        ROWS = arena(12928, 6, S2)
        FA, FB, GA, GB = (arena(14560 + 1088 * j, 4, S2) for j in range(4))
        BR = arena(18912, 4, S2)
        BETA_B, GC_B, EGC = (arena(20000 + 1088 * j, 4, S2) for j in range(3))
        KBT, KBET, QD, KDT = (arena(23264 + 1088 * j, 4, S2) for j in range(4))
        FOX = place_attention(Attn("F", 0), 27616)
        Y8 = arena(31840, 8, S2)
        GP = 2 * len(WIDTHS)
        GI = {"U": arena(0, GP, P), "X": arena(1280, GP, P), "XT": arena(2560, GP, P), "Y": arena(3840, GP, P),
              "groups": [(0, 3), (3, 3), (6, 2), (8, 2)]}
        ATT, DEC = arena(5120, GP, TC), arena(34016, GP, TC)
        VBN, KBEN, KDN = (arena(at, GP, P) for at in (10880, 14560, 20000))
        WT = arena(34016, 2 * GP, TC)
        UN = arena(35296, 2, P)
        GS = [arena(36128, 4, P), arena(35552, 4, P)]
        MIX_H, MIX_L = parts("mixer", 23264, KC, S2)
        DK = 128

        hs = {k: sem("hybrid_" + k) for k in (
            "small_ready", "z_ready", "rows_ready", "one_plus", "log_ready", "sigmoid_ready", "cleared", "values_turned",
            "fox_bound", "bound", "l2_ready", "l2_mean", "l2_root", "spread", "spread_taken", "prep", "grams", "decay",
            "decay_exp", "gram_taken", "turned", "turned_taken", "w_ready", "w_taken", "u_ready", "u_taken", "o_ready",
            "o_taken", "s_ready", "s_taken", "gate", "onorm", "osum", "omean", "oroot", "outputs")}

        def pe_hybrid_in(pe):
            small = vec("hyb_small").rearrange("p (k c) -> p k c", k=KC)
            for k in range(KC):
                mm = nc.tensor.matmul(PS[0:T2, 5, 0:S2], small[:, k], H[:, k], start=(k == 0), stop=(k == KC - 1))
            mm.then_inc(hs["small_ready"], 1)

        def dve_hybrid_rows(dve):
            z, t, sp, c, nc_ = (ROWS[0:36, j] for j in range(5))
            dve.wait_ge(hs["small_ready"], 1)
            dve_chain(nc.vector.tensor_scalar(z, PS[0:36, 5, 0:S2], vec("gate_b", 0, 1, 36), const("gate_sign", 36), ALU.add, ALU.mult))
            dve.sem_inc(hs["z_ready"], 1)
            dve.wait_ge(hs["one_plus"], 1)
            dve_chain(nc.vector.tensor_scalar(t, t, 1.0, None, ALU.add))
            dve_chain(nc.vector.tensor_scalar(SM[0:36, 1:2], SM[0:36, 0:1], -1.0, None, ALU.mult))
            dve.sem_inc(hs["z_ready"], 1)
            dve.wait_ge(hs["log_ready"], 1)
            dve_chain(nc.vector.scalar_tensor_tensor(out=sp, in0=z, scalar=0.0, in1=t, op0=ALU.max, op1=ALU.add))
            dve_chain(nc.vector.tensor_scalar(sp, sp, SM[0:36, 1:2], None, ALU.mult))
            dve_chain(nc.vector.tensor_tensor_scan(ROWS[0:8, 3], const("row_one", 8), ROWS[0:8, 2], 0.0, ALU.mult, ALU.add))
            dve_chain(nc.vector.tensor_tensor_scan(ROWS[32:36, 3], C[32:36, CONST["restart"][0]:CONST["restart"][0] + S2],
                                                   ROWS[32:36, 2], 0.0, ALU.mult, ALU.add))
            dve_chain(nc.vector.tensor_scalar(ROWS[0:8, 3], ROWS[0:8, 3], 8.0, None, ALU.mult))
            dve_chain(nc.vector.tensor_scalar(ROWS[0:8, 4], ROWS[0:8, 3], -1.0, None, ALU.mult))
            dve_chain(nc.vector.tensor_scalar(ROWS[32:36, 4], ROWS[32:36, 3], -1.0, None, ALU.mult))
            dve.sem_inc(hs["rows_ready"], 1)

        def dve_convolution(dve, share):
            dve_chain.settle()
            each = 4 * 12 // F_HEADS
            for back, j in [divmod(i, 12) for i in range(share * each, (share + 1) * each)]:
                tap = vec("conv", 4 * j + 3 - back, 1)
                if back == 0:
                    dve_chain.later(nc.vector.tensor_scalar(CO[:, j], HP[:, GQ + j], tap, None, ALU.mult))
                else:
                    dve_chain.later(nc.vector.scalar_tensor_tensor(
                        out=CO[:, j, back:], in0=HP[:, GQ + j, 0:S2 - back], scalar=tap, in1=CO[:, j, back:],
                        op0=ALU.mult, op1=ALU.add))

        def act_hybrid_rows(act):
            act.wait_ge(hs["z_ready"], 1)
            act_chain(nc.scalar.activation(ROWS[0:36, 1], ROWS[0:36, 0], ACT.Abs))
            act_chain(nc.scalar.activation(ROWS[0:36, 1], ROWS[0:36, 1], ACT.Exp, scale=-1.0))
            act_chain(nc.scalar.activation(SM[0:36, 0:1], vec("gate_b", 1, 1, 36), ACT.Exp))
            act.sem_inc(hs["one_plus"], 1)
            act.wait_ge(hs["z_ready"], 2)
            act_chain(nc.scalar.activation(ROWS[0:36, 1], ROWS[0:36, 1], ACT.Ln))
            act.sem_inc(hs["log_ready"], 1)
            act_chain(nc.scalar.activation(ROWS[64:68, 0], PS[64:68, 5, 0:S2], ACT.Sigmoid))
            act.sem_inc(hs["sigmoid_ready"], 1)
            for c in range(4):
                act.wait_ge(hs["values_turned"], c + 1)
                act_chain(nc.scalar.activation(FVN[:, c], PS[0:T2, c, 0:512], ACT.Copy))
            load_log_exp(act)

        def pool_hybrid_rows(pool):
            for j, v in enumerate((FA, FB, GA, GB)):
                nc.gpsimd.memset(v, 0.0).then_inc(hs["cleared"], 1)
            pool.wait_ge(hs["cleared"], 4)
            for j, (v, p) in enumerate(((FA, 32), (FA, 96), (FB, 0), (FB, 64), (GA, 32), (GB, 0))):
                nc.gpsimd.memset(v[p:p + 1], 1.0).then_inc(hs["cleared"], 1)

        def sp_hybrid_rows(sp):
            sp.wait_ge(hs["cleared"], 10)
            sp.wait_ge(hs["rows_ready"], 1)
            sp.wait_ge(hs["sigmoid_ready"], 1)
            for h in range(F_HEADS):
                p = 64 * (h % 2)
                sp.dma_start(FA[p:p + 1, h // 2], ROWS[h:h + 1, 3]).then_inc(hs["fox_bound"], 16)
                sp.dma_start(FB[p + 32:p + 33, h // 2], ROWS[h:h + 1, 4]).then_inc(hs["fox_bound"], 16)
            for h in range(G_HEADS):
                sp.dma_start(GA[0:1, h], ROWS[32 + h:33 + h, 3]).then_inc(hs["bound"], 16)
                sp.dma_start(GB[32:33, h], ROWS[32 + h:33 + h, 4]).then_inc(hs["bound"], 16)
                sp.dma_start(BR[0:1, h], ROWS[64 + h:65 + h, 0]).then_inc(hs["bound"], 16)

        FOX_ROW_DMAS, ROW_DMAS = 2 * F_HEADS, 3 * G_HEADS

        def pe_fox_values(pe):
            for c in range(4):
                for j in range(4):
                    mm = nc.tensor.transpose(PS[0:T2, c, j * P:(j + 1) * P], HP[:, FV + j, c * T2:(c + 1) * T2], IDENT)
                mm.then_inc(hs["values_turned"], 1)

        def act_delta_prep(act):
            act_chain(nc.scalar.activation(CO, CO, ACT.Silu))
            act_chain(nc.scalar.activation(SQ[:, :, :], CO[:, 0:8], ACT.Square))
            act.sem_inc(hs["l2_ready"], 1)
            act_chain(nc.scalar.activation(HP[:, GZ:GZ + 4], HP[:, GZ:GZ + 4], ACT.Silu))
            load_log_exp(act)
            act.wait_ge(hs["l2_mean"], 1)
            act_chain(nc.scalar.activation(H[:, :, :], H[:, :, :], ACT.Ln))
            act_chain(nc.scalar.activation(H[:, :, :], H[:, :, :], ACT.Exp, scale=-0.5))
            act.sem_inc(hs["l2_root"], 1)
            act.wait_ge(hs["spread"], 8)
            act_chain(nc.scalar.activation(GC_B, PS[:, 0:4, 0:S2], ACT.Copy))
            act_chain(nc.scalar.activation(EGC, PS[:, 0:4, 0:S2], ACT.Exp))
            act_chain(nc.scalar.activation(BETA_B, PS[:, 4:8, 0:S2], ACT.Copy))
            act.sem_inc(hs["spread_taken"], 1)
            act.wait_ge(hs["prep"], 1)
            act_chain(nc.scalar.activation(KDT, KDT, ACT.Exp))
            act.sem_inc(hs["spread_taken"], 1)

        def pe_delta_prep(pe):
            pe.wait_ge(hs["l2_ready"], 1)
            for j in range(8):
                mm = nc.tensor.matmul(PS[:, j, 0:S2], ONES, SQ[:, j], start=True, stop=True)
            mm.then_inc(hs["l2_ready"], 1)
            pe.wait_ge(hs["l2_mean"], 1)
            pe.wait_ge(hs["bound"], 16 * ROW_DMAS)
            for j in range(8):
                row = GA[0:1, j] if j < 4 else BR[0:1, j - 4]
                nc.tensor.matmul(PS[:, j, 0:S2], ONES[0:1, :], row, start=True, stop=True).then_inc(hs["spread"], 1)

        def dve_delta_prep(dve):
            dve.wait_ge(hs["l2_ready"], 2)
            dve_chain(nc.vector.tensor_scalar(H[:, :, :], PS[:, :, 0:S2], EPS, None, ALU.add))
            dve.sem_inc(hs["l2_mean"], 1)
            dve.wait_ge(hs["l2_root"], 1)
            q, k, v = CO[:, 0:4], CO[:, 4:8], CO[:, 8:12]
            flat = lambda a: a.rearrange("p a b -> p (a b)")
            dve_chain(nc.vector.scalar_tensor_tensor(out=flat(q), in0=flat(q), scalar=DK ** -0.5, in1=flat(H[:, 0:4]),
                                                     op0=ALU.mult, op1=ALU.mult))
            dve_chain(nc.vector.tensor_tensor(k, k, H[:, 4:8], ALU.mult))
            dve.wait_ge(hs["spread_taken"], 1)
            for c, w in enumerate(WIDTHS):
                t = span(c)
                dve_chain(nc.vector.tensor_tensor(KDT[:, :, t], GC_B[:, :, t.stop - 1:t.stop].broadcast_to([P, 4, w]), GC_B[:, :, t],
                                                  ALU.subtract))
            dve.sem_inc(hs["prep"], 1)
            dve_chain(nc.vector.tensor_tensor(KBT, k, BETA_B, ALU.mult))
            dve_chain(nc.vector.tensor_tensor(KBET, KBT, EGC, ALU.mult))
            dve_chain(nc.vector.tensor_tensor(QD, q, EGC, ALU.mult))
            dve_chain(nc.vector.tensor_tensor(v, v, BETA_B, ALU.mult))
            dve.wait_ge(hs["spread_taken"], 2)
            dve_chain(nc.vector.tensor_tensor(KDT, KDT, k, ALU.mult))

        def gram(c):
            return PS[:, c, 0:6 * TC].rearrange("p (m q t) -> p m q t", m=3, q=2)

        def pe_delta_grams(pe):
            for c, w in enumerate(WIDTHS):
                cols = span(c)
                for h in range(4):
                    q, o = divmod(h, 2)
                    out_ = gram(c)[o * TC:o * TC + w]
                    nc.tensor.matmul(out_[:, 0, q, 0:w], CO[:, 4 + h, cols], KBT[:, h, cols], start=True, stop=True)
                    nc.tensor.matmul(out_[:, 1, q, 0:w], CO[:, 4 + h, cols], CO[:, h, cols], start=True, stop=True)
                    mm = nc.tensor.matmul(out_[:, 2, q, 0:w], GB[0:33, h, cols], GA[0:33, h, cols], start=True, stop=True)
                mm.then_inc(hs["grams"], 1)
            for j in range(3 * len(WIDTHS)):
                src, c = (CO[:, 8:12], KBET, KDT)[j % 3], j // 3
                if j >= 3:
                    pe.wait_ge(hs["turned_taken"], j - 2)
                for h in range(4):
                    mm = nc.tensor.transpose(PS[0:WIDTHS[c], 5 + j % 3, h * P:(h + 1) * P], src[:, h, span(c)], IDENT)
                mm.then_inc(hs["turned"], 1)

        def act_delta_grams(act):
            for c, w in enumerate(WIDTHS):
                act.wait_ge(hs["decay"], c + 1)
                d = DEC[:, 2 * c:2 * c + 2, 0:w]
                nc.scalar.activation(d, d, ACT.Exp).then_inc(hs["decay_exp"], 1)
            for j in range(3 * len(WIDTHS)):
                act.wait_ge(hs["turned"], j + 1)
                dest = (VBN, KBEN, KDN)[j % 3][:, 2 * (j // 3):2 * (j // 3) + 2]
                for o in range(2):
                    step = nc.scalar.activation(dest[half(o)], by_parity(wholes(5 + j % 3, 4))[half(0), o], ACT.Copy)
                step.then_inc(hs["turned_taken"], 1)

        def dve_delta_grams(dve):
            dve_chain(nc.vector.memset(GI["U"][:, GP - 2:GP], 0.0))
            u4 = GI["U"].rearrange("p m (two t) -> p m two t", two=2)
            for c, w in enumerate(WIDTHS):
                s = slice(2 * c, 2 * c + 2)
                dve.wait_ge(hs["grams"], c + 1)
                nc.vector.tensor_tensor(DEC[:, s, 0:w], gram(c)[:, 2, :, 0:w], const("neg_tri")[:, 0:w].unsqueeze(1).broadcast_to([P, 2, w]),
                                        ALU.add).then_inc(hs["decay"], 1)
            for c, w in enumerate(WIDTHS):
                s = slice(2 * c, 2 * c + 2)
                dve.wait_ge(hs["decay_exp"], c + 1)
                nc.vector.tensor_tensor(ATT[:, s, 0:w], gram(c)[:, 1, :, 0:w], DEC[:, s, 0:w], ALU.mult)
                dve_chain(nc.vector.tensor_tensor(DEC[:, s, 0:w], gram(c)[:, 0, :, 0:w], DEC[:, s, 0:w], ALU.mult))
                tri = const("tri_pair").rearrange("p (two t) -> p two t", two=2)
                dve_chain(nc.vector.tensor_tensor(u4[:, s, :, 0:w], DEC[:, s, 0:w].unsqueeze(2).broadcast_to([P, 2, 2, w]),
                                                  tri[:, :, 0:w].unsqueeze(1).broadcast_to([P, 2, 2, w]), ALU.mult))
            dve_first_level(GI, GP)

        def two_banks(bank, n):
            return PS[:, bank:bank + 2, 0:2 * n].rearrange("p o (q t) -> p o q t", q=2)

        def pe_delta_scan(pe):
            XT = GI["XT"]
            for c, w in enumerate(WIDTHS):
                if c >= 4:
                    pe.wait_ge(hs["w_taken"], c - 3)
                for h in range(4):
                    q, o = divmod(h, 2)
                    mm = nc.tensor.matmul(two_banks(2 * (c % 4), TC)[:, o, q, 0:w], KBEN[half(o), 2 * c + q], XT[half(o), 2 * c + q, o * TC:o * TC + w],
                                          start=True, stop=True)
                mm.then_inc(hs["w_ready"], 1)
            for c, w in enumerate(WIDTHS):
                if c == 0:
                    pe.wait_ge(hs["w_taken"], len(WIDTHS))
                if c:
                    pe.wait_ge(hs["s_taken"], c)
                for q in range(2):
                    for o in range(2):
                        out_, rows = PS[o * TC:o * TC + w, 5, q * P:(q + 1) * P], slice(o * TC, o * TC + w)
                        if c:
                            nc.tensor.matmul(out_, WT[:, 4 * c + 2 * q + o, 0:w], GS[c % 2][:, 2 * q + o], start=True, stop=False)
                        mm = nc.tensor.matmul(out_, XT[:, 2 * c + q, rows], VBN[:, 2 * c + q], start=(c == 0), stop=True)
                mm.then_inc(hs["u_ready"], 1)
                pe.wait_ge(hs["u_taken"], c + 1)
                for h in range(4):
                    if c == len(WIDTHS) - 1:
                        break
                    q, o = divmod(h, 2)
                    mm = nc.tensor.matmul(two_banks(6, P)[:, o, q], KDN[half(o), 2 * c + q], UN[half(o), q], start=True, stop=True)
                    if h == 3:
                        mm.then_inc(hs["s_ready"], 1)
                if c:
                    pe.wait_ge(hs["o_taken"], c)
                for h in range(4):
                    q, o = divmod(h, 2)
                    out_ = two_banks(3, TC)[:, o, q, 0:w]
                    if c:
                        nc.tensor.matmul(out_, GS[c % 2][:, h], QD[:, h, span(c)], start=True, stop=False)
                    mm = nc.tensor.matmul(out_, UN[half(o), q], ATT[half(o), 2 * c + q, 0:w], start=(c == 0), stop=True)
                mm.then_inc(hs["o_ready"], 1)

        def act_delta_scan(act):
            for c, w in enumerate(WIDTHS):
                act.wait_ge(hs["w_ready"], c + 1)
                nc.scalar.activation(by_parity(WT[:, 4 * c:4 * c + 4, 0:w]), two_banks(2 * (c % 4), TC)[:, :, :, 0:w], ACT.Copy, scale=-1.0).then_inc(hs["w_taken"], 1)
            for c, w in enumerate(WIDTHS):
                act.wait_ge(hs["o_ready"], c + 1)
                nc.scalar.activation(by_parity(Y8[:, 4:8, span(c)]), two_banks(3, TC)[:, :, :, 0:w], ACT.Copy).then_inc(hs["o_taken"], 1)

        def dve_delta_scan(dve):
            for c in range(len(WIDTHS)):
                dve.wait_ge(hs["u_ready"], c + 1)
                if c:
                    dve.wait_ge(hs["o_ready"], c)
                nc.vector.tensor_copy(UN, wholes(5, 2)).then_inc(hs["u_taken"], 1)
                if c == len(WIDTHS) - 1:
                    break
                new, end = GS[(c + 1) % 2], span(c).stop
                if c:
                    dve_chain(nc.vector.tensor_tensor(new, GS[c % 2], EGC[:, :, end - 1:end].broadcast_to([P, 4, P]), ALU.mult))
                dve.wait_ge(hs["s_ready"], c + 1)
                if c:
                    step = nc.vector.tensor_tensor(by_parity(new), by_parity(new), two_banks(6, P), ALU.add)
                else:
                    step = nc.vector.tensor_copy(by_parity(new), two_banks(6, P))
                step.then_inc(hs["s_taken"], 1)
                dve.wait_ge(hs["s_taken"], c + 1)

        def act_delta_out(act):
            act_chain(nc.scalar.activation(SQ[:, 0:4], Y8[:, 4:8], ACT.Square))
            act.sem_inc(hs["onorm"], 1)
            act.wait_ge(hs["omean"], 1)
            act_chain(nc.scalar.activation(SQ[:, 4:8], SQ[:, 4:8], ACT.Ln))
            act_chain(nc.scalar.activation(SQ[:, 4:8], SQ[:, 4:8], ACT.Exp, scale=-0.5))
            act.sem_inc(hs["oroot"], 1)

        def pe_delta_out(pe):
            pe.wait_ge(hs["onorm"], 1)
            for h in range(4):
                mm = nc.tensor.matmul(PS[:, 4 + h, 0:S2], ONES, SQ[:, h], start=True, stop=True)
            mm.then_inc(hs["osum"], 1)

        def dve_delta_out(dve):
            dve.wait_ge(hs["osum"], 1)
            dve_chain(nc.vector.tensor_scalar(SQ[:, 4:8], PS[:, 4:8, 0:S2], 1.0 / 128, EPS, ALU.mult, ALU.add))
            dve.sem_inc(hs["omean"], 1)
            dve.wait_ge(hs["oroot"], 1)
            flat = lambda a: a.rearrange("p a b -> p (a b)")
            y = flat(Y8[:, 4:8])
            dve_chain(nc.vector.scalar_tensor_tensor(out=y, in0=y, scalar=vec("o_gain"), in1=flat(SQ[:, 4:8]), op0=ALU.mult, op1=ALU.mult))
            dve_chain(nc.vector.tensor_tensor(y, y, flat(HP[:, GZ:GZ + 4]), ALU.mult))
            dve.sem_inc(hs["outputs"], KC)
        LI, LO = arena(0, KC, 288), arena(2304, 4, D)
        XV = [arena(6528 + 2176 * j, KC, S2) for j in range(3)]
        R_, K_, V_ = (arena(13056 + 2176 * j, KC, S2) for j in range(3))
        RKV = arena(13056, 24, S2)
        LD, A_, G_, KK, B_, AC = (arena(19584 + 2176 * j, KC, S2) for j in range(6))
        BONUS = A_
        KKT, RT, BT, KT, BH, KH = (arena(2176 * j, KC, S2) for j in range(6))
        KKT_RT = arena(0, 2, KC, S2)
        LT = arena(34624, 4, S2)
        G3 = [AR[:, at:at + KC * 3 * TC].rearrange("p (k m t) -> p k m t", k=KC, m=3) for at in (27136, 28672)]
        BHN, KHN, VN = ([arena(at + 512 * j, KC, TC) for at in (30464, 19584)] for j in range(3))
        RI = [{"U": arena(at, KC, P), "X": arena(13056, KC, P), "XT": arena(14080, KC, P), "Y": arena(15104, KC, P),
               "groups": [(0, 2), (2, 2), (4, 2), (6, 2)]} for at in (26112, 32000)]
        RS_, RS2 = arena(34624, KC, 64), arena(35136, KC, 64)
        UR, UV = arena(35648, KC, 64), arena(36160, KC, 64)
        YT = H
        RV = [parts("rwkv_r", 26112, KC, S2), parts("rwkv_k", 30464, KC, S2), parts("rwkv_v", 0, KC, S2)]
        RO_H, RO_L = parts("rwkv_out", 0, KC, S2)
        EC = sb("chunk_decay", [P, KC, len(WIDTHS)])
        MU1 = sb("one_minus_k_a", [P, KC])

        rs = {k: sem("rwkv_" + k) for k in (
            "shifted", "lora_in", "lora_act", "lora_out", "lora_taken", "lora_loaded", "mixed", "sq", "ssum", "smean", "sroot",
            "cum", "ex", "k_decayed", "ex_used", "bonus_in", "bonus_sum", "grams", "gram_taken", "turned", "turned_taken",
            "ur_ready", "ur_taken", "u_ready", "u_taken", "y_ready", "y_taken", "s_ready", "s_taken",
            "gn_sum", "gn_centred", "gn_sq", "gn_var", "gn_mean", "gn_root", "out_ready")}

        def flat(a):
            return a.rearrange("p a b -> p (a b)")

        def dve_shift(dve):
            dve_chain(nc.vector.tensor_tensor(SQ[:, :, 1:S2], H[:, :, 0:S2 - 1], H[:, :, 1:S2], ALU.subtract))
            dve_chain(nc.vector.tensor_scalar(SQ[:, :, 0:1], H[:, :, 0:1], -1.0, None, ALU.mult))

        def dve_variant(j, dest):
            for k in range(KC):
                step = nc.vector.scalar_tensor_tensor(out=dest[:, k], in0=SQ[:, k], scalar=vec("mu", KC * j + k, 1), in1=H[:, k],
                                                      op0=ALU.mult, op1=ALU.add)
                step.then_inc(rs["mixed"], 1)

        def dve_lora(dve):
            dve_shift(dve)
            for j, b in ((1, 0), (4, 1), (5, 2)):
                dve_variant(j, XV[b])
            for m in range(KC):
                for q, dest in enumerate((LD, A_, G_)):
                    n = 3 * m + q
                    dve.wait_ge(rs["lora_out"], n + 1)
                    if q < 2:
                        step = nc.vector.tensor_scalar(dest[:, m], PS[:, 4 + n % 4, 0:S2], vec(("w0", "a0")[q], m, 1), None, ALU.add)
                    else:
                        step = nc.vector.tensor_copy(dest[:, m], PS[:, 4 + n % 4, 0:S2])
                    step.then_inc(rs["lora_taken"], 1)

        def pe_lora(pe):
            pe.wait_ge(rs["lora_loaded"], 32)
            spans = [(0, 0, 64), (1, 64, 64), (2, 128, 128), (2, 256, 32)]
            for j, (b, at, width) in enumerate(spans):
                pe.wait_ge(rs["mixed"], KC * (b + 1))
                for k in range(KC):
                    mm = nc.tensor.matmul(PS[0:width, j, 0:S2], LI[:, k, at:at + width], XV[b][:, k], start=(k == 0), stop=(k == KC - 1))
                mm.then_inc(rs["lora_in"], 1)
            pe.wait_ge(rs["lora_act"], 4)
            for m in range(KC):
                cols = slice(m * P, (m + 1) * P)
                for q in range(3):
                    n = 3 * m + q
                    if n >= 4:
                        pe.wait_ge(rs["lora_taken"], n - 3)
                    out_ = PS[:, 4 + n % 4, 0:S2]
                    if q < 2:
                        mm = nc.tensor.matmul(out_, LO[0:64, q, cols], LT[0:64, q], start=True, stop=True)
                    else:
                        nc.tensor.matmul(out_, LO[:, 2, cols], LT[:, 2], start=True, stop=False)
                        mm = nc.tensor.matmul(out_, LO[0:32, 3, cols], LT[0:32, 3], start=False, stop=True)
                    mm.then_inc(rs["lora_out"], 1)

        def act_lora(act):
            for j, (width, func) in enumerate(((64, ACT.Tanh), (64, ACT.Copy), (128, ACT.Sigmoid), (32, ACT.Sigmoid))):
                act.wait_ge(rs["lora_in"], j + 1)
                nc.scalar.activation(LT[0:width, j], PS[0:width, j, 0:S2], func).then_inc(rs["lora_act"], 1)

        def dve_variants(dve):
            for j, b in ((0, 0), (2, 1), (3, 2)):
                dve_variant(j, XV[b])
                dve_parts(dve, ("r", b), XV[b], *RV[b])

        def act_variants(act):
            for b in range(3):
                act_parts(act, ("r", b), XV[b], RV[b][0], rs["mixed"], KC * (3 + b))

        def act_decays(act):
            act_chain(nc.scalar.activation(LD, LD, ACT.Sigmoid))
            act_chain(nc.scalar.activation(A_, A_, ACT.Sigmoid))
            act.sem_inc(rs["cum"], 1)
            load_log_exp(act)
            act.wait_ge(rs["sq"], 1)
            act_chain(nc.scalar.activation(H[:, :, :], KK, ACT.Square))
            act.sem_inc(rs["ssum"], 1)
            act.wait_ge(rs["ex_used"], 1)
            nc.scalar.activation(LD, AC, ACT.Exp).then_inc(rs["ex"], 1)
            act.wait_ge(rs["smean"], 1)
            act_chain(nc.scalar.activation(H[:, :, :], H[:, :, :], ACT.Ln))
            nc.scalar.activation(H[:, :, :], H[:, :, :], ACT.Exp, scale=-0.5).then_inc(rs["sroot"], 1)
            act.wait_ge(rs["ex_used"], 2)
            nc.scalar.activation(LD, AC, ACT.Exp, scale=-1.0).then_inc(rs["ex"], 1)
            for use in (3, 4):
                act.wait_ge(rs["ex_used"], use)
                nc.scalar.activation(H[:, :, :], SQ[:, :, :], ACT.Exp).then_inc(rs["ex"], 1)

        def pe_decays(pe):
            pe.wait_ge(rs["ssum"], 1)
            for k in range(KC):
                mm = nc.tensor.matmul(PS[:, k, 0:S2], HALF, H[:, k], start=True, stop=True)
            mm.then_inc(rs["ssum"], 1)
            pe.wait_ge(rs["bonus_in"], 1)
            for k in range(KC):
                mm = nc.tensor.matmul(PS[:, k, 0:S2], HALF, KKT[:, k], start=True, stop=True)
            mm.then_inc(rs["bonus_sum"], 1)

        def dve_decays(dve):
            def per(name, k):
                return vec(name, k, 1)
            for k in range(KC):
                dve_chain.later(nc.vector.tensor_scalar(KK[:, k], K_[:, k], per("k_k", k), None, ALU.mult))
            dve_chain(nc.vector.tensor_scalar(MU1[:, :], vec("k_a"), -1.0, 1.0, ALU.mult, ALU.add))
            dve.sem_inc(rs["sq"], 1)
            dve.wait_ge(rs["cum"], 1)
            dve_chain.later(nc.vector.tensor_scalar(LD, LD, -math.exp(-0.5), None, ALU.mult))
            for k in range(KC):
                dve_chain.later(nc.vector.tensor_scalar(B_[:, k], A_[:, k], per("k_a", k), MU1[:, k:k + 1], ALU.mult, ALU.add))
            dve_chain.settle()
            dve_chain.later(nc.vector.tensor_tensor(K_, K_, B_, ALU.mult))
            for k in range(KC):
                dve_chain.later(nc.vector.tensor_tensor_scan(AC[:, k], const("restart"), LD[:, k], 0.0, ALU.mult, ALU.add))
            dve_chain.settle()
            dve_chain(nc.vector.tensor_tensor(SQ[:, :, :], AC, LD, ALU.subtract))
            dve.sem_inc(rs["ex_used"], 1)
            dve.wait_ge(rs["ssum"], 2)
            dve_chain(nc.vector.tensor_scalar(H[:, :, :], PS[:, :, 0:S2], EPS, None, ALU.add))
            dve.sem_inc(rs["smean"], 1)
            for k in range(KC):
                dve_chain.later(nc.vector.scalar_tensor_tensor(out=KKT[:, k], in0=R_[:, k], scalar=per("r_k", k), in1=K_[:, k],
                                                               op0=ALU.mult, op1=ALU.mult))
            dve_chain.settle()
            dve.sem_inc(rs["bonus_in"], 1)
            dve.wait_ge(rs["ex"], 1)
            dve_chain.later(nc.vector.tensor_tensor(RT, R_, LD, ALU.mult))
            for c in range(len(WIDTHS)):
                end = span(c).stop
                dve_chain.later(nc.vector.tensor_copy(EC[:, :, c:c + 1], LD[:, :, end - 1:end]))
            dve_chain.settle()
            dve.sem_inc(rs["ex_used"], 1)
            dve.wait_ge(rs["sroot"], 1)
            dve_chain(nc.vector.tensor_tensor(KK, KK, H[:, :, :], ALU.mult))
            dve.sem_inc(rs["ex_used"], 1)
            dve_chain(nc.vector.tensor_tensor(B_, KK, A_, ALU.mult))
            dve.wait_ge(rs["bonus_sum"], 1)
            dve_chain.later(nc.vector.tensor_tensor(BONUS, PS[:, :, 0:S2], V_, ALU.mult))
            dve.wait_ge(rs["ex"], 2)
            dve_chain.later(nc.vector.tensor_tensor(BT, B_, LD, ALU.mult))
            dve.wait_ge(rs["ex"], 3)
            for c, w in enumerate(WIDTHS):
                t = span(c)
                dve_chain.later(nc.vector.tensor_tensor(SQ[:, :, t], AC[:, :, t.stop - 1:t.stop].broadcast_to([P, KC, w]),
                                                        AC[:, :, t], ALU.subtract))
            dve_chain(nc.vector.tensor_tensor(KKT, KK, H[:, :, :], ALU.mult))
            dve.sem_inc(rs["ex_used"], 1)
            dve.wait_ge(rs["ex"], 4)
            dve_chain(nc.vector.tensor_tensor(BH, B_, H[:, :, :], ALU.mult))

        def pool_decays(pool):
            pool.wait_ge(rs["ex"], 2)
            nc.gpsimd.tensor_tensor(KT, K_, LD, ALU.mult).then_inc(rs["k_decayed"], 1)
            pool.wait_ge(rs["ex"], 4)
            nc.gpsimd.tensor_tensor(KH, K_, H[:, :, :], ALU.mult).then_inc(rs["k_decayed"], 1)

        def pe_grams(pe, c, b):
            cols, w = span(c), WIDTHS[c]
            for k in (2 * b, 2 * b + 1):
                for m, left in enumerate((BT, KT)):
                    for o in range(2):
                        out_ = PS[o * TC:o * TC + w, 4 + b, 256 * (k % 2) + 128 * m:][:, 0:P].rearrange("p (a t) -> p a t", a=2)
                        mm = nc.tensor.matmul(out_[:, :, 0:w], left[half(o), k, cols], KKT_RT[half(o), :, k, cols], start=True, stop=True)
            mm.then_inc(rs["grams"], 1)

        def pe_turn(pe, c, j):
            pe.wait_ge(rs["gram_taken"], 4 * c + 2 * (j % 2) + 2)
            if j == 2:
                pe.wait_ge(rs["turned_taken"], 3 * c + 1)
            for k in range(KC):
                mm = nc.tensor.transpose(PS[0:WIDTHS[c], 4 + 2 * (j % 2) + k // 4, (k % 4) * P:(k % 4 + 1) * P],
                                         (BH, KH, V_)[j][:, k, span(c)], IDENT)
            mm.then_inc(rs["turned"], 1)

        def act_turn(act, c, j):
            act.wait_ge(rs["turned"], 3 * c + j + 1)
            for o in range(2):
                step = nc.scalar.activation((BHN, KHN, VN)[j][c % 2][half(o)], PS[half(0), 4 + 2 * (j % 2):6 + 2 * (j % 2), :].rearrange(
                    "p a (b v) -> p (a b) v", b=4)[:, :, o * 64:(o + 1) * 64], ACT.Copy)
            step.then_inc(rs["turned_taken"], 1)

        def dve_grams(dve, c, b):
            w = WIDTHS[c]
            u4 = RI[c % 2]["U"].rearrange("p k (two t) -> p k two t", two=2)
            tri_pair = const("tri_pair").rearrange("p (two t) -> p two t", two=2)[:, :, 0:w].unsqueeze(1).broadcast_to([P, 2, 2, w])
            tri = const("tri").rearrange("p (m t) -> p m t", m=3)[:, :, 0:w].unsqueeze(1).broadcast_to([P, 2, 3, w])
            s = slice(2 * b, 2 * b + 2)
            psum = PS[:, 4 + b, :].rearrange("p (k m t) -> p k m t", k=2, m=4)[:, :, :, 0:w]
            dve.wait_ge(rs["grams"], 4 * c + b + 1)
            nc.vector.tensor_tensor(u4[:, s, :, 0:w], psum[:, :, 0:1].broadcast_to([P, 2, 2, w]), tri_pair, ALU.mult)
            nc.vector.tensor_tensor(G3[c % 2][:, s, :, 0:w], psum[:, :, 1:4], tri, ALU.mult).then_inc(rs["gram_taken"], 1)

        def dve_first(dve, c):
            dve.wait_ge(rs["gram_taken"], 4 * (c + 1))
            if c:
                dve.wait_ge(rs["u_ready"], c)
            dve_first_level(RI[c % 2], KC)

        def pe_rwkv_grams(pe):
            for b in range(4):
                pe_grams(pe, 0, b)
            for j in range(3):
                pe_turn(pe, 0, j)

        def act_rwkv_grams(act):
            for j in range(3):
                act_turn(act, 0, j)

        def dve_rwkv_grams(dve):
            for b in range(4):
                dve_grams(dve, 0, b)
            dve_first(dve, 0)

        HEADS = [(k, half(o), o * TC) for k in range(KC) for o in range(2)]

        def pe_rwkv_scan(pe, c):
            cols, w, last = span(c), WIDTHS[c], c == len(WIDTHS) - 1
            g3, bhn, khn, vn = G3[c % 2], BHN[c % 2], KHN[c % 2], VN[c % 2]
            for k, r, at in HEADS:
                o = PS[at:at + w, 0, k * 64:(k + 1) * 64]
                if c:
                    nc.tensor.matmul(o, KKT[r, k, cols], STATE[c % 2][r, k], start=True, stop=False)
                mm = nc.tensor.matmul(o, g3[r, k, 1, 0:w], vn[r, k], start=(c == 0), stop=True)
            mm.then_inc(rs["ur_ready"], 1)
            if not last:
                pe_grams(pe, c + 1, 0)
            pe.wait_ge(rs["ur_taken"], c + 1)
            for k in range(KC):
                mm = nc.tensor.matmul(PS[:, 1, k * 64:(k + 1) * 64], RI[0]["XT"][:, k], UR[:, k], start=True, stop=True)
            mm.then_inc(rs["u_ready"], 1)
            if not last:
                pe_grams(pe, c + 1, 1)
            pe.wait_ge(rs["u_taken"], c + 1)
            if not last:
                for k, r, at in HEADS:
                    o = PS[r, 2, k * 64:(k + 1) * 64]
                    nc.tensor.matmul(o, bhn[r, k], UV[r, k], start=True, stop=False)
                    mm = nc.tensor.matmul(o, khn[r, k], vn[r, k], start=False, stop=True)
                mm.then_inc(rs["s_ready"], 1)
                pe_grams(pe, c + 1, 2)
                pe_grams(pe, c + 1, 3)
            for k, r, at in HEADS:
                o = PS[r, 3, k * TC:k * TC + w]
                if c:
                    nc.tensor.matmul(o, STATE[c % 2][r, k], RT[r, k, cols], start=True, stop=False)
                nc.tensor.matmul(o, UV[r, k], g3[r, k, 0, 0:w], start=(c == 0), stop=False)
                mm = nc.tensor.matmul(o, vn[r, k], g3[r, k, 2, 0:w], start=False, stop=True)
            mm.then_inc(rs["y_ready"], 1)
            for j in range(0 if last else 3):
                pe_turn(pe, c + 1, j)

        STATE = [RS_, RS2]

        def act_rwkv_scan(act, c):
            act.wait_ge(rs["u_ready"], c + 1)
            nc.scalar.activation(UV, halves(1, KC), ACT.Copy, scale=-1.0).then_inc(rs["u_taken"], 1)
            act.wait_ge(rs["y_ready"], c + 1)
            act_chain(nc.scalar.activation(YT[:, :, span(c)], halves(3, KC)[:, :, 0:WIDTHS[c]], ACT.Copy))
            for j in range(3 if c < len(WIDTHS) - 1 else 0):
                act_turn(act, c + 1, j)

        def dve_rwkv_scan(dve, c):
            dve.wait_ge(rs["ur_ready"], c + 1)
            nc.vector.tensor_copy(UR, halves(0, KC)).then_inc(rs["ur_taken"], 1)
            if c == len(WIDTHS) - 1:
                return
            new, old = STATE[(c + 1) % 2], STATE[c % 2]
            dve_grams(dve, c + 1, 0)
            if c:
                dve_chain(nc.vector.tensor_tensor(new, old, EC[:, :, c:c + 1].broadcast_to([P, KC, 64]), ALU.mult))
            dve_grams(dve, c + 1, 1)
            dve.wait_ge(rs["s_ready"], c + 1)
            if c:
                dve_chain(nc.vector.tensor_tensor(new, new, halves(2, KC), ALU.add))
            else:
                dve_chain(nc.vector.tensor_copy(new, halves(2, KC)))
            dve_grams(dve, c + 1, 2)
            dve_grams(dve, c + 1, 3)
            dve_first(dve, c + 1)

        GN_EPS = 64e-5

        def pe_rwkv_out(pe):
            for k in range(KC):
                nc.tensor.matmul(PS[:, k, 0:S2], HALF, YT[:, k], start=True, stop=True).then_inc(rs["gn_sum"], 1)
            for k in range(KC):
                pe.wait_ge(rs["gn_sq"], k + 1)
                nc.tensor.matmul(PS[:, k, 0:S2], HALF, SQ[:, k], start=True, stop=True).then_inc(rs["gn_var"], 1)

        def act_rwkv_out(act):
            for k in range(KC):
                act.wait_ge(rs["gn_centred"], k + 1)
                nc.scalar.activation(SQ[:, k], YT[:, k], ACT.Square).then_inc(rs["gn_sq"], 1)
            for q in range(2):
                v = SQ[:, 4 * q:4 * q + 4]
                act.wait_ge(rs["gn_mean"], q + 1)
                act_chain(nc.scalar.activation(v, v, ACT.Ln))
                nc.scalar.activation(v, v, ACT.Exp, scale=-0.5).then_inc(rs["gn_root"], 1)

        def dve_rwkv_out(dve):
            for k in range(KC):
                dve.wait_ge(rs["gn_sum"], k + 1)
                nc.vector.scalar_tensor_tensor(out=YT[:, k], in0=PS[:, k, 0:S2], scalar=-1.0 / 64, in1=YT[:, k],
                                               op0=ALU.mult, op1=ALU.add).then_inc(rs["gn_centred"], 1)
            for q in range(2):
                v = slice(4 * q, 4 * q + 4)
                dve.wait_ge(rs["gn_var"], 4 * q + 4)
                nc.vector.tensor_scalar(SQ[:, v], PS[:, v, 0:S2], 1.0 / 64, GN_EPS, ALU.mult, ALU.add).then_inc(rs["gn_mean"], 1)
            for q in range(2):
                v = slice(4 * q, 4 * q + 4)
                dve.wait_ge(rs["gn_root"], q + 1)
                dve_chain(nc.vector.tensor_tensor(YT[:, v], YT[:, v], SQ[:, v], ALU.mult))
                for k in range(4 * q, 4 * q + 4):
                    dve_chain.later(nc.vector.scalar_tensor_tensor(out=YT[:, k], in0=YT[:, k], scalar=vec("ln_w", k, 1), in1=BONUS[:, k],
                                                                   op0=ALU.mult, op1=ALU.add))
                dve_chain.settle()
                for k in range(4 * q, 4 * q + 4):
                    nc.vector.scalar_tensor_tensor(out=YT[:, k], in0=YT[:, k], scalar=vec("ln_bb", k, 1), in1=G_[:, k],
                                                   op0=ALU.add, op1=ALU.mult).then_inc(rs["out_ready"], 1)
        tokens_loaded, loaded, first_loaded, stored = sem("tokens_loaded"), sem("parameters_loaded"), sem("first_block_loaded"), sem("output_stored")
        final_ready = sem("final_ready")
        with nc.Block() as block:

            @block.sync
            def _(sp):
                sp.dma_start(X[:, :, :], x_in).then_inc(tokens_loaded, 16)
                sp.dma_start(C[:, :], const_in).then_inc(loaded, 16)
                sp.dma_start(V[:, :], vec_in[:, 0:VEC_W]).then_inc(loaded, 16)

                def load_block(n, slot):
                    sp.dma_start(W[:, slot], weights_in[n]).then_inc(landed[slot], 16)

                def stream(first, last):
                    n = first
                    while n < last and (n < RING or n % RING):
                        if n >= RING:
                            sp.wait_ge(weights_low, 2 * (n - RING + 1))
                        load_block(n, n % RING)
                        n += 1
                    rounds = (last - n) // RING
                    if rounds:
                        with sp.Fori(0, rounds) as g:
                            for u in range(RING):
                                sp.wait_ge(weights_low, g * (2 * RING) + 2 * (n + u - RING + 1))
                                load_block(g * RING + n + u, u)
                        n += rounds * RING
                    while n < last:
                        sp.wait_ge(weights_low, 2 * (n - RING + 1))
                        load_block(n, n % RING)
                        n += 1

                mix0 = BLOCKS["mix_out", 0][0] + SPLIT
                stream(0, RING)
                sp.dma_start(POS, pos_in).then_inc(first_loaded, 16)
                sp.dma_start(AR[:, FIRST_AT:FIRST_AT + FIRST_W], first_in).then_inc(first_loaded, 16)
                stream(RING, mix0)
                sp_hybrid_rows(sp)
                mix1 = BLOCKS["mix_in", 1][0] + SPLIT
                stream(mix0, mix1)
                sp.wait_ge(stage_end, 4 * STAGES_BEFORE_RWKV)
                sp.dma_start(LI, vec_in[:, VEC_W:VEC_W + KC * 288].rearrange("p (k c) -> p k c", k=KC)).then_inc(rs["lora_loaded"], 16)
                sp.dma_start(LO, vec_in[:, VEC_W + KC * 288:].rearrange("p (k c) -> p k c", k=4)).then_inc(rs["lora_loaded"], 16)
                stream(mix1, N_BLOCKS)
                sp.wait_ge(final_ready, 1)
                sp.dma_start(out, H[:, :, META:S2]).then_inc(stored, 16)
                sp.wait_ge(stored, 16)

            @block.tensor
            def _(pe):
                pe.wait_ge(loaded, 32)
                for l in range(DEPTH):
                    pe_norm(pe, l, S1)
                    pe_project(pe, ("w_in", l), ("w_in", l), H1_H, H1_L, S1)
                    end_stage(pe, "pe")
                    pe_shape(pe, l)
                    end_stage(pe, "pe")
                    pe_attention(pe, attn["A", l], PT[:, AQ:AQ + 4], PT[:, AK:AK + 4], AVN)
                    end_stage(pe, "pe")
                    pe_attention(pe, attn["C", l], PT[:, CQ:CQ + 4], PT[:, CK:CK + 4], CVN)
                    end_stage(pe, "pe")
                    pe_diff_norm(pe, l)
                    pe_sgu(pe, l)
                    end_stage(pe, "pe")
                    pe_merge(pe, l)
                    pe_project(pe, ("w_out", l), ("w_out", l), H1_H, H1_L, S1)
                    end_stage(pe, "pe")
                pe_norm(pe, 2, S1)
                end_stage(pe, "pe")
                norm = 3
                for l in range(DEPTH):
                    for f in range(2):
                        pe_norm(pe, norm, S2)
                        norm += 1
                        pe_ffn(pe, 2 * l + f, l, f)
                        if f:
                            continue
                        pe_norm(pe, norm, S2)
                        norm += 1
                        if l == 0:
                            pe.wait_ge(normed_ready, KC * norm)
                            pe_project(pe, ("mix_in", 0), ("hybrid", 0), MIX_H, MIX_L, S2)
                            pe_hybrid_in(pe)
                            end_stage(pe, "pe")
                            pe_fox_values(pe)
                            end_stage(pe, "pe")
                            pe.wait_ge(hs["fox_bound"], 16 * FOX_ROW_DMAS)
                            pe_attention(pe, FOX, HP[:, FQ:FQ + 4], HP[:, FK:FK + 4], FVN, gates=(FA, FB))
                            end_stage(pe, "pe")
                            pe_delta_prep(pe)
                            end_stage(pe, "pe")
                            pe_delta_grams(pe)
                            end_stage(pe, "pe")
                            pe_inverse(pe, 0, GI)
                            end_stage(pe, "pe")
                            pe_delta_scan(pe)
                            end_stage(pe, "pe")
                            pe_delta_out(pe)
                            end_stage(pe, "pe")
                            pe_project(pe, ("mix_out", 0), ("hybrid", 1), MIX_H, MIX_L, S2)
                            end_stage(pe, "pe")
                        else:
                            end_stage(pe, "pe")
                            pe_lora(pe)
                            end_stage(pe, "pe")
                            for q in range(3):
                                pe_project(pe, ("mix_in", 1), ("r", q), *RV[q], S2, part=(8 * q, 8))
                            end_stage(pe, "pe")
                            pe_decays(pe)
                            end_stage(pe, "pe")
                            pe_rwkv_grams(pe)
                            end_stage(pe, "pe")
                            for c in range(len(WIDTHS)):
                                pe_inverse(pe, 1 + c, RI[c % 2])
                                end_stage(pe, "pe")
                                pe_rwkv_scan(pe, c)
                                end_stage(pe, "pe")
                            pe_rwkv_out(pe)
                            pe_project(pe, ("mix_out", 1), ("r", 3), RO_H, RO_L, S2)
                            end_stage(pe, "pe")
                pe_norm(pe, norm, S2)

            @block.scalar
            def _(act):
                nonlocal act_chain
                act_chain = Chain(act, "act_chain")
                load_log_exp(act)
                act.wait_ge(tokens_loaded, 16)
                act.sem_inc(gates_taken, 2)
                for l in range(DEPTH):
                    act_norm(act, l, XA, S1)
                    act_parts(act, ("w_in", l), H[:, :, 0:S1], H1_H, normed_ready, KC * l)
                    if l == 0:
                        act_setup(act)
                        load_log_exp(act)
                    take_outputs(act, act_split, ("w_in", l), (0,), act_take(PT, S1))
                    end_stage(act, "act")
                    act_shape(act, l)
                    end_stage(act, "act")
                    act_attention(act, attn["A", l])
                    end_stage(act, "act")
                    act_attention(act, attn["C", l])
                    end_stage(act, "act")
                    act_diff_norm(act, l)
                    act_sgu(act, l)
                    act_branch_parts(act, l)
                    end_stage(act, "act")
                    act_merge(act, l)
                    take_outputs(act, act_split, ("w_out", l), (), None)
                    end_stage(act, "act")
                act_norm(act, 2, XA, S1)
                end_stage(act, "act")
                norm = 3
                for l in range(DEPTH):
                    for f in range(2):
                        act_norm(act, norm, X[:, :, :], S2)
                        act_parts(act, ("ffn", 2 * l + f), H, H2_H, normed_ready, KC * norm)
                        norm += 1
                        act_ffn(act, 2 * l + f, l, f)
                        if f:
                            continue
                        act_norm(act, norm, X[:, :, :], S2)
                        norm += 1
                        if l == 0:
                            act_parts(act, ("hybrid", 0), H, MIX_H, normed_ready, KC * (norm - 1))
                            take_outputs(act, act_split, ("mix_in", 0), (0,), act_take(HP, S2))
                            end_stage(act, "act")
                            act_hybrid_rows(act)
                            end_stage(act, "act")
                            act_attention(act, FOX)
                            end_stage(act, "act")
                            act_delta_prep(act)
                            end_stage(act, "act")
                            act_delta_grams(act)
                            end_stage(act, "act")
                            act_inverse(act, 0, GI)
                            end_stage(act, "act")
                            act_delta_scan(act)
                            end_stage(act, "act")
                            act_delta_out(act)
                            act_parts(act, ("hybrid", 1), Y8, MIX_H, hs["outputs"], 0)
                            end_stage(act, "act")
                            take_outputs(act, act_split, ("mix_out", 0), (), None)
                            end_stage(act, "act")
                        else:
                            end_stage(act, "act")
                            act_lora(act)
                            end_stage(act, "act")
                            act_variants(act)
                            take_outputs(act, act_split, ("mix_in", 1), (0,), act_take(RKV, S2))
                            end_stage(act, "act")
                            act_decays(act)
                            end_stage(act, "act")
                            act_rwkv_grams(act)
                            end_stage(act, "act")
                            for c in range(len(WIDTHS)):
                                act_inverse(act, 1 + c, RI[c % 2])
                                end_stage(act, "act")
                                act_rwkv_scan(act, c)
                                end_stage(act, "act")
                            act_rwkv_out(act)
                            act_parts(act, ("r", 3), YT, RO_H, rs["out_ready"], 0)
                            take_outputs(act, act_split, ("mix_out", 1), (), None)
                            end_stage(act, "act")
                act_norm(act, norm, X[:, :, :], S2)

            @block.vector
            def _(dve):
                nonlocal dve_chain
                dve_chain = Chain(dve, "dve_chain")
                dve.wait_ge(tokens_loaded, 16)
                dve.sem_inc(residual_ready, KC)
                for n in range(SPLIT):
                    dve_split(dve, n)
                dve.sem_inc(taken[0], 2)
                dve.sem_inc(taken[1], 2)
                dve.sem_inc(ups_taken, 2)
                dve.wait_ge(loaded, 32)
                for l in range(DEPTH):
                    if l:
                        dve.sem_inc(residual_ready, KC)
                    dve_norm(dve, l, XA, S1, vec("norm_g", KC * l, KC), H)
                    dve_parts(dve, ("w_in", l), H[:, :, 0:S1], H1_H, H1_L)
                    if l == 0:
                        dve.wait_ge(first_loaded, 32)
                        dve_setup(dve)
                    take_outputs(dve, dve_split, ("w_in", l), (1,), dve_take(PT, S1))
                    end_stage(dve, "dve")
                    dve_shape(dve, l)
                    end_stage(dve, "dve")
                    dve_attention(dve, attn["A", l], mask_a, YS[:, 0:4], NEG_LAM[:, l:l + 1])
                    end_stage(dve, "dve")
                    dve_attention(dve, attn["C", l], mask_c, YS[:, 8:12])
                    end_stage(dve, "dve")
                    dve_diff_norm(dve, l)
                    dve_sgu(dve, l)
                    dve_branch_parts(dve, l)
                    end_stage(dve, "dve")
                    dve_merge(dve, l)
                    take_outputs(dve, dve_split, ("w_out", l), (0, 1), dve_add(XA, S1))
                    end_stage(dve, "dve")
                dve.sem_inc(residual_ready, KC)
                dve_norm(dve, 2, XA, S1, vec("final_g"), XA)
                end_stage(dve, "dve")
                norm = 3
                for l in range(DEPTH):
                    for f in range(2):
                        if (l, f) != (1, 0):
                            dve.sem_inc(residual_ready, KC)
                        dve_norm(dve, norm, X, S2, vec("ffn_g", KC * (2 * l + f), KC), H)
                        dve_parts(dve, ("ffn", 2 * l + f), H, H2_H, H2_L)
                        norm += 1
                        dve_ffn(dve, 2 * l + f, l, f)
                        if f:
                            continue
                        dve_norm(dve, norm, X, S2, vec("mix_g", KC * l, KC), H)
                        norm += 1
                        if l == 0:
                            dve_parts(dve, ("hybrid", 0), H, MIX_H, MIX_L)
                            take_outputs(dve, dve_split, ("mix_in", 0), (1,), dve_take(HP, S2))
                            end_stage(dve, "dve")
                            dve_hybrid_rows(dve)
                            end_stage(dve, "dve")
                            dve_attention(dve, FOX, const("mask_f").rearrange("p (a b) -> p a b", a=NT2), Y8[:, 0:4],
                                          beside=lambda h: dve_convolution(dve, h))
                            end_stage(dve, "dve")
                            dve_delta_prep(dve)
                            end_stage(dve, "dve")
                            dve_delta_grams(dve)
                            end_stage(dve, "dve")
                            dve_inverse(dve, 0, GI)
                            end_stage(dve, "dve")
                            dve_delta_scan(dve)
                            end_stage(dve, "dve")
                            dve_delta_out(dve)
                            dve_parts(dve, ("hybrid", 1), Y8, MIX_H, MIX_L)
                            end_stage(dve, "dve")
                            take_outputs(dve, dve_split, ("mix_out", 0), (0, 1), dve_add(X, S2))
                            end_stage(dve, "dve")
                        else:
                            end_stage(dve, "dve")
                            dve_lora(dve)
                            end_stage(dve, "dve")
                            dve_variants(dve)
                            take_outputs(dve, dve_split, ("mix_in", 1), (1,), dve_take(RKV, S2))
                            end_stage(dve, "dve")
                            dve_decays(dve)
                            end_stage(dve, "dve")
                            dve_rwkv_grams(dve)
                            end_stage(dve, "dve")
                            for c in range(len(WIDTHS)):
                                dve_inverse(dve, 1 + c, RI[c % 2])
                                end_stage(dve, "dve")
                                dve_rwkv_scan(dve, c)
                                end_stage(dve, "dve")
                            dve_rwkv_out(dve)
                            dve_parts(dve, ("r", 3), YT, RO_H, RO_L)
                            take_outputs(dve, dve_split, ("mix_out", 1), (0, 1), dve_add(X, S2))
                            end_stage(dve, "dve")
                dve_norm(dve, norm, X, S2, vec("final2_g"), H)
                dve.sem_inc(final_ready, 1)

            @block.gpsimd
            def _(pool):
                for l in range(DEPTH):
                    end_stage(pool, "pool")
                    pool_shape(pool, l)
                    for _ in range(5):
                        end_stage(pool, "pool")
                end_stage(pool, "pool")
                for l in range(DEPTH):
                    for f in range(2):
                        if f:
                            continue
                        if l == 0:
                            end_stage(pool, "pool")
                            pool_hybrid_rows(pool)
                            for _ in range(4):
                                end_stage(pool, "pool")
                            for _ in range(4):
                                end_stage(pool, "pool")
                        else:
                            for _ in range(3):
                                end_stage(pool, "pool")
                            pool_decays(pool)
                            end_stage(pool, "pool")
                            for _ in range(1 + 2 * len(WIDTHS)):
                                end_stage(pool, "pool")
                            end_stage(pool, "pool")


def kernel(**inputs):
    import concourse.bacc as bacc
    from concourse.bass_utils import run_bass_kernel_spmd

    i = {k: np.asarray(v) for k, v in inputs.items()}
    constants, first = host_constants()
    vectors, lora = host_vectors(i, first)
    x = np.concatenate([i["meta_2"], i["x"][0]], 0)
    arrays = {
        "x_in": np.ascontiguousarray(x.reshape(S2, KC, P).transpose(2, 1, 0)),
        "pos_in": np.ascontiguousarray(np.broadcast_to(i["positions"].reshape(1, S1), (P, S1))),
        "const_in": constants,
        "first_in": first,
        "vec_in": np.concatenate([vectors, lora], 1),
        "weights_in": host_weights(i),
    }
    nc = bacc.Bacc("TRN2", target_bir_lowering=False, num_devices=1,
                   dynamic_dma_scratch_size=256)
    args = {n: nc.dram_tensor(n, a.shape, mybir.dt.from_np(a.dtype), kind="ExternalInput").ap() for n, a in arrays.items()}
    out = nc.dram_tensor("out", (P, KC, S1), F32, kind="ExternalOutput").ap()
    build(nc, out=out, **args)
    result = run_bass_kernel_spmd(nc, [arrays], core_ids=[0]).results[0]["out"]
    return np.ascontiguousarray(result.transpose(2, 1, 0).reshape(1, S1, D))
```
